# Optimizing a Trainium2 kernel written in Bass

```python
import math
import jax, jax.numpy as jnp
from jax import lax
import numpy as np

D_MODEL = 1024
BATCH = 1
SEQ = 256
DEPTH = 2

N_META = 16
Q_BLOCK = 128
ROPE_THETA = 500000.0
RMS_EPS = 1e-6
NEG_INF = -1e30

DIFF_HEADS = D_MODEL // 256
DIFF_DH = 64
DIFF_VD = 2 * DIFF_DH
DIFF_WIDTH = DIFF_HEADS * DIFF_VD
FOX_HEADS = D_MODEL // 128
FOX_DH = 64
FOX_WIDTH = FOX_HEADS * FOX_DH
D_FF = 2816
N_EXPERTS = 8
TOP_K = 2
D_FF_EXPERT = 3584
N_DENSE = (DEPTH + 1) // 2
N_MOE = DEPTH // 2

IN_SPLIT_SIZES = (DIFF_HEADS * 2 * DIFF_DH, DIFF_HEADS * 2 * DIFF_DH, DIFF_WIDTH,
                  FOX_WIDTH, FOX_WIDTH, FOX_WIDTH, FOX_HEADS, D_MODEL, D_MODEL)
IN_COLS = sum(IN_SPLIT_SIZES)

kernel_name = 'hybrid_diffattn_fox_moe_block'

def rmsnorm(x, g):
    xf = x.astype(jnp.float32)
    y = xf * lax.rsqrt(jnp.mean(xf * xf, axis=-1, keepdims=True) + RMS_EPS)
    return (y * g.astype(jnp.float32)).astype(x.dtype)

def rope_tables(L, dh):
    rd = dh // 4
    inv = ROPE_THETA ** (-jnp.arange(0, rd, 2, dtype=jnp.float32) / rd)
    ang = jnp.arange(L, dtype=jnp.float32)[:, None] * inv[None, :]
    return jnp.cos(ang), jnp.sin(ang)

def rope_partial(x, cos, sin):
    rd = x.shape[-1] // 4
    half = rd // 2
    shape = (1, cos.shape[0]) + (1,) * (x.ndim - 3) + (half,)
    c = cos.reshape(shape).astype(x.dtype)
    s = sin.reshape(shape).astype(x.dtype)
    x1 = x[..., :half]
    x2 = x[..., half:rd]
    return jnp.concatenate([x1 * c - x2 * s, x2 * c + x1 * s, x[..., rd:]], axis=-1)

def query_blocks(L):
    n_real = (L - N_META) // Q_BLOCK
    return [(0, N_META)] + [(N_META + i * Q_BLOCK, N_META + (i + 1) * Q_BLOCK) for i in range(n_real)]

def causal_mask(qs, qe):
    t = jnp.arange(qs, qe)[:, None]
    s = jnp.arange(qe)[None, :]
    return s <= t

def diff_attention(q, k, v, lam, lam_init, subln_g):
    B, L = q.shape[0], q.shape[1]
    scale = DIFF_DH ** -0.5
    q1, q2 = q[..., 0, :], q[..., 1, :]
    k1, k2 = k[..., 0, :], k[..., 1, :]
    outs = []
    for qs, qe in query_blocks(L):
        mask = causal_mask(qs, qe)
        s1 = jnp.einsum('bqhd,bkhd->bhqk', q1[:, qs:qe], k1[:, :qe]).astype(jnp.float32) * scale
        s2 = jnp.einsum('bqhd,bkhd->bhqk', q2[:, qs:qe], k2[:, :qe]).astype(jnp.float32) * scale
        p1 = jax.nn.softmax(jnp.where(mask, s1, NEG_INF), axis=-1)
        p2 = jax.nn.softmax(jnp.where(mask, s2, NEG_INF), axis=-1)
        a = (p1 - lam * p2).astype(v.dtype)
        outs.append(jnp.einsum('bhqk,bkhd->bqhd', a, v[:, :qe]))
    o = jnp.concatenate(outs, axis=1)
    o = rmsnorm(o, subln_g) * (1.0 - lam_init)
    return o.reshape(B, L, DIFF_WIDTH)

def forgetting_attention(q, k, v, f_logit, b_f):
    B, L = q.shape[0], q.shape[1]
    scale = FOX_DH ** -0.5
    log_f = jax.nn.log_sigmoid(f_logit.astype(jnp.float32) + b_f.astype(jnp.float32))
    c = jnp.transpose(lax.cumsum(log_f, axis=1), (0, 2, 1))
    outs = []
    for qs, qe in query_blocks(L):
        mask = causal_mask(qs, qe)
        s = jnp.einsum('bqhd,bkhd->bhqk', q[:, qs:qe], k[:, :qe]).astype(jnp.float32) * scale
        s = s + c[:, :, qs:qe, None] - c[:, :, None, :qe]
        p = jax.nn.softmax(jnp.where(mask, s, NEG_INF), axis=-1).astype(v.dtype)
        outs.append(jnp.einsum('bhqk,bkhd->bqhd', p, v[:, :qe]))
    o = jnp.concatenate(outs, axis=1)
    return o.reshape(B, L, FOX_WIDTH)

def split_cols(z):
    points = []
    acc = 0
    for size in IN_SPLIT_SIZES[:-1]:
        acc += size
        points.append(acc)
    return jnp.split(z, points, axis=-1)

def mixer(hn, w_in, b_forget, diff_lambda, diff_subln_g, w_branch_diff, w_branch_fox, w_out, cos, sin, lam_init):
    B, L, _ = hn.shape
    z = hn @ w_in
    dq, dk, dv, fq, fk, fv, ff, ga, gb = split_cols(z)
    dq = rope_partial(dq.reshape(B, L, DIFF_HEADS, 2, DIFF_DH), cos, sin)
    dk = rope_partial(dk.reshape(B, L, DIFF_HEADS, 2, DIFF_DH), cos, sin)
    dv = dv.reshape(B, L, DIFF_HEADS, DIFF_VD)
    lp = diff_lambda.astype(jnp.float32)
    lam = jnp.exp(jnp.sum(lp[0] * lp[1])) - jnp.exp(jnp.sum(lp[2] * lp[3])) + lam_init
    o_a = diff_attention(dq, dk, dv, lam, lam_init, diff_subln_g)
    o_b = forgetting_attention(fq.reshape(B, L, FOX_HEADS, FOX_DH),
                               fk.reshape(B, L, FOX_HEADS, FOX_DH),
                               fv.reshape(B, L, FOX_HEADS, FOX_DH), ff, b_forget)
    merged = jax.nn.sigmoid(ga) * (o_a @ w_branch_diff) + jax.nn.sigmoid(gb) * (o_b @ w_branch_fox)
    return merged @ w_out

def swiglu(h, wg, wu, wd):
    return (jax.nn.silu(h @ wg) * (h @ wu)) @ wd

def moe_ffn(h, router, wg, wu, wd):
    logits = jnp.einsum('bld,de->ble', h, router).astype(jnp.float32)
    top_v, top_i = lax.top_k(logits, TOP_K)
    w = jax.nn.softmax(top_v, axis=-1)
    comb = jnp.sum(jax.nn.one_hot(top_i, N_EXPERTS, dtype=jnp.float32) * w[..., None], axis=-2)
    comb = comb.astype(h.dtype)
    y = jnp.zeros_like(h)
    for e in range(N_EXPERTS):
        y = y + comb[..., e:e + 1] * swiglu(h, wg[e], wu[e], wd[e])
    return y

def setup_inputs(seed: int = 0) -> dict:
    key = jax.random.key(seed)
    ks = jax.random.split(key, 20)
    f32 = jnp.float32

    def nrm(k, shape, scale):
        return jax.random.normal(k, shape, f32) * scale

    return {
        'x': nrm(ks[0], (BATCH, SEQ, D_MODEL), 1.0),
        'meta_tokens': nrm(ks[1], (N_META, D_MODEL), 1.0),
        'norm_mix_g': 1.0 + nrm(ks[2], (DEPTH, D_MODEL), 0.02),
        'w_in': nrm(ks[3], (DEPTH, D_MODEL, IN_COLS), D_MODEL ** -0.5),
        'b_forget': jax.random.uniform(ks[4], (DEPTH, FOX_HEADS), f32, 1.0, 6.0),
        'diff_lambda': nrm(ks[5], (DEPTH, 4, DIFF_DH), 0.1),
        'diff_subln_g': 1.0 + nrm(ks[6], (DEPTH, DIFF_VD), 0.02),
        'w_branch_diff': nrm(ks[7], (DEPTH, DIFF_WIDTH, D_MODEL), DIFF_WIDTH ** -0.5),
        'w_branch_fox': nrm(ks[8], (DEPTH, FOX_WIDTH, D_MODEL), FOX_WIDTH ** -0.5),
        'w_out': nrm(ks[9], (DEPTH, D_MODEL, D_MODEL), D_MODEL ** -0.5),
        'norm_ffn_g': 1.0 + nrm(ks[10], (DEPTH, D_MODEL), 0.02),
        'ffn_w_gate': nrm(ks[11], (N_DENSE, D_MODEL, D_FF), D_MODEL ** -0.5),
        'ffn_w_up': nrm(ks[12], (N_DENSE, D_MODEL, D_FF), D_MODEL ** -0.5),
        'ffn_w_down': nrm(ks[13], (N_DENSE, D_FF, D_MODEL), D_FF ** -0.5),
        'moe_router': nrm(ks[14], (N_MOE, D_MODEL, N_EXPERTS), D_MODEL ** -0.5),
        'moe_w_gate': nrm(ks[15], (N_MOE, N_EXPERTS, D_MODEL, D_FF_EXPERT), D_MODEL ** -0.5),
        'moe_w_up': nrm(ks[16], (N_MOE, N_EXPERTS, D_MODEL, D_FF_EXPERT), D_MODEL ** -0.5),
        'moe_w_down': nrm(ks[17], (N_MOE, N_EXPERTS, D_FF_EXPERT, D_MODEL), D_FF_EXPERT ** -0.5),
        'final_norm_g': 1.0 + nrm(ks[18], (D_MODEL,), 0.02),
    }

def reference(x, meta_tokens, norm_mix_g, w_in, b_forget, diff_lambda, diff_subln_g, w_branch_diff,
              w_branch_fox, w_out, norm_ffn_g, ffn_w_gate, ffn_w_up, ffn_w_down, moe_router,
              moe_w_gate, moe_w_up, moe_w_down, final_norm_g):
    B = x.shape[0]
    meta = jnp.broadcast_to(meta_tokens[None].astype(x.dtype), (B, N_META, D_MODEL))
    h = jnp.concatenate([meta, x], axis=1)
    L = h.shape[1]
    cos, sin = rope_tables(L, DIFF_DH)
    for layer in range(DEPTH):
        lam_init = 0.8 - 0.6 * math.exp(-0.3 * layer)
        hn = rmsnorm(h, norm_mix_g[layer])
        h = h + mixer(hn, w_in[layer], b_forget[layer], diff_lambda[layer], diff_subln_g[layer],
                      w_branch_diff[layer], w_branch_fox[layer], w_out[layer], cos, sin, lam_init)
        hn = rmsnorm(h, norm_ffn_g[layer])
        j = layer // 2
        if layer % 2 == 0:
            h = h + swiglu(hn, ffn_w_gate[j], ffn_w_up[j], ffn_w_down[j])
        else:
            h = h + moe_ffn(hn, moe_router[j], moe_w_gate[j], moe_w_up[j], moe_w_down[j])
    return rmsnorm(h, final_norm_g)[:, N_META:]


_drawn_inputs = setup_inputs


def setup_inputs(seed=0):
    import zlib

    import numpy as np

    out = dict(_drawn_inputs(seed))
    spreads = {}
    factors = {}
    for name, (base, spread) in spreads.items():
        noise = np.random.default_rng([zlib.crc32(name.encode()), seed]).standard_normal(out[name].shape)
        drawn = base * np.exp(spread * noise) if base else spread * noise
        out[name] = __import__('jax').numpy.asarray(drawn.astype(out[name].dtype))
    for name, factor in factors.items():
        out[name] = (out[name] * factor).astype(out[name].dtype)
    return out
```

```python
import math
from contextlib import ExitStack

import concourse.bass as bass
from concourse import mybir

F32 = mybir.dt.float32
F32R = mybir.dt.float32r
I32 = mybir.dt.int32
ACT = mybir.ActivationFunctionType
ALU = mybir.AluOpType
AX = mybir.AxisListType.X

P = 128
D = 1024
KD = D // P
NMETA = 16
SEQ = 256
T = NMETA + SEQ
LAYERS = 2
DFF = 2816
FT = DFF // P
NE = 8
DFE = 3584
EPS = 1e-6
SCALE = 64 ** -0.5
BIG = 1e30
WIN = [0, NMETA, NMETA + P]
IN_COLS = 5128
FF_COL = 3072
GATE_COL = FF_COL + 8
SEG = [(0, 16), (16, 144), (160, 272)]

NRAW = 6
NSPLIT = 3
COLS = 2048
MIX_PIECES = 28
FFN_BLOCKS = DFF // 256
FFN_PIECES = 2 * FFN_BLOCKS + 12
LAYER1 = MIX_PIECES + FFN_PIECES
MOE0 = LAYER1 + MIX_PIECES
UNITS = DFE // 512
JOB = 6 * UNITS
AHEAD = 3
OVER0 = MOE0 + NE * JOB + AHEAD
MAX_OVER = 3
assert MOE0 % NRAW == 0 and JOB % NRAW == 0 and JOB % NSPLIT == 0 and MOE0 % NSPLIT == 0
DOWN_K = [(0, 8), (8, 8), (16, 6)]

MIX_TILES = 69
FFN_TILES = 4 * FFN_BLOCKS + 8
V_TILE, GATE_TILE, BD_TILE, BF_TILE, OUT_TILE = 17, 29, 45, 53, 61
DOWN_TILE = MIX_TILES + 4 * FFN_BLOCKS
FFN_STRIPS = 4 * FFN_BLOCKS + 24


def strips_to_tile(t):
    if t < DOWN_TILE:
        return t + 1
    if t < MIX_TILES + FFN_TILES:
        dp, i = divmod(t - DOWN_TILE, 2)
        return DOWN_TILE + 6 * dp + 4 + i + 1
    return t + 1 + FFN_STRIPS - FFN_TILES


def strips_to_piece(j):
    l, j = divmod(j, LAYER1)
    base = l * (MIX_TILES + FFN_STRIPS)
    for first, last, start, each in ((0, 8, 1, 2), (8, 12, V_TILE, 3), (12, 20, GATE_TILE, 2),
                                     (20, 24, BD_TILE, 4), (24, LAYER1, OUT_TILE, 2)):
        if j < last:
            return base + start + each * (j - first + 1)

C_MASK, C_ID, C_TRI, C_IOTA, C_ROT, C_COS, C_SIN, C_REV = 0, 432, 560, 688, 944, 1072, 1344, 1616
C_W = 1632
V_GMIX, V_GFFN, V_GFIN, V_SUB, V_BF, V_FF, V_RT = 0, 16, 32, 40, 42, 44, 172
V_W = 236


class Chain:

    def __init__(self, eng, sem):
        self.eng, self.sem, self.base, self.k = eng, sem, 0, 0

    def __call__(self, ins):
        self.k += 1
        ins.then_inc(self.sem, 1)
        self.eng.wait_ge(self.sem, self.base + self.k)

    def enter(self, turn, per):
        self.start, self.per = self.k, per
        self.base, self.k = turn * per + self.start, 0

    def leave(self, turns):
        assert self.k == self.per, (self.k, self.per)
        self.base, self.k = 0, self.start + turns * self.per


def trunk(nc, xT, w_in, lam, w_bd, w_bf, w_out, f_g, f_u, f_d, m_g, m_u, m_d, consts, vecs, outT):
    lam_init = [0.8 - 0.6 * math.exp(-0.3 * l) for l in range(LAYERS)]
    ctx = ExitStack()
    with ctx:
        def sb(name, shape, dt=F32, scope=ctx):
            return scope.enter_context(nc.sbuf_tensor(name, shape, dt))

        def bank(name):
            return ctx.enter_context(nc.psum_tensor(name, [P, 512], F32))

        def sem(name):
            return ctx.enter_context(nc.semaphore(name))

        raw = sb("raw", [P, NRAW, COLS])
        w_hi = sb("w_hi", [P, NSPLIT, COLS], F32R)
        w_lo = sb("w_lo", [P, NSPLIT, COLS], F32R)
        h = sb("h", [P, KD, T])
        x_hi = [sb(f"x_hi{i}", [P, KD, T], F32R) for i in range(2)]
        x_lo = [sb(f"x_lo{i}", [P, KD, T], F32R) for i in range(2)]
        sq = sb("sq", [P, 2, T])
        rb = sb("rb", [P, T])
        rt = sb("rt", [P, 3])
        cst = sb("cst", [P, C_W])
        vec = sb("vec", [P, V_W])
        ones = sb("ones", [P, P])
        eps = sb("eps", [P, 1])
        ff_hi = sb("ff_hi", [P, 248], F32R)
        ff_lo = sb("ff_lo", [P, 248], F32R)
        rw_hi = sb("rw_hi", [P, KD, NE], F32R)
        rw_lo = sb("rw_lo", [P, KD, NE], F32R)
        lam4 = sb("lam4", [P, 4])
        nlam = sb("nlam", [P, LAYERS])
        subg = sb("subg", [P, LAYERS])
        with ExitStack() as att:
            qk = [sb(f"qk{i}", [P, 8, T], scope=att) for i in range(2)]
            v = sb("v", [P, 3, D], scope=att)
            gate = sb("gate", [P, 16, T], scope=att)
            score = sb("score", [P, 2, 432], scope=att)
            aT = sb("aT", [P, 2, 656], scope=att)
            o_raw = sb("o_raw", [P, T], scope=att)
            mx = sb("mx", [P, 6], scope=att)
            nmx = sb("nmx", [P, 2, 6], scope=att)
            sm = sb("sm", [P, 2, 6], scope=att)
            rs = sb("rs", [P, 6], scope=att)
            aT_row = aT[:, :, :].rearrange("p a b -> p (a b)")
            fz = aT_row[0:8, 0:3 * T].rearrange("p (a b) -> p a b", a=3)
            rope_t = aT_row[:, 3 * T:4 * T]
            cneg = gate[0:8, 15, :]
            o_sq = sq[:, 0, :]
            o_rs = sq[:, 1, :]
        with ExitStack() as ffn:
            ffh_hi = sb("ffh_hi", [P, FT, T], F32R, scope=ffn)
            ffh_lo = sb("ffh_lo", [P, FT, T], F32R, scope=ffn)
            gbuf = sb("gbuf", [P, 2, T], scope=ffn)
            ubuf = sb("ubuf", [P, 2, T], scope=ffn)
        with ExitStack() as moe:
            xt_hi = sb("xt_hi", [P, 2, D], F32R, scope=moe)
            xt_lo = sb("xt_lo", [P, 2, D], F32R, scope=moe)
            xg_hi = sb("xg_hi", [P, D], F32R, scope=moe)
            xg_lo = sb("xg_lo", [P, D], F32R, scope=moe)
            sg = sb("sg", [P, 512], scope=moe)
            hb = sb("hb", [P, 512], scope=moe)
            hT_hi = sb("hT_hi", [P, 512], F32R, scope=moe)
            hT_lo = sb("hT_lo", [P, 512], F32R, scope=moe)
            y_hi = sb("y_hi", [P, D], F32R, scope=moe)
            y_lo = sb("y_lo", [P, D], F32R, scope=moe)
            pick = sb("pick", [P, 2, P], F32R, scope=moe)
            pickw = sb("pickw", [P, 2, P], scope=moe)
            put_hi = sb("put_hi", [P, 2 * P], F32R, scope=moe)
            put_lo = sb("put_lo", [P, 2 * P], F32R, scope=moe)
            ident_r = sb("ident_r", [P, P], F32R, scope=moe)
            lg = sb("lg", [P, 2, NE], scope=moe)
            eq = sb("eq", [P, 2, NE], scope=moe)
            sel1 = sb("sel1", [P, 2, NE], scope=moe)
            sel2 = sb("sel2", [P, 2, NE], scope=moe)
            mask = sb("mask", [P, 2, NE], scope=moe)
            comb = sb("comb", [P, 2, NE + 1], scope=moe)
            pos = sb("pos", [P, 2, NE + 1], scope=moe)
            top = sb("top", [P, 8, 2], scope=moe)
            cnt = sb("cnt", [P, 3, NE], scope=moe)
            tab_f = sb("tab_f", [P, 4], scope=moe)
            tab = sb("tab", [P, 4], I32, scope=moe)
            outb = sb("outb", [P, KD, SEQ], scope=moe)

        PJ = [bank("pj0"), bank("pj1")]
        SB = [bank("s0"), bank("s1")]
        TP = [bank("tp0"), bank("tp1"), bank("tp2")]
        OB = bank("ob")

        params_in = sem("params_in")
        x_in = sem("x_in")
        pool_set = sem("pool_set")
        small_hi = sem("small_hi")
        small_lo = sem("small_lo")
        lam_sum = sem("lam_sum")
        lam_exp = sem("lam_exp")
        lam_ready = sem("lam_ready")
        landed = [sem(f"landed{i}") for i in range(NRAW)]
        hi_done = sem("hi_done")
        lo_done = sem("lo_done")
        piece_used = sem("piece_used")
        x_hi_done = sem("x_hi_done")
        x_lo_done = sem("x_lo_done")
        sq_ready = sem("sq_ready")
        stat_done = sem("stat_done")
        rstd_ready = sem("rstd_ready")
        rt_psum = sem("rt_psum")
        rt_ready = sem("rt_ready")
        strip_done = sem("strip_done")
        proj_free = sem("proj_free")
        rot_done = sem("rot_done")
        rope_done = sem("rope_done")
        fz_ready = sem("fz_ready")
        fz_act = sem("fz_act")
        cneg_ready = sem("cneg_ready")
        gate_e = sem("gate_e")
        merged = sem("merged")
        s_done = sem("s_done")
        s_free = sem("s_free")
        nmx_ready = sem("nmx_ready")
        exp_done = sem("exp_done")
        a_ready = sem("a_ready")
        tr_done = sem("tr_done")
        aT_ready = sem("aT_ready")
        pv_done = sem("pv_done")
        o_free = sem("o_free")
        o_sq_ready = sem("o_sq_ready")
        o_stat = sem("o_stat")
        o_rs_ready = sem("o_rs_ready")
        o_norm = sem("o_norm")
        o_hi = sem("o_hi")
        o_lo = sem("o_lo")
        silu_f = sem("silu_f")
        ffh = sem("ffh")
        ffh_hi_done = sem("ffh_hi_done")
        ffh_lo_done = sem("ffh_lo_done")
        logit_done = sem("logit_done")
        xt_psum = sem("xt_psum")
        xt_hi_done = sem("xt_hi_done")
        xt_lo_done = sem("xt_lo_done")
        ident_done = sem("ident_done")
        top_diff = sem("top_diff")
        top_exp = sem("top_exp")
        mask_ready = sem("mask_ready")
        rank_done = sem("rank_done")
        table_ready = sem("table_ready")
        silu_done = sem("silu_done")
        hm_done = sem("hm_done")
        hT_psum = sem("hT_psum")
        hT_hi_done = sem("hT_hi_done")
        hT_lo_done = sem("hT_lo_done")
        y_hi_done = sem("y_hi_done")
        y_lo_done = sem("y_lo_done")
        pick_ready = sem("pick_ready")
        xg_psum = sem("xg_psum")
        xg_hi_done = sem("xg_hi_done")
        xg_lo_done = sem("xg_lo_done")
        put_psum = sem("put_psum")
        put_hi_done = sem("put_hi_done")
        put_lo_done = sem("put_lo_done")
        sc_psum = sem("sc_psum")
        sc_add = sem("sc_add")
        h_final = sem("h_final")
        out_ready = sem("out_ready")
        out_done = sem("out_done")
        dve_chain = sem("dve_chain")
        dve_chain2 = sem("dve_chain2")
        act_chain = sem("act_chain")

        def k_major(ap):
            return ap.rearrange("(k p) n -> p k n", p=P)

        def dense_source(l, j):
            if j < 12:
                c = (0, 512, 1536, 2048, 1024, 2560)[j // 2] + 256 * (j % 2)
                return k_major(w_in[l, :, c:c + 256])
            if j < 20:
                c = GATE_COL + 256 * (j - 12)
                return k_major(w_in[l, :, c:c + 256])
            if j < 24:
                w = w_bd if j < 22 else w_bf
                c = 512 * (j % 2)
                return k_major(w[l, :, c:c + 512])
            if j < MIX_PIECES:
                c = 256 * (j - 24)
                return k_major(w_out[l, :, c:c + 256])
            j -= MIX_PIECES
            if j < 2 * FFN_BLOCKS:
                w = f_u if j % 2 else f_g
                c = 256 * (j // 2)
                return k_major(w[0, :, c:c + 256])
            dp, part = divmod(j - 2 * FFN_BLOCKS, 3)
            k0, nk = DOWN_K[part]
            return k_major(f_d[0, P * k0:P * (k0 + nk), 256 * dp:256 * dp + 256])

        def dense_cols(j):
            j -= MIX_PIECES + 2 * FFN_BLOCKS
            return 256 * DOWN_K[j % 3][1] if j >= 0 else COLS

        def job_order():
            order = [("g", 0, 0), ("g", 0, 1), ("u", 0, 0), ("u", 0, 1)]
            for n in range(1, UNITS):
                order += [("g", n, 0), ("g", n, 1), ("u", n, 0), ("u", n, 1), ("d", n - 1, 0), ("d", n - 1, 1)]
            return order + [("d", UNITS - 1, 0), ("d", UNITS - 1, 1)]

        def expert_source(e, kind, n, half):
            if kind == "d":
                r = 512 * n + 256 * half
                return k_major(m_d[0, e, r:r + 256, :])
            w = m_g if kind == "g" else m_u
            return k_major(w[0, e, 512 * half:512 * half + 512, 512 * n:512 * n + 512])

        def uses(j, turn):
            return j // NRAW + 1 + turn * (JOB // NRAW)

        block = ctx.enter_context(nc.Block())

        @block.sync
        def _(sp):
            sp.dma_start(cst[:, :], consts).then_inc(params_in, 16)
            sp.dma_start(vec[:, :], vecs).then_inc(params_in, 16)
            sp.dma_start(sq[:, :, :].rearrange("p a b -> p (a b)")[:, 0:512], lam).then_inc(params_in, 16)
            sp.dma_start(h[:, :, :], xT).then_inc(x_in, 16)

            def load(j, source, turn=0):
                s = j % NRAW
                if j >= NRAW:
                    sp.wait_ge(lo_done, turn * JOB + (j - NRAW + 1))
                n = source.shape[1] * source.shape[2]
                sp.dma_start(raw[:, s, 0:n].rearrange("p (k c) -> p k c", k=source.shape[1]),
                             source).then_inc(landed[s], 16)

            for l in range(LAYERS):
                for j in range(MIX_PIECES + (FFN_PIECES if l == 0 else 0)):
                    load(l * LAYER1 + j, dense_source(l, j))
            with sp.Fori(0, NE) as e:
                for q, (kind, n, half) in enumerate(job_order()):
                    load(MOE0 + q, expert_source(e, kind, n, half), e)
            for q in range(AHEAD):
                load(MOE0 + NE * JOB + q, consts[:, 0:16].rearrange("p (a b) -> p a b", a=1))
            sp.wait_ge(table_ready, 1)
            over = sp.value_load(tab[0:1, 3:4], min_val=0, max_val=MAX_OVER)
            with sp.Fori(0, MAX_OVER) as o:
                with sp.If(o < over):
                    e = sp.value_load(tab[0:1, bass.ds(o, 1)], min_val=0, max_val=NE - 1)
                    for q, (kind, n, half) in enumerate(job_order()):
                        load(OVER0 + q, expert_source(e, kind, n, half), o)
            for c in range(KD):
                sp.wait_ge(out_ready, c + 1)
                sp.dma_start(outT[:, c, :], outb[:, c, :]).then_inc(out_done, 16)
            sp.wait_ge(out_done, 16 * KD)
            for s in range(AHEAD):
                sp.wait_ge(hi_done, MOE0 + NE * JOB + AHEAD)

        @block.gpsimd
        def _(pool):
            pool.memset(ones[:, :], 1.0).then_inc(pool_set, 1)
            pool.memset(eps[:, :], EPS).then_inc(pool_set, 1)
            pool.memset(ff_hi[:, :].bitcast(F32), 0.0).then_inc(pool_set, 1)
            pool.memset(ff_lo[:, :].bitcast(F32), 0.0).then_inc(pool_set, 1)

        @block.scalar
        def _(act):
            link = Chain(act, act_chain)

            def split(j, turn=0, skipped=0, cols=COLS):
                act.wait_ge(landed[j % NRAW], uses(j, turn) * 16)
                if NSPLIT <= j < MOE0 + NSPLIT:
                    act.wait_ge(strip_done, strips_to_piece(j - NSPLIT))
                elif j >= NSPLIT:
                    act.wait_ge(piece_used, turn * JOB + (j - NSPLIT + 1 - skipped - MOE0))
                act.activation(w_hi[:, j % NSPLIT, 0:cols], raw[:, j % NRAW, 0:cols], ACT.Copy).then_inc(hi_done, 1)

            def split_dense(l, j):
                if j < MIX_PIECES + (FFN_PIECES if l == 0 else 0):
                    split(l * LAYER1 + j, cols=dense_cols(j))
                else:
                    j -= MIX_PIECES + (FFN_PIECES if l == 0 else 0)
                    split((LAYER1 if l == 0 else MOE0) + j)

            def x_part(n, c, gain):
                act.activation(x_hi[n % 2][:, c, :], h[:, c, :], ACT.Copy, scale=gain).then_inc(x_hi_done, 1)
                square(n, c)

            def square(n, c):
                i = 8 * n + c
                if i >= 2:
                    act.wait_ge(stat_done, i - 1)
                act.activation(sq[:, c % 2, :], h[:, c, :], ACT.Square).then_inc(sq_ready, 1)

            def rstd(n):
                act.wait_ge(stat_done, 8 * n + 8)
                link(act.activation(rb[:, :], OB[:, 0:T], ACT.Ln, bias=eps[:, 0:1], scale=1.0 / D))
                act.activation(rb[:, :], rb[:, :], ACT.Exp, scale=-0.5).then_inc(rstd_ready, 1)

            act.wait_ge(params_in, 48)
            act.wait_ge(pool_set, 4)
            act.activation(ff_hi[:, 0:128], vec[:, V_FF:V_FF + 128], ACT.Copy).then_inc(small_hi, 1)
            act.activation(rw_hi[:, :, :].rearrange("p a b -> p (a b)"), vec[:, V_RT:V_RT + 64], ACT.Copy)\
                .then_inc(small_hi, 1)
            act.wait_ge(lam_sum, 4)
            act.activation(lam4[:, :], lam4[:, :], ACT.Exp).then_inc(lam_exp, 1)
            act.wait_ge(x_in, 16)
            for c in range(KD):
                x_part(0, c, vec[:, V_GMIX + c:V_GMIX + c + 1])
            for j in range(AHEAD):
                split_dense(0, j)
            rstd(0)

            def attention_exp(l, u):
                un = 8 * l + u
                act.wait_ge(nmx_ready, un + 1)
                for m in range(2):
                    for i, (c0, w) in enumerate(SEG):
                        k = 3 * m + i
                        ins = act.activation(score[:, m, c0:c0 + w], score[:, m, c0:c0 + w], ACT.Exp,
                                             bias=nmx[:, u % 2, k:k + 1], accum_out=sm[:, u % 2, k:k + 1])
                ins.then_inc(exp_done, 1)

            def evacuate_aT(l, u):
                un = 8 * l + u
                act.wait_ge(tr_done, un + 1)
                if un:
                    act.wait_ge(pv_done, un)
                heads = 1 if u < 4 else 2
                for m in range(heads):
                    act.activation(aT[:, m, 0:384], TP[m][:, 0:384], ACT.Copy)
                    act.activation(aT[0:16, m, 384:400], TP[m][0:16, 384:400], ACT.Copy)
                act.activation(aT[0:16, 0:heads, 400:656],
                               TP[2][0:16, 0:256 * heads].rearrange("p (m c) -> p m c", m=heads),
                               ACT.Copy).then_inc(aT_ready, 1)

            def o_square(l, u):
                act.wait_ge(o_free, 4 * l + u + 1)
                act.activation(o_sq, o_raw[:, :], ACT.Square).then_inc(o_sq_ready, 1)

            def o_rstd(l, u):
                act.wait_ge(o_stat, 4 * l + u + 1)
                link(act.activation(o_rs, TP[1][:, 0:T], ACT.Ln, bias=eps[:, 0:1], scale=1.0 / P))
                act.activation(o_rs, o_rs, ACT.Exp, scale=-0.5).then_inc(o_rs_ready, 1)

            def o_part(l, u):
                if u < 4:
                    act.wait_ge(o_norm, 4 * l + u + 1)
                    source = o_raw[:, :]
                else:
                    act.wait_ge(pv_done, 8 * l + u + 1)
                    source = OB[:, 0:T]
                act.activation(x_hi[1][:, u, :], source, ACT.Copy).then_inc(o_hi, 1)

            for l in range(LAYERS):
                for j in range(12):
                    split_dense(l, j + AHEAD)
                    if j == 1:
                        act.wait_ge(fz_ready, l + 1)
                        link(act.activation(fz[:, 1, :], fz[:, 0, :], ACT.Abs))
                        link(act.activation(fz[:, 1, :], fz[:, 1, :], ACT.Exp, scale=-1.0))
                        act.activation(fz[:, 1, :], fz[:, 1, :], ACT.Ln, bias=1.0).then_inc(fz_act, 1)
                for u in range(8):
                    attention_exp(l, u)
                    for i in range(2):
                        g = 2 * u + i
                        act.wait_ge(proj_free, l * (MIX_TILES + FFN_TILES) + GATE_TILE + g + 1)
                        act.activation(gate[:, g, :], gate[:, g, :], ACT.Exp, scale=-1.0).then_inc(gate_e, 1)
                    split_dense(l, 12 + u + AHEAD)
                    if 1 <= u <= 4:
                        o_rstd(l, u - 1)
                    evacuate_aT(l, u)
                    if 1 <= u <= 4:
                        o_part(l, u - 1)
                    if u < 4:
                        o_square(l, u)
                    else:
                        o_part(l, u)
                split_dense(l, 20 + AHEAD)
                split_dense(l, 21 + AHEAD)
                for j in range(22, 24):
                    for i in range(4):
                        c = 4 * (j - 22) + i
                        act.wait_ge(merged, 8 * l + c + 1)
                        act.activation(x_hi[0][:, c, :], gate[:, 8 + c, :], ACT.Copy).then_inc(x_hi_done, 1)
                    split_dense(l, j + AHEAD)
                n = 2 * l + 1
                for j in range(24, 28):
                    for c in (2 * (j - 24), 2 * (j - 24) + 1):
                        act.wait_ge(proj_free, l * (MIX_TILES + FFN_TILES) + OUT_TILE + c + 1)
                        x_part(n, c, vec[:, V_GFFN + 8 * l + c:V_GFFN + 8 * l + c + 1])
                    split_dense(l, j + AHEAD)
                rstd(n)
                if l == 0:
                    for b in range(FFN_BLOCKS):
                        for i in range(2):
                            act.wait_ge(proj_free, MIX_TILES + 4 * b + i + 1)
                            act.activation(gbuf[:, i, :], gbuf[:, i, :], ACT.Silu).then_inc(silu_f, 1)
                        split_dense(0, MIX_PIECES + 2 * b + AHEAD)
                        for i in range(2):
                            act.wait_ge(ffh, 2 * b + i + 1)
                            act.activation(ffh_hi[:, 2 * b + i, :], ubuf[:, i, :], ACT.Copy).then_inc(ffh_hi_done, 1)
                        split_dense(0, MIX_PIECES + 2 * b + 1 + AHEAD)
                    for dp in range(4):
                        for part in range(3):
                            if part == 2:
                                for c in (2 * dp, 2 * dp + 1):
                                    act.wait_ge(proj_free, DOWN_TILE + c + 1)
                                    x_part(2, c, vec[:, V_GMIX + 8 + c:V_GMIX + 8 + c + 1])
                            split_dense(0, MIX_PIECES + 2 * FFN_BLOCKS + 3 * dp + part + AHEAD)
                    rstd(2)

            link(act.activation(ident_r[:, :], cst[:, C_ID:C_ID + P], ACT.Copy))
            act.nop().then_inc(ident_done, 1)
            act.wait_ge(rt_ready, 3)
            for i in range(4):
                tt, half = divmod(i, 2)
                act.wait_ge(xt_psum, i + 1)
                act.activation(xt_hi[:, tt, 512 * half:512 * half + 512], XT_BANK(SB, TP, i)[:, :], ACT.Copy,
                               scale=rt[:, tt + 1:tt + 2]).then_inc(xt_hi_done, 1)
            act.wait_ge(top_diff, 1)
            act.activation(top[:, 4, :], top[:, 3, :], ACT.Exp).then_inc(top_exp, 1)

            def xg_part(g):
                act.wait_ge(xg_psum, g + 1)
                act.activation(xg_hi[:, 0:512], SB[0][:, :], ACT.Copy)
                act.activation(xg_hi[:, 512:1024], SB[1][:, :], ACT.Copy).then_inc(xg_hi_done, 1)

            def put_part(s):
                act.wait_ge(put_psum, s + 1)
                act.activation(put_hi[:, :], OB[:, 0:2 * P], ACT.Copy).then_inc(put_hi_done, 1)

            def job(J, j0, turn, skipped, main):
                q = 0

                def used():
                    nonlocal q
                    if main or q + AHEAD < JOB:
                        split(j0 + q + AHEAD, turn, skipped)
                    q += 1

                def hT_part(n):
                    act.wait_ge(hT_psum, J * UNITS + (n + 1))
                    act.activation(hT_hi[:, :], TP[0][:, :], ACT.Copy).then_inc(hT_hi_done, 1)

                if not main:
                    for k in range(AHEAD):
                        split(j0 + k, turn, skipped)
                    xg_part(J + 1)
                    put_part(J)
                for n in range(UNITS):
                    used()
                    if n == 2 and main:
                        put_part(J)
                    act.wait_ge(piece_used, J * JOB + (6 * n if n else 2))
                    act.activation(sg[:, :], (PJ if n % 2 == 0 else SB)[0][:, :], ACT.Silu).then_inc(silu_done, 1)
                    used()
                    if n:
                        hT_part(n - 1)
                    used()
                    if n == UNITS - 1:
                        hT_part(n)
                        if main:
                            xg_part(J + 1)
                    used()
                    if n:
                        used()
                        used()
                used()
                act.wait_ge(piece_used, J * JOB + JOB)
                act.activation(y_hi[:, 0:512], TP[1][:, :], ACT.Copy)
                act.activation(y_hi[:, 512:1024], TP[2][:, :], ACT.Copy).then_inc(y_hi_done, 1)
                used()

            act.nop().then_inc(silu_done, 1)
            xg_part(0)
            with act.Fori(0, NE) as e:
                job(e, MOE0, e, 0, True)
            act.wait_ge(table_ready, 1)
            over = act.value_load(tab[0:1, 3:4], min_val=0, max_val=MAX_OVER)
            with act.Fori(0, MAX_OVER) as o:
                with act.If(o < over):
                    job(o + NE, OVER0, o, AHEAD, False)
            act.wait_ge(h_final, 1)
            for c in range(KD):
                square(4, c)
            act.wait_ge(stat_done, 40)
            link(act.activation(rb[:, :], OB[:, 0:T], ACT.Ln, bias=eps[:, 0:1], scale=1.0 / D))
            act.activation(rb[:, :], rb[:, :], ACT.Exp, scale=-0.5).then_inc(rstd_ready, 1)

        @block.vector
        def _(dve):
            link = Chain(dve, dve_chain)

            def split(j, turn=0, cols=COLS):
                dve.wait_ge(hi_done, turn * JOB + (j + 1))
                dve.tensor_tensor(w_lo[:, j % NSPLIT, 0:cols], raw[:, j % NRAW, 0:cols],
                                  w_hi[:, j % NSPLIT, 0:cols].bitcast(F32), ALU.subtract).then_inc(lo_done, 1)

            def split_dense(l, j):
                if j < MIX_PIECES + (FFN_PIECES if l == 0 else 0):
                    split(l * LAYER1 + j, cols=dense_cols(j))
                else:
                    j -= MIX_PIECES + (FFN_PIECES if l == 0 else 0)
                    split((LAYER1 if l == 0 else MOE0) + j)

            def x_part(n, c, gain):
                dve.wait_ge(x_hi_done, X_HI_COUNT(n) + c + 1)
                dve.scalar_tensor_tensor(x_lo[n % 2][:, c, :], h[:, c, :], gain, x_hi[n % 2][:, c, :].bitcast(F32),
                                         ALU.mult, ALU.subtract).then_inc(x_lo_done, 1)

            dve.wait_ge(params_in, 48)
            lam_raw = sq[:, :, :].rearrange("p a b -> p (a b)")
            for k in range(4):
                dve.tensor_tensor_reduce(out=o_raw[:, 64 * k:64 * k + 64], in0=lam_raw[:, 128 * k:128 * k + 64],
                                         in1=lam_raw[:, 128 * k + 64:128 * k + 128], scale=1.0, scalar=0.0,
                                         op0=ALU.mult, op1=ALU.add, accum_out=lam4[:, k:k + 1]).then_inc(lam_sum, 1)
            dve.wait_ge(small_hi, 2)
            dve.tensor_tensor(ff_lo[:, 0:128], vec[:, V_FF:V_FF + 128], ff_hi[:, 0:128].bitcast(F32),
                              ALU.subtract).then_inc(small_lo, 1)
            dve.tensor_tensor(rw_lo[:, :, :].rearrange("p a b -> p (a b)"), vec[:, V_RT:V_RT + 64],
                              rw_hi[:, :, :].rearrange("p a b -> p (a b)").bitcast(F32),
                              ALU.subtract).then_inc(small_lo, 1)
            dve.wait_ge(lam_exp, 1)
            for l in range(LAYERS):
                link(dve.tensor_tensor(nlam[:, l:l + 1], lam4[:, 2 * l + 1:2 * l + 2], lam4[:, 2 * l:2 * l + 1],
                                       ALU.subtract))
                link(dve.tensor_scalar(nlam[:, l:l + 1], nlam[:, l:l + 1], -lam_init[l], None, ALU.add))
                link(dve.tensor_scalar(subg[:, l:l + 1], vec[:, V_SUB + l:V_SUB + l + 1], 1.0 - lam_init[l], None,
                                       ALU.mult))
            for c in range(KD):
                x_part(0, c, vec[:, V_GMIX + c:V_GMIX + c + 1])
            for j in range(AHEAD):
                split_dense(0, j)

            def attention_max(l, u):
                un = 8 * l + u
                for m in range(2):
                    dve.wait_ge(s_done, 2 * un + m + 1)
                    for i, (c0, w) in enumerate(SEG):
                        k = 3 * m + i
                        ins = dve.tensor_tensor_reduce(
                            out=score[:, m, c0:c0 + w], in0=SB[m][:, c0:c0 + w],
                            in1=cst[:, C_MASK + c0:C_MASK + c0 + w], scale=SCALE, scalar=-3e38,
                            op0=ALU.add, op1=ALU.max, accum_out=mx[:, k:k + 1])
                    ins.then_inc(s_free, 1)
                dve.wait_ge(s_free, 2 * un + 2)
                dve.tensor_scalar(nmx[:, u % 2, :], mx[:, :], -1.0, None, ALU.mult).then_inc(nmx_ready, 1)
                dve.wait_ge(nmx_ready, un + 1)

            def attention_normalise(l, u):
                un = 8 * l + u
                dve.wait_ge(exp_done, un + 1)
                link(dve.reciprocal(rs[:, :], sm[:, u % 2, :]))
                if u < 4:
                    link(dve.tensor_scalar(rs[:, 3:6], rs[:, 3:6], nlam[:, l:l + 1], None, ALU.mult))
                    for i, (c0, w) in enumerate(SEG):
                        a = score[:, 0, c0:c0 + w]
                        ins = dve.tensor_scalar(a, a, rs[:, i:i + 1], None, ALU.mult)
                    link(ins)
                    for i, (c0, w) in enumerate(SEG):
                        a = score[:, 0, c0:c0 + w]
                        ins = dve.scalar_tensor_tensor(a, score[:, 1, c0:c0 + w], rs[:, 3 + i:4 + i], a,
                                                       ALU.mult, ALU.add)
                else:
                    for m in range(2):
                        for i, (c0, w) in enumerate(SEG):
                            a = score[:, m, c0:c0 + w]
                            ins = dve.tensor_scalar(a, a, rs[:, 3 * m + i:3 * m + i + 1], None, ALU.mult)
                ins.then_inc(a_ready, 1)
                dve.wait_ge(a_ready, un + 1)

            def free(t):
                dve.wait_ge(proj_free, t + 1)

            def rope(l, i):
                dve.wait_ge(rot_done, 8 * l + i + 1)
                link(dve.tensor_tensor(rope_t, TP[1 + i % 2][:, 0:T], cst[:, C_SIN:C_SIN + T], ALU.mult))
                link(dve.tensor_tensor(qk[0][:, i, :], qk[0][:, i, :], cst[:, C_COS:C_COS + T], ALU.mult))
                dve.tensor_tensor(qk[0][:, i, :], qk[0][:, i, :], rope_t, ALU.add).then_inc(rope_done, 1)
                dve.wait_ge(rope_done, 8 * l + i + 1)

            def o_evacuate(l, u):
                un = 8 * l + u
                if u < 4:
                    dve.wait_ge(pv_done, un + 1)
                    dve.tensor_copy(o_raw[:, :], OB[:, 0:T]).then_inc(o_free, 1)
                    dve.wait_ge(o_free, 4 * l + u + 1)
                else:
                    dve.wait_ge(o_hi, un + 1)
                    dve.tensor_tensor(x_lo[1][:, u, :], OB[:, 0:T], x_hi[1][:, u, :].bitcast(F32),
                                      ALU.subtract).then_inc(o_lo, 1)

            def o_normalise(l, u):
                dve.wait_ge(o_rs_ready, 4 * l + u + 1)
                dve.scalar_tensor_tensor(o_raw[:, :], o_raw[:, :], subg[:, l:l + 1], o_rs, ALU.mult,
                                         ALU.mult).then_inc(o_norm, 1)
                dve.wait_ge(o_norm, 4 * l + u + 1)

            def o_part(l, u):
                dve.wait_ge(o_hi, 8 * l + u + 1)
                dve.tensor_tensor(x_lo[1][:, u, :], o_raw[:, :], x_hi[1][:, u, :].bitcast(F32),
                                  ALU.subtract).then_inc(o_lo, 1)
                dve.wait_ge(o_lo, 8 * l + u + 1)

            for l in range(LAYERS):
                t0 = l * (MIX_TILES + FFN_TILES)
                dve.wait_ge(rstd_ready, 2 * l + 1)
                dve.wait_ge(strip_done, strips_to_tile(t0))
                dve.tensor_tensor(fz[:, 0, :], PJ[t0 % 2][0:8, 0:T], rb[0:8, :], ALU.mult).then_inc(proj_free, 1)
                free(t0)
                dve.tensor_scalar(fz[:, 0, :], fz[:, 0, :], vec[0:8, V_BF + l:V_BF + l + 1], None,
                                  ALU.add).then_inc(fz_ready, 1)
                dve.wait_ge(fz_ready, l + 1)
                for j in range(8):
                    for i in range(2):
                        t = t0 + 1 + 2 * j + i
                        dve.wait_ge(strip_done, strips_to_tile(t))
                        dve.tensor_tensor(qk[j // 4][:, (2 * j + i) % 8, :], PJ[t % 2][:, 0:T], rb[:, :],
                                          ALU.mult).then_inc(proj_free, 1)
                    free(t)
                    split_dense(l, j + AHEAD)
                    if 1 <= j <= 4:
                        rope(l, 2 * j - 2)
                        rope(l, 2 * j - 1)
                    if j == 0:
                        dve.wait_ge(rt_psum, l + 1)
                        dve.tensor_copy(rt[:, :], TP[0][:, 0:6].rearrange("p (a b) -> p a b", b=2)[:, :, 0])\
                            .then_inc(rt_ready, 1)
                    if j == 5:
                        dve.wait_ge(fz_act, l + 1)
                        link(dve.tensor_scalar(fz[:, 0, :], fz[:, 0, :], 0.0, None, ALU.min))
                        link(dve.tensor_tensor(fz[:, 2, :], fz[:, 0, :], fz[:, 1, :], ALU.subtract))
                        a, s = 2, 1
                        while s < T:
                            b = 1 if a == 2 else 2
                            dve.tensor_copy(fz[:, b, 0:s], fz[:, a, 0:s])
                            link(dve.tensor_tensor(fz[:, b, s:T], fz[:, a, s:T], fz[:, a, 0:T - s], ALU.add))
                            a, s = b, 2 * s
                        dve.tensor_scalar(cneg, fz[:, a, :], -1.0 / SCALE, None, ALU.mult)\
                            .then_inc(cneg_ready, 1)
                        dve.wait_ge(cneg_ready, l + 1)
                for j in range(8, 12):
                    for w in range(3):
                        t = t0 + V_TILE + 3 * (j - 8) + w
                        dve.wait_ge(rt_ready, l + 1)
                        dve.wait_ge(strip_done, strips_to_tile(t))
                        dve.tensor_scalar(v[:, w, 256 * (j - 8):256 * (j - 8) + 256], PJ[t % 2][:, 0:256],
                                          rt[:, w:w + 1], None, ALU.mult).then_inc(proj_free, 1)
                    free(t)
                    split_dense(l, j + AHEAD)
                attention_max(l, 0)
                for u in range(8):
                    for i in range(2):
                        g = 2 * u + i
                        t = t0 + GATE_TILE + g
                        dve.wait_ge(strip_done, strips_to_tile(t))
                        dve.tensor_tensor(gate[:, g, :], PJ[t % 2][:, 0:T], rb[:, :], ALU.mult).then_inc(proj_free, 1)
                        free(t)
                        if i == 0:
                            attention_normalise(l, u)
                    split_dense(l, 12 + u + AHEAD)
                    dve.wait_ge(gate_e, 16 * l + 2 * u + 2)
                    link(dve.tensor_scalar(gate[:, 2 * u:2 * u + 2, :], gate[:, 2 * u:2 * u + 2, :], 1.0, None,
                                           ALU.add))
                    link(dve.reciprocal(gate[:, 2 * u:2 * u + 2, :], gate[:, 2 * u:2 * u + 2, :]))
                    if 1 <= u <= 4:
                        o_normalise(l, u - 1)
                        o_part(l, u - 1)
                    if u < 7:
                        attention_max(l, u + 1)
                    o_evacuate(l, u)
                for j in range(20, 24):
                    for i in range(4):
                        c = 4 * (j % 2) + i
                        t = t0 + (BD_TILE if j < 22 else BF_TILE) + c
                        g = c if j < 22 else 8 + c
                        dve.wait_ge(strip_done, strips_to_tile(t))
                        dve.tensor_tensor(gate[:, g, :], PJ[t % 2][:, 0:T], gate[:, g, :], ALU.mult)\
                            .then_inc(proj_free, 1)
                        free(t)
                        if j >= 22:
                            dve.tensor_tensor(gate[:, g, :], gate[:, g, :], gate[:, c, :], ALU.add)\
                                .then_inc(merged, 1)
                            dve.wait_ge(merged, 8 * l + c + 1)
                            dve.wait_ge(x_hi_done, X_HI_COUNT(2 * l + 1) - 8 + c + 1)
                            dve.tensor_tensor(x_lo[0][:, c, :], gate[:, g, :], x_hi[0][:, c, :].bitcast(F32),
                                              ALU.subtract).then_inc(x_lo_done, 1)
                    split_dense(l, j + AHEAD)
                n = 2 * l + 1
                for j in range(24, 28):
                    for i in range(2):
                        c = 2 * (j - 24) + i
                        t = t0 + OUT_TILE + c
                        dve.wait_ge(strip_done, strips_to_tile(t))
                        dve.tensor_tensor(h[:, c, :], PJ[t % 2][:, 0:T], h[:, c, :], ALU.add).then_inc(proj_free, 1)
                        free(t)
                        x_part(n, c, vec[:, V_GFFN + 8 * l + c:V_GFFN + 8 * l + c + 1])
                    split_dense(l, j + AHEAD)
                if l == 0:
                    f0 = MIX_TILES
                    dve.wait_ge(rstd_ready, 2)
                    for b in range(FFN_BLOCKS):
                        for i in range(2):
                            t = f0 + 4 * b + i
                            dve.wait_ge(strip_done, strips_to_tile(t))
                            dve.tensor_tensor(gbuf[:, i, :], PJ[t % 2][:, 0:T], rb[:, :], ALU.mult)\
                                .then_inc(proj_free, 1)
                        split_dense(0, MIX_PIECES + 2 * b + AHEAD)
                        for i in range(2):
                            t = f0 + 4 * b + 2 + i
                            dve.wait_ge(strip_done, strips_to_tile(t))
                            dve.tensor_tensor(ubuf[:, i, :], PJ[t % 2][:, 0:T], rb[:, :], ALU.mult)\
                                .then_inc(proj_free, 1)
                            free(t)
                            dve.wait_ge(silu_f, 2 * b + i + 1)
                            dve.tensor_tensor(ubuf[:, i, :], ubuf[:, i, :], gbuf[:, i, :], ALU.mult)\
                                .then_inc(ffh, 1)
                        dve.wait_ge(ffh, 2 * b + 2)
                        split_dense(0, MIX_PIECES + 2 * b + 1 + AHEAD)
                        for i in range(2):
                            dve.wait_ge(ffh_hi_done, 2 * b + i + 1)
                            dve.tensor_tensor(ffh_lo[:, 2 * b + i, :], ubuf[:, i, :],
                                              ffh_hi[:, 2 * b + i, :].bitcast(F32), ALU.subtract)\
                                .then_inc(ffh_lo_done, 1)
                    for dp in range(4):
                        for part in range(3):
                            if part == 2:
                                for i in range(2):
                                    c = 2 * dp + i
                                    t = f0 + 4 * FFN_BLOCKS + c
                                    dve.wait_ge(strip_done, strips_to_tile(t))
                                    dve.tensor_tensor(h[:, c, :], PJ[t % 2][:, 0:T], h[:, c, :], ALU.add)\
                                        .then_inc(proj_free, 1)
                                    free(t)
                                    x_part(2, c, vec[:, V_GMIX + 8 + c:V_GMIX + 8 + c + 1])
                            split_dense(0, MIX_PIECES + 2 * FFN_BLOCKS + 3 * dp + part + AHEAD)

            dve.memset(y_hi[:, :].bitcast(F32), 0.0)
            dve.memset(y_lo[:, :].bitcast(F32), 0.0)
            dve.memset(put_hi[:, :].bitcast(F32), 0.0)
            dve.memset(put_lo[:, :].bitcast(F32), 0.0)
            dve.memset(pos[:, :, NE:NE + 1], -1.0)
            link(dve.memset(comb[:, :, NE:NE + 1], 0.0))
            dve.wait_ge(rt_psum, 3)
            dve.tensor_copy(rt[:, :], TP[0][:, 0:6].rearrange("p (a b) -> p a b", b=2)[:, :, 0]).then_inc(rt_ready, 1)
            dve.wait_ge(rt_ready, 3)
            dve.wait_ge(logit_done, 1)
            for tt in range(2):
                link(dve.tensor_scalar(lg[:, tt, :], OB[:, 8 * tt:8 * tt + 8], rt[:, tt + 1:tt + 2], None, ALU.mult))
            rev = cst[:, C_REV:C_REV + 16].rearrange("p (a b) -> p a b", a=2)

            def wide(ap):
                return ap.unsqueeze(2).broadcast_to([P, 2, NE])

            def first_max(sel, value):
                link(dve.tensor_reduce(value, lg[:, :, :], AX, ALU.max))
                link(dve.tensor_tensor(eq[:, :, :], lg[:, :, :], wide(value), ALU.is_equal))
                link(dve.tensor_tensor(eq[:, :, :], eq[:, :, :], rev, ALU.mult))
                link(dve.tensor_reduce(top[:, 2, :], eq[:, :, :], AX, ALU.max))
                link(dve.tensor_tensor(sel[:, :, :], eq[:, :, :], wide(top[:, 2, :]), ALU.is_equal))

            first_max(sel1, top[:, 0, :])
            link(dve.scalar_tensor_tensor(lg[:, :, :], sel1[:, :, :], -3e38, lg[:, :, :], ALU.mult, ALU.add))
            first_max(sel2, top[:, 1, :])
            link(dve.tensor_tensor(mask[:, :, :], sel1[:, :, :], sel2[:, :, :], ALU.add))
            dve.nop().then_inc(mask_ready, 1)
            link(dve.tensor_tensor(top[:, 3, :], top[:, 1, :], top[:, 0, :], ALU.subtract))
            dve.nop().then_inc(top_diff, 1)
            dve.wait_ge(top_exp, 1)
            link(dve.tensor_scalar(top[:, 5, :], top[:, 4, :], 1.0, None, ALU.add))
            link(dve.reciprocal(top[:, 5, :], top[:, 5, :]))
            link(dve.tensor_tensor(top[:, 6, :], top[:, 4, :], top[:, 5, :], ALU.mult))
            link(dve.tensor_tensor(sel1[:, :, :], sel1[:, :, :], wide(top[:, 5, :]), ALU.mult))
            link(dve.tensor_tensor(sel2[:, :, :], sel2[:, :, :], wide(top[:, 6, :]), ALU.mult))
            link(dve.tensor_tensor(comb[:, :, 0:NE], sel1[:, :, :], sel2[:, :, :], ALU.add))
            dve.wait_ge(rank_done, 1)
            link(dve.tensor_copy(cnt[:, :, :], OB[:, 32:56].rearrange("p (a b) -> p a b", a=3)))
            link(dve.scalar_tensor_tensor(pos[:, :, 0:NE], cnt[:, 0:2, :], 1.0, mask[:, :, :], ALU.add, ALU.mult))
            link(dve.tensor_scalar(pos[:, :, 0:NE], pos[:, :, 0:NE], -1.0, None, ALU.add))
            for i in range(4):
                tt, half = divmod(i, 2)
                dve.wait_ge(xt_hi_done, i + 1)
                dve.scalar_tensor_tensor(xt_lo[:, tt, 512 * half:512 * half + 512], XT_BANK(SB, TP, i)[:, :],
                                         rt[:, tt + 1:tt + 2],
                                         xt_hi[:, tt, 512 * half:512 * half + 512].bitcast(F32),
                                         ALU.mult, ALU.subtract).then_inc(xt_lo_done, 1)

            def build_pick(e, block):
                iota = cst[:, C_IOTA + P * block:C_IOTA + P * block + P]
                for tt in range(2):
                    where = pos[:, tt, bass.ds(e, 1)]
                    dve.tensor_scalar(pick[:, tt, :], iota, where, None, ALU.is_equal)
                    ins = dve.tensor_scalar(pickw[:, tt, :], iota, where, comb[:, tt, bass.ds(e, 1)], ALU.is_equal,
                                            ALU.mult)
                ins.then_inc(pick_ready, 1)

            build_pick(0, 0)
            o1, o2, o3 = cnt[0:1, 0, :], cnt[0:1, 1, :], cnt[0:1, 2, :]
            link(dve.tensor_scalar(o1, o3, float(P), None, ALU.is_gt))
            link(dve.tensor_reduce(tab_f[0:1, 3:4], o1, AX, ALU.add))
            for o in range(MAX_OVER):
                link(dve.tensor_tensor(o2, o1, rev[0:1, 0, :], ALU.mult))
                link(dve.tensor_reduce(tab_f[0:1, o:o + 1], o2, AX, ALU.max))
                link(dve.tensor_scalar(o2, o2, tab_f[0:1, o:o + 1], None, ALU.is_lt))
                link(dve.tensor_tensor(o1, o1, o2, ALU.mult))
                link(dve.tensor_scalar(tab_f[0:1, o:o + 1], tab_f[0:1, o:o + 1], -1.0, float(NE), ALU.mult, ALU.add))
                link(dve.tensor_scalar(tab_f[0:1, o:o + 1], tab_f[0:1, o:o + 1], float(NE - 1), None, ALU.min))
            dve.tensor_copy(tab[0:1, :], tab_f[0:1, :]).then_inc(table_ready, 1)
            dve.wait_ge(table_ready, 1)

            def xg_part(g):
                dve.wait_ge(xg_hi_done, g + 1)
                dve.tensor_tensor(xg_lo[:, 0:512], SB[0][:, :], xg_hi[:, 0:512].bitcast(F32), ALU.subtract)
                dve.tensor_tensor(xg_lo[:, 512:1024], SB[1][:, :], xg_hi[:, 512:1024].bitcast(F32),
                                  ALU.subtract).then_inc(xg_lo_done, 1)

            def put_part(s):
                dve.wait_ge(put_hi_done, s + 1)
                dve.tensor_tensor(put_lo[:, :], OB[:, 0:2 * P], put_hi[:, :].bitcast(F32), ALU.subtract)\
                    .then_inc(put_lo_done, 1)

            def add_scatter(s):
                for r in range(4):
                    dve.wait_ge(sc_psum, s * 4 + (r + 1))
                    dve.tensor_tensor(h[:, 2 * r:2 * r + 2, NMETA:T],
                                      SC_BANK(OB, SB, r)[:, :].rearrange("p (a b) -> p a b", a=2),
                                      h[:, 2 * r:2 * r + 2, NMETA:T], ALU.add).then_inc(sc_add, 1)

            def job(J, j0, turn, main, e=None):
                q = 0

                def used():
                    nonlocal q
                    if main or q + AHEAD < JOB:
                        split(j0 + q + AHEAD, turn)
                    q += 1

                def hT_part(n):
                    dve.wait_ge(hT_hi_done, J * UNITS + (n + 1))
                    dve.tensor_tensor(hT_lo[:, :], TP[0][:, :], hT_hi[:, :].bitcast(F32), ALU.subtract)\
                        .then_inc(hT_lo_done, 1)

                if not main:
                    for k in range(AHEAD):
                        split(j0 + k, turn)
                    dve.wait_ge(xg_psum, J + 1)
                    dve.wait_ge(put_psum, J)
                    build_pick(e, 1)
                    xg_part(J + 1)
                    put_part(J)
                for n in range(UNITS):
                    used()
                    if n == 2 and main:
                        put_part(J)
                    if n == 4 and main:
                        dve.wait_ge(xg_psum, J + 1)
                        dve.wait_ge(put_psum, J + 1)
                        build_pick(J + 1, 0)
                    used()
                    if n:
                        hT_part(n - 1)
                    used()
                    dve.wait_ge(silu_done, J * UNITS + (n + 2))
                    dve.wait_ge(piece_used, J * JOB + (6 * n + 2 if n else 4))
                    dve.tensor_tensor(hb[:, :], (PJ if n % 2 == 0 else SB)[1][:, :], sg[:, :], ALU.mult)\
                        .then_inc(hm_done, 1)
                    if n == UNITS - 1:
                        hT_part(n)
                        if main:
                            xg_part(J + 1)
                    used()
                    if n == 0 and main:
                        add_scatter(J)
                    if n:
                        used()
                        used()
                used()
                dve.wait_ge(y_hi_done, J + 1)
                dve.tensor_tensor(y_lo[:, 0:512], TP[1][:, :], y_hi[:, 0:512].bitcast(F32), ALU.subtract)
                dve.tensor_tensor(y_lo[:, 512:1024], TP[2][:, :], y_hi[:, 512:1024].bitcast(F32),
                                  ALU.subtract).then_inc(y_lo_done, 1)
                used()
                if not main:
                    add_scatter(J + 1)

            dve.nop().then_inc(hm_done, 1)
            dve.nop().then_inc(hT_lo_done, 1)
            dve.nop().then_inc(y_lo_done, 1)
            dve.nop().then_inc(put_lo_done, 1)
            dve.nop().then_inc(sc_add, 1)
            xg_part(0)
            with dve.Fori(0, NE) as e:
                job(e, MOE0, e, True)
            add_scatter(NE)
            over = dve.value_load(tab[0:1, 3:4], min_val=0, max_val=MAX_OVER)
            with dve.Fori(0, MAX_OVER) as o:
                with dve.If(o < over):
                    e = dve.value_load(tab[0:1, bass.ds(o, 1)], min_val=0, max_val=NE - 1)
                    job(o + NE, OVER0, o, False, e)
            dve.drain().then_inc(h_final, 1)
            dve.wait_ge(rstd_ready, 5)
            for c in range(KD):
                dve.scalar_tensor_tensor(outb[:, c, :], h[:, c, NMETA:T], vec[:, V_GFIN + c:V_GFIN + c + 1],
                                         rb[:, NMETA:T], ALU.mult, ALU.mult).then_inc(out_ready, 1)

        @block.tensor
        def _(pe):
            def mm3(out, l_hi, l_lo, r_hi, r_lo, first, last):
                pe.matmul(out, l_hi, r_hi, start=first, stop=False)
                pe.matmul(out, l_hi, r_lo, start=False, stop=False)
                return pe.matmul(out, l_lo, r_hi, start=False, stop=last)

            ident = cst[:, C_ID:C_ID + P]

            def stat(n, c):
                pe.wait_ge(sq_ready, 8 * n + c + 1)
                pe.matmul(OB[:, 0:T], ones[:, :], sq[:, c % 2, :], start=(c == 0), stop=(c == KD - 1))\
                    .then_inc(stat_done, 1)

            def row_rstd(k):
                for w in range(3):
                    ins = pe.matmul(TP[0][:, 2 * w:2 * w + 2], rb[0:1, WIN[w]:WIN[w] + P], ones[0:1, 0:2],
                                    start=True, stop=True)
                ins.then_inc(rt_psum, 1)

            def take(j, turn=0):
                pe.wait_ge(lo_done, turn * JOB + (j + 1))
                return w_hi[:, j % NSPLIT, :], w_lo[:, j % NSPLIT, :]

            def begin(t):
                if t >= 2:
                    pe.wait_ge(proj_free, t - 1)
                return PJ[t % 2]

            def stationary(t, hi, lo, width, f, k0, nk, r_hi, r_lo, r0, first=True, last=True):
                for k in range(nk):
                    c = width * k + P * f
                    ins = mm3(PJ[t % 2][:, 0:T], hi[:, c:c + P], lo[:, c:c + P], r_hi[:, r0 + k, :],
                              r_lo[:, r0 + k, :], first and k == 0, last and k == nk - 1)
                return ins

            def queries_keys(l, u):
                un = 8 * l + u
                src, i = qk[u // 4], u % 4
                if u == 0:
                    pe.wait_ge(rope_done, 8 * l + 8)
                if u == 4:
                    pe.wait_ge(cneg_ready, l + 1)
                if un:
                    pe.wait_ge(s_free, 2 * un)
                for m in range(2):
                    r = slice(64 * m, 64 * m + 64)
                    for s, (c0, w) in enumerate(SEG):
                        out = SB[m][:, c0:c0 + w]
                        ins = pe.matmul(out, src[r, i, WIN[s]:WIN[s] + P], src[r, 4 + i, 0:w], start=True,
                                        stop=(u < 4))
                        if u >= 4:
                            head = 2 * (u - 4) + m
                            ins = pe.matmul(out, cst[0:8, C_ID + head:C_ID + head + 1].to_broadcast([8, P]),
                                            cneg[:, 0:w], start=False, stop=True)
                    ins.then_inc(s_done, 1)

            def transposes(l, u):
                un = 8 * l + u
                pe.wait_ge(a_ready, un + 1)
                if un:
                    pe.wait_ge(aT_ready, un)
                if u == 0:
                    pe.wait_ge(rt_ready, l + 1)
                if u >= 4:
                    pe.wait_ge(o_rs_ready, 4 * l + 4)
                for m in range(1 if u < 4 else 2):
                    a = score[:, m, :]
                    c1, c2 = SEG[1][0], SEG[2][0]
                    for out, src in ((TP[m][:, 0:128], a[:, c1 + 16:c1 + 144]),
                                     (TP[m][:, 128:256], a[:, c2 + 16:c2 + 144]),
                                     (TP[m][:, 256:384], a[:, c2 + 144:c2 + 272]),
                                     (TP[2][0:16, 256 * m:256 * m + 128], a[:, c1:c1 + 16]),
                                     (TP[2][0:16, 256 * m + 128:256 * m + 256], a[:, c2:c2 + 16])):
                        pe.transpose(out, src, ident)
                    ins = pe.transpose(TP[m][0:16, 384:400], a[0:16, 0:16], ident[0:16, 0:16])
                ins.then_inc(tr_done, 1)

            def values(l, u):
                un = 8 * l + u
                pe.wait_ge(aT_ready, un + 1)
                if 1 <= u <= 4:
                    pe.wait_ge(o_free, 4 * l + u)
                elif un:
                    pe.wait_ge(o_lo, un)
                for m in range(1 if u < 4 else 2):
                    c, w = (P * u, P) if u < 4 else (512 + P * (u - 4) + 64 * m, 64)
                    r = slice(64 * m, 64 * m + w)
                    pe.matmul(OB[r, 0:T], v[0:16, 0, c:c + w], aT[0:16, m, 384:656], start=True, stop=False)
                    pe.matmul(OB[r, 16:T], v[:, 1, c:c + w], aT[:, m, 0:256], start=False, stop=False)
                    ins = pe.matmul(OB[r, 144:T], v[:, 2, c:c + w], aT[:, m, 256:384], start=False, stop=True)
                ins.then_inc(pv_done, 1)

            def o_statistics(l, u):
                pe.wait_ge(o_sq_ready, 4 * l + u + 1)
                pe.matmul(TP[1][:, 0:T], ones[:, :], o_sq, start=True, stop=True).then_inc(o_stat, 1)

            pe.wait_ge(pool_set, 4)
            pe.wait_ge(params_in, 48)
            for c in range(KD):
                stat(0, c)
            pe.wait_ge(small_lo, 2)
            for l in range(LAYERS):
                t0 = l * (MIX_TILES + FFN_TILES)
                p0 = l * LAYER1
                xh, xl = x_hi[0], x_lo[0]
                begin(t0)
                for k in range(KD):
                    pe.wait_ge(x_lo_done, X_HI_COUNT(2 * l) + k + 1)
                    c = 64 * l + 8 * k
                    ins = mm3(PJ[t0 % 2][:, 0:T], ff_hi[:, c:c + P], ff_lo[:, c:c + P], xh[:, k, :], xl[:, k, :],
                              k == 0, k == KD - 1)
                ins.then_inc(strip_done, 1)
                for j in range(8):
                    hi, lo = take(p0 + j)
                    for i in range(2):
                        t = t0 + 1 + 2 * j + i
                        begin(t)
                        ins = stationary(t, hi, lo, 256, i, 0, KD, xh, xl, 0)
                        ins.then_inc(strip_done, 1)
                    if j == 0:
                        pe.wait_ge(rstd_ready, 2 * l + 1)
                        row_rstd(l)
                    if 1 <= j <= 4:
                        for i in (2 * j - 2, 2 * j - 1):
                            pe.wait_ge(proj_free, t0 + 2 + i)
                            if i >= 2:
                                pe.wait_ge(rope_done, 8 * l + i - 1)
                            elif l:
                                pe.wait_ge(aT_ready, 8 * l)
                            pe.matmul(TP[1 + i % 2][:, 0:T], cst[:, C_ROT:C_ROT + P], qk[0][:, i, :], start=True,
                                      stop=True).then_inc(rot_done, 1)
                for j in range(8, 12):
                    hi, lo = take(p0 + j)
                    for w in range(3):
                        t = t0 + V_TILE + 3 * (j - 8) + w
                        begin(t)
                        for k in range(KD):
                            ins = mm3(PJ[t % 2][:, 0:256], xh[:, k, WIN[w]:WIN[w] + P], xl[:, k, WIN[w]:WIN[w] + P],
                                      hi[:, 256 * k:256 * k + 256], lo[:, 256 * k:256 * k + 256], k == 0,
                                      k == KD - 1)
                        ins.then_inc(strip_done, 1)
                pe.wait_ge(proj_free, t0 + GATE_TILE)
                queries_keys(l, 0)
                for u in range(8):
                    hi, lo = take(p0 + 12 + u)
                    for i in range(2):
                        t = t0 + GATE_TILE + 2 * u + i
                        begin(t)
                        stationary(t, hi, lo, 256, i, 0, KD, xh, xl, 0).then_inc(strip_done, 1)
                    if 1 <= u <= 4:
                        o_statistics(l, u - 1)
                    transposes(l, u)
                    if u < 7:
                        queries_keys(l, u + 1)
                    values(l, u)
                for j in range(20, 24):
                    hi, lo = take(p0 + j)
                    pe.wait_ge(o_lo, 8 * l + (4 if j < 22 else 8))
                    for i in range(4):
                        t = t0 + (BD_TILE if j < 22 else BF_TILE) + 4 * (j % 2) + i
                        begin(t)
                        stationary(t, hi, lo, 512, i, 0, 4, x_hi[1], x_lo[1], 0 if j < 22 else 4)\
                            .then_inc(strip_done, 1)
                n = 2 * l + 1
                pe.wait_ge(x_lo_done, X_HI_COUNT(n))
                for j in range(24, 28):
                    hi, lo = take(p0 + j)
                    for i in range(2):
                        c = 2 * (j - 24) + i
                        t = t0 + OUT_TILE + c
                        begin(t)
                        stationary(t, hi, lo, 256, i, 0, KD, xh, xl, 0).then_inc(strip_done, 1)
                        if c >= 1:
                            stat(n, c - 1)
                stat(n, KD - 1)
                if l == 0:
                    f0 = MIX_TILES
                    for b in range(FFN_BLOCKS):
                        for s in range(2):
                            hi, lo = take(MIX_PIECES + 2 * b + s)
                            for i in range(2):
                                t = f0 + 4 * b + 2 * s + i
                                begin(t)
                                for k in range(KD):
                                    if b == 0 and s == 0 and i == 0:
                                        pe.wait_ge(x_lo_done, X_HI_COUNT(1) + k + 1)
                                    c = 256 * k + P * i
                                    ins = mm3(PJ[t % 2][:, 0:T], hi[:, c:c + P], lo[:, c:c + P], x_hi[1][:, k, :],
                                              x_lo[1][:, k, :], k == 0, k == KD - 1)
                                ins.then_inc(strip_done, 1)
                    for dp in range(4):
                        for part, (k0, nk) in enumerate(DOWN_K):
                            hi, lo = take(MIX_PIECES + 2 * FFN_BLOCKS + 3 * dp + part)
                            pe.wait_ge(ffh_lo_done, k0 + nk)
                            for i in range(2):
                                t = f0 + 4 * FFN_BLOCKS + 2 * dp + i
                                if part == 0:
                                    begin(t)
                                ins = stationary(t, hi, lo, 256, i, 0, nk, ffh_hi, ffh_lo, k0, first=(part == 0),
                                                 last=(part == 2))
                                ins.then_inc(strip_done, 1)
                        if dp:
                            stat(2, 2 * dp - 2)
                            stat(2, 2 * dp - 1)
                    stat(2, 6)
                    stat(2, 7)

            pe.wait_ge(rstd_ready, 4)
            row_rstd(2)
            for tt in range(2):
                for k in range(KD):
                    pe.wait_ge(x_lo_done, X_HI_COUNT(3) + k + 1)
                    w = slice(WIN[tt + 1], WIN[tt + 1] + P)
                    ins = mm3(OB[:, 8 * tt:8 * tt + 8], x_hi[1][:, k, w], x_lo[1][:, k, w], rw_hi[:, k, :],
                              rw_lo[:, k, :], k == 0, k == KD - 1)
            ins.then_inc(logit_done, 1)
            pe.wait_ge(ident_done, 1)
            for i in range(4):
                tt, half = divmod(i, 2)
                w = slice(WIN[tt + 1], WIN[tt + 1] + P)
                for k in range(4):
                    out = XT_BANK(SB, TP, i)[:, P * k:P * k + P]
                    pe.matmul(out, x_hi[1][:, 4 * half + k, w], ident_r[:, :], start=True, stop=False)
                    ins = pe.matmul(out, x_lo[1][:, 4 * half + k, w], ident_r[:, :], start=False, stop=True)
                ins.then_inc(xt_psum, 1)
            pe.wait_ge(mask_ready, 1)
            tri = cst[:, C_TRI:C_TRI + P]
            pe.matmul(OB[:, 32:40], tri, mask[:, 0, :], start=True, stop=True)
            pe.matmul(OB[:, 40:48], tri, mask[:, 1, :], start=True, stop=False)
            pe.matmul(OB[:, 40:48], ones[:, :], mask[:, 0, :], start=False, stop=True)
            pe.matmul(OB[:, 48:56], ones[:, :], mask[:, 0, :], start=True, stop=False)
            pe.matmul(OB[:, 48:56], ones[:, :], mask[:, 1, :], start=False, stop=True).then_inc(rank_done, 1)

            def gather(g):
                pe.wait_ge(pick_ready, g + 1)
                for c in range(KD):
                    out = SB[c // 4][:, P * (c % 4):P * (c % 4) + P]
                    for tt in range(2):
                        pe.matmul(out, xt_hi[:, tt, P * c:P * c + P], pick[:, tt, :], start=(tt == 0), stop=False)
                        ins = pe.matmul(out, xt_lo[:, tt, P * c:P * c + P], pick[:, tt, :], start=False,
                                        stop=(tt == 1))
                ins.then_inc(xg_psum, 1)

            def put_transpose(s):
                pe.wait_ge(pick_ready, s + 1)
                for tt in range(2):
                    ins = pe.transpose(OB[:, P * tt:P * tt + P], pickw[:, tt, :], ident)
                ins.then_inc(put_psum, 1)

            def scatter(s):
                pe.wait_ge(y_lo_done, s + 1)
                pe.wait_ge(put_lo_done, s + 1)
                for r in range(4):
                    if r == 3:
                        pe.wait_ge(sc_add, s * 4 + 2)
                    for i in range(2):
                        c = P * (2 * r + i)
                        ins = mm3(SC_BANK(OB, SB, r)[:, 256 * i:256 * i + 256], y_hi[:, c:c + P], y_lo[:, c:c + P],
                                  put_hi[:, :], put_lo[:, :], True, True)
                    ins.then_inc(sc_psum, 1)

            def job(J, j0, turn, main):
                q = 0

                def piece():
                    nonlocal q
                    q += 1
                    return take(j0 + q - 1, turn)

                def up_half(out, half):
                    hi, lo = piece()
                    for k in range(4):
                        c = P * (4 * half + k)
                        ins = mm3(out, xg_hi[:, c:c + P], xg_lo[:, c:c + P], hi[:, 512 * k:512 * k + 512],
                                  lo[:, 512 * k:512 * k + 512], half == 0 and k == 0, half == 1 and k == 3)
                    ins.then_inc(piece_used, 1)

                def turn_hidden(n):
                    pe.wait_ge(hm_done, J * UNITS + (n + 2))
                    pe.wait_ge(hT_lo_done, J * UNITS + (n + 1))
                    for i in range(4):
                        ins = pe.transpose(TP[0][:, P * i:P * i + P], hb[:, P * i:P * i + P], ident)
                    ins.then_inc(hT_psum, 1)

                def down(n):
                    pe.wait_ge(hT_lo_done, J * UNITS + (n + 2))
                    if n == 0:
                        pe.wait_ge(y_lo_done, J + 1)
                    for half in range(2):
                        hi, lo = piece()
                        for i in range(2):
                            c = P * (2 * half + i)
                            for s in range(2):
                                d = D * i + 512 * s
                                ins = mm3(TP[1 + s][:, :], hT_hi[:, c:c + P], hT_lo[:, c:c + P], hi[:, d:d + 512],
                                          lo[:, d:d + 512], n == 0 and c == 0, n == UNITS - 1 and c == 3 * P)
                        ins.then_inc(piece_used, 1)

                if not main:
                    gather(J + 1)
                    put_transpose_over(J)
                pe.wait_ge(xg_lo_done, J + (1 if main else 2))
                for n in range(UNITS):
                    G, U = PJ if n % 2 == 0 else SB
                    if n == 1 and main:
                        pe.wait_ge(sc_add, J * 4 + 3)
                    elif n == 1:
                        pe.wait_ge(xg_lo_done, J + 2)
                    else:
                        pe.wait_ge(silu_done, J * UNITS + (n if n else 1))
                    up_half(G[:, :], 0)
                    if n == 2 and main:
                        pe.wait_ge(sc_add, J * 4 + 5)
                        put_transpose(J)
                    up_half(G[:, :], 1)
                    if n == 1 and main:
                        pe.wait_ge(sc_add, J * 4 + 4)
                    elif n != 1:
                        pe.wait_ge(hm_done, J * UNITS + (n if n else 1))
                    up_half(U[:, :], 0)
                    if n:
                        turn_hidden(n - 1)
                    up_half(U[:, :], 1)
                    if n == 0 and main:
                        scatter(J)
                    if n:
                        down(n - 1)
                    if n == UNITS - 1:
                        if main:
                            gather(J + 1)
                        turn_hidden(n)
                        down(n)
                if not main:
                    scatter(J + 1)

            def put_transpose_over(s):
                for tt in range(2):
                    ins = pe.transpose(OB[:, P * tt:P * tt + P], pickw[:, tt, :], ident)
                ins.then_inc(put_psum, 1)

            pe.wait_ge(xt_lo_done, 4)
            pe.wait_ge(proj_free, LAYERS * MIX_TILES + FFN_TILES)
            gather(0)
            with pe.Fori(0, NE) as e:
                job(e, MOE0, e, True)
            pe.wait_ge(xg_lo_done, NE + 1)
            scatter(NE)
            pe.wait_ge(table_ready, 1)
            over = pe.value_load(tab[0:1, 3:4], min_val=0, max_val=MAX_OVER)
            with pe.Fori(0, MAX_OVER) as o:
                with pe.If(o < over):
                    pe.wait_ge(sc_add, o * 4 + (4 * NE + 5))
                    job(o + NE, OVER0, o, False)
            pe.wait_ge(h_final, 1)
            for c in range(KD):
                stat(4, c)


def X_HI_COUNT(n):
    return 8 * n + 8 * ((n + 1) // 2)


def XT_BANK(SB, TP, i):
    return (SB[0], SB[1], TP[1], TP[2])[i]


def SC_BANK(OB, SB, r):
    return (OB, SB[0], SB[1], OB)[r]


def kernel(**inputs):
    import numpy as np
    import concourse.bacc as bacc
    from concourse import mybir as mb
    from concourse.bass_utils import run_bass_kernel_spmd as run

    a = {k: np.asarray(x) for k, x in inputs.items()}
    f32 = np.float32

    def on_partitions(x):
        return np.ascontiguousarray(np.moveaxis(x.reshape(*x.shape[:-1], -1, P), -1, 0).reshape(P, -1))

    tokens = np.concatenate([a["meta_tokens"], a["x"][0]], axis=0)
    xT = np.ascontiguousarray(tokens.T.reshape(KD, P, T).transpose(1, 0, 2))

    vecs = np.zeros((P, V_W), f32)
    vecs[:, V_GMIX:V_GMIX + 16] = on_partitions(a["norm_mix_g"])
    vecs[:, V_GFFN:V_GFFN + 16] = on_partitions(a["norm_ffn_g"])
    vecs[:, V_GFIN:V_GFIN + 8] = on_partitions(a["final_norm_g"])
    vecs[:, V_SUB:V_SUB + 2] = a["diff_subln_g"].T
    vecs[0:8, V_BF:V_BF + 2] = a["b_forget"].T
    ff = a["w_in"][:, :, FF_COL:FF_COL + 8].reshape(LAYERS, KD, P, 8)
    vecs[:, V_FF:V_FF + 128] = ff.transpose(2, 0, 1, 3).reshape(P, -1)
    vecs[:, V_RT:V_RT + 64] = a["moe_router"][0].reshape(KD, P, NE).transpose(1, 0, 2).reshape(P, -1)
    lam = np.ascontiguousarray(np.broadcast_to(a["diff_lambda"].reshape(1, -1), (P, 512)))

    c = np.zeros((P, C_W), f32)
    rows = np.arange(P)
    for (c0, w), start in zip(SEG, WIN):
        seen = np.arange(w)[None, :] <= (start + rows)[:, None]
        c[:, C_MASK + c0:C_MASK + c0 + w] = np.where(seen, 0.0, -BIG / SCALE)
    c[:, C_ID:C_ID + P] = np.eye(P)
    c[:, C_TRI:C_TRI + P] = rows[:, None] < rows[None, :]
    c[:, C_IOTA:C_IOTA + 2 * P] = np.arange(2 * P)
    inv = f32(500000.0) ** (-np.arange(0, 16, 2, dtype=f32) / f32(16))
    ang = np.arange(T, dtype=f32)[None, :] * inv[:, None].astype(f32)
    d = rows % 64
    c[:, C_COS:C_COS + T] = np.where(d[:, None] < 16, np.cos(ang)[d % 8], 1.0)
    c[:, C_SIN:C_SIN + T] = np.where(d[:, None] < 16, np.sin(ang)[d % 8], 0.0) * np.where(d < 8, -1, 1)[:, None]
    for p in rows[d < 16]:
        c[p ^ 8, C_ROT + p] = 1.0
    c[:, C_REV:C_REV + 16] = NE - np.arange(16) % NE

    arrays = {"xT": xT, "w_in": a["w_in"], "lam": lam, "w_bd": a["w_branch_diff"], "w_bf": a["w_branch_fox"],
              "w_out": a["w_out"], "f_g": a["ffn_w_gate"], "f_u": a["ffn_w_up"], "f_d": a["ffn_w_down"],
              "m_g": a["moe_w_gate"], "m_u": a["moe_w_up"], "m_d": a["moe_w_down"], "consts": c, "vecs": vecs}
    nc = bacc.Bacc("TRN2", target_bir_lowering=False, num_devices=1)
    args = [nc.dram_tensor(name, x.shape, mb.dt.from_np(x.dtype), kind="ExternalInput").ap()
            for name, x in arrays.items()]
    out = nc.dram_tensor("outT", (P, KD, SEQ), mb.dt.float32, kind="ExternalOutput").ap()
    trunk(nc, *args, out)
    r = run(nc, [arrays], core_ids=[0])
    got = r.results[0]["outT"]
    return np.ascontiguousarray(got.transpose(1, 0, 2).reshape(D, SEQ).T).reshape(1, SEQ, D)
```

```python
import math
from contextlib import ExitStack

import concourse.bass as bass
from concourse import mybir

F32 = mybir.dt.float32
F32R = mybir.dt.float32r
I32 = mybir.dt.int32
ACT = mybir.ActivationFunctionType
ALU = mybir.AluOpType
AX = mybir.AxisListType.X

P = 128
D = 1024
KD = D // P
NMETA = 16
SEQ = 256
T = NMETA + SEQ
LAYERS = 2
DFF = 2816
FT = DFF // P
NE = 8
DFE = 3584
EPS = 1e-6
SCALE = 64 ** -0.5
BIG = 1e30
WIN = [0, NMETA, NMETA + P]
IN_COLS = 5128
FF_COL = 3072
GATE_COL = FF_COL + 8
SEG = [(0, 16), (16, 144), (160, 272)]

NRAW = 6
COLS = 2048
NHALF = 6
HCOLS = COLS // 2
HI_AHEAD = NHALF
LO_AHEAD = NHALF - 1
MIX_PIECES = 28
FFN_BLOCKS = DFF // 256
FFN_PIECES = 2 * FFN_BLOCKS + 12
LAYER1 = MIX_PIECES + FFN_PIECES
MOE0 = LAYER1 + MIX_PIECES
UNITS = DFE // 512
JOB = 6 * UNITS
HJOB = 2 * JOB
EMPTY = NHALF // 2
OVER0 = MOE0 + NE * JOB + EMPTY
MAX_OVER = 3
assert MOE0 % NRAW == 0 and JOB % NRAW == 0 and HJOB % NHALF == 0 and 2 * MOE0 % NHALF == 0
DOWN_K = [(0, 8), (8, 8), (16, 6)]

MIX_TILES = 69
FFN_TILES = 4 * FFN_BLOCKS + 8
V_TILE, GATE_TILE, BD_TILE, BF_TILE, OUT_TILE = 17, 29, 45, 53, 61
DOWN_TILE = MIX_TILES + 4 * FFN_BLOCKS
FFN_STRIPS = 4 * FFN_BLOCKS + 24


def strips_to_tile(t):
    if t < DOWN_TILE:
        return t + 1
    if t < MIX_TILES + FFN_TILES:
        dp, i = divmod(t - DOWN_TILE, 2)
        return DOWN_TILE + 6 * dp + 4 + i + 1
    return t + 1 + FFN_STRIPS - FFN_TILES


def strips_to_half(i):
    j, half = divmod(i, 2)
    l, j = divmod(j, LAYER1)
    base = l * (MIX_TILES + FFN_STRIPS)
    if 8 <= j < 12:
        return base + V_TILE + 3 * (j - 7)
    for first, last, start, each in ((0, 8, 1, 1), (12, 20, GATE_TILE, 1), (20, 24, BD_TILE, 2),
                                     (24, LAYER1, OUT_TILE, 1)):
        if first <= j < last:
            return base + start + each * (2 * (j - first) + half + 1)


C_MASK, C_ID, C_TRI, C_IOTA, C_ROT, C_COS, C_SIN, C_REV = 0, 432, 560, 688, 944, 1072, 1344, 1616
C_W = 1632
V_GMIX, V_GFFN, V_GFIN, V_SUB, V_BF, V_FF, V_RT = 0, 16, 32, 40, 42, 44, 172
V_W = 236


class Chain:

    def __init__(self, eng, sem):
        self.eng, self.sem, self.base, self.k = eng, sem, 0, 0

    def __call__(self, ins):
        self.k += 1
        ins.then_inc(self.sem, 1)
        self.eng.wait_ge(self.sem, self.base + self.k)

    def enter(self, turn, per):
        self.start, self.per = self.k, per
        self.base, self.k = turn * per + self.start, 0

    def leave(self, turns):
        assert self.k == self.per, (self.k, self.per)
        self.base, self.k = 0, self.start + turns * self.per


def trunk(nc, xT, w_in, lam, w_bd, w_bf, w_out, f_g, f_u, f_d, m_g, m_u, m_d, consts, vecs, outT):
    lam_init = [0.8 - 0.6 * math.exp(-0.3 * l) for l in range(LAYERS)]
    ctx = ExitStack()
    with ctx:
        def sb(name, shape, dt=F32, scope=ctx):
            return scope.enter_context(nc.sbuf_tensor(name, shape, dt))

        def bank(name):
            return ctx.enter_context(nc.psum_tensor(name, [P, 512], F32))

        def sem(name):
            return ctx.enter_context(nc.semaphore(name))

        raw = sb("raw", [P, NRAW, COLS])
        w_hi = sb("w_hi", [P, NHALF, HCOLS], F32R)
        w_lo = sb("w_lo", [P, NHALF, HCOLS], F32R)
        h = sb("h", [P, KD, T])
        x_hi = [sb(f"x_hi{i}", [P, KD, T], F32R) for i in range(2)]
        x_lo = [sb(f"x_lo{i}", [P, KD, T], F32R) for i in range(2)]
        sq = sb("sq", [P, 2, T])
        rb = sb("rb", [P, T])
        rt = sb("rt", [P, 3])
        cst = sb("cst", [P, C_W])
        vec = sb("vec", [P, V_W])
        ones = sb("ones", [P, P])
        eps = sb("eps", [P, 1])
        ff_hi = sb("ff_hi", [P, 248], F32R)
        ff_lo = sb("ff_lo", [P, 248], F32R)
        rw_hi = sb("rw_hi", [P, KD, NE], F32R)
        rw_lo = sb("rw_lo", [P, KD, NE], F32R)
        lam4 = sb("lam4", [P, 4])
        nlam = sb("nlam", [P, LAYERS])
        subg = sb("subg", [P, LAYERS])
        with ExitStack() as att:
            qk = [sb(f"qk{i}", [P, 8, T], scope=att) for i in range(2)]
            v = sb("v", [P, 3, D], scope=att)
            gate = sb("gate", [P, 16, T], scope=att)
            score = sb("score", [P, 2, 432], scope=att)
            aT = sb("aT", [P, 2, 656], scope=att)
            o_raw = sb("o_raw", [P, T], scope=att)
            mx = sb("mx", [P, 6], scope=att)
            nmx = sb("nmx", [P, 2, 6], scope=att)
            sm = sb("sm", [P, 2, 6], scope=att)
            rs = sb("rs", [P, 6], scope=att)
            aT_row = aT[:, :, :].rearrange("p a b -> p (a b)")
            fz = aT_row[0:8, 0:3 * T].rearrange("p (a b) -> p a b", a=3)
            rope_t = aT_row[:, 3 * T:4 * T]
            cneg = gate[0:8, 15, :]
            lam_raw = score[:, :, :].rearrange("p a b -> p (a b)")[:, 0:512]
            o_sq = sq[:, 0, :]
            o_rs = sq[:, 1, :]
        with ExitStack() as ffn:
            ffh_hi = sb("ffh_hi", [P, FT, T], F32R, scope=ffn)
            ffh_lo = sb("ffh_lo", [P, FT, T], F32R, scope=ffn)
            gbuf = sb("gbuf", [P, 2, T], scope=ffn)
            ubuf = sb("ubuf", [P, 2, T], scope=ffn)
        with ExitStack() as moe:
            xt_hi = sb("xt_hi", [P, 2, D], F32R, scope=moe)
            xt_lo = sb("xt_lo", [P, 2, D], F32R, scope=moe)
            xg_hi = sb("xg_hi", [P, D], F32R, scope=moe)
            xg_lo = sb("xg_lo", [P, D], F32R, scope=moe)
            sg = sb("sg", [P, 512], scope=moe)
            hb = sb("hb", [P, 512], scope=moe)
            hT_hi = sb("hT_hi", [P, 512], F32R, scope=moe)
            hT_lo = sb("hT_lo", [P, 512], F32R, scope=moe)
            y_hi = sb("y_hi", [P, D], F32R, scope=moe)
            y_lo = sb("y_lo", [P, D], F32R, scope=moe)
            pick = sb("pick", [P, 2, P], F32R, scope=moe)
            pickw = sb("pickw", [P, 2, P], scope=moe)
            put_hi = sb("put_hi", [P, 2 * P], F32R, scope=moe)
            put_lo = sb("put_lo", [P, 2 * P], F32R, scope=moe)
            ident_r = sb("ident_r", [P, P], F32R, scope=moe)
            lg = sb("lg", [P, 2, NE], scope=moe)
            eq = sb("eq", [P, 2, NE], scope=moe)
            sel1 = sb("sel1", [P, 2, NE], scope=moe)
            sel2 = sb("sel2", [P, 2, NE], scope=moe)
            mask = sb("mask", [P, 2, NE], scope=moe)
            comb = sb("comb", [P, 2, NE + 1], scope=moe)
            pos = sb("pos", [P, 2, NE + 1], scope=moe)
            top = sb("top", [P, 8, 2], scope=moe)
            cnt = sb("cnt", [P, 3, NE], scope=moe)
            tab_f = sb("tab_f", [P, 4], scope=moe)
            tab = sb("tab", [P, 4], I32, scope=moe)
            outb = sb("outb", [P, KD, SEQ], scope=moe)

        PJ = [bank("pj0"), bank("pj1")]
        SB = [bank("s0"), bank("s1")]
        TP = [bank("tp0"), bank("tp1"), bank("tp2")]
        OB = bank("ob")

        vec_in = sem("vec_in")
        tables_in = sem("tables_in")
        x_in = sem("x_in")
        pool_set = sem("pool_set")
        small_hi = sem("small_hi")
        small_lo = sem("small_lo")
        lam_sum = sem("lam_sum")
        lam_exp = sem("lam_exp")
        lam_ready = sem("lam_ready")
        landed = [sem(f"landed{i}") for i in range(NRAW)]
        hi_done = sem("hi_done")
        lo_done = sem("lo_done")
        half_used = sem("half_used")
        x_hi_done = sem("x_hi_done")
        x_lo_done = sem("x_lo_done")
        sq_ready = sem("sq_ready")
        stat_done = sem("stat_done")
        rstd_ready = sem("rstd_ready")
        rt_psum = sem("rt_psum")
        rt_ready = sem("rt_ready")
        strip_done = sem("strip_done")
        proj_free = sem("proj_free")
        rot_done = sem("rot_done")
        rope_done = sem("rope_done")
        fz_ready = sem("fz_ready")
        fz_act = sem("fz_act")
        cneg_ready = sem("cneg_ready")
        gate_e = sem("gate_e")
        merged = sem("merged")
        s_done = sem("s_done")
        s_free = sem("s_free")
        nmx_ready = sem("nmx_ready")
        exp_done = sem("exp_done")
        a_ready = sem("a_ready")
        tr_done = sem("tr_done")
        aT_ready = sem("aT_ready")
        pv_done = sem("pv_done")
        o_free = sem("o_free")
        o_sq_ready = sem("o_sq_ready")
        o_stat = sem("o_stat")
        o_rs_ready = sem("o_rs_ready")
        o_norm = sem("o_norm")
        o_hi = sem("o_hi")
        o_lo = sem("o_lo")
        silu_f = sem("silu_f")
        ffh = sem("ffh")
        ffh_hi_done = sem("ffh_hi_done")
        ffh_lo_done = sem("ffh_lo_done")
        logit_done = sem("logit_done")
        xt_psum = sem("xt_psum")
        xt_hi_done = sem("xt_hi_done")
        xt_lo_done = sem("xt_lo_done")
        ident_done = sem("ident_done")
        top_diff = sem("top_diff")
        top_exp = sem("top_exp")
        mask_ready = sem("mask_ready")
        rank_done = sem("rank_done")
        table_ready = sem("table_ready")
        silu_done = sem("silu_done")
        hm_done = sem("hm_done")
        hT_psum = sem("hT_psum")
        hT_hi_done = sem("hT_hi_done")
        hT_lo_done = sem("hT_lo_done")
        y_hi_done = sem("y_hi_done")
        y_lo_done = sem("y_lo_done")
        pick_ready = sem("pick_ready")
        xg_psum = sem("xg_psum")
        xg_hi_done = sem("xg_hi_done")
        xg_lo_done = sem("xg_lo_done")
        put_psum = sem("put_psum")
        put_hi_done = sem("put_hi_done")
        put_lo_done = sem("put_lo_done")
        sc_psum = sem("sc_psum")
        sc_add = sem("sc_add")
        h_final = sem("h_final")
        out_ready = sem("out_ready")
        out_done = sem("out_done")
        dve_chain = sem("dve_chain")
        act_chain = sem("act_chain")

        def k_major(ap):
            return ap.rearrange("(k p) n -> p k n", p=P)

        def dense_source(l, j):
            if j < 12:
                c = (0, 512, 1536, 2048, 1024, 2560)[j // 2] + 256 * (j % 2)
                return k_major(w_in[l, :, c:c + 256])
            if j < 20:
                c = GATE_COL + 256 * (j - 12)
                return k_major(w_in[l, :, c:c + 256])
            if j < 24:
                w = w_bd if j < 22 else w_bf
                c = 512 * (j % 2)
                return k_major(w[l, :, c:c + 512])
            if j < MIX_PIECES:
                c = 256 * (j - 24)
                return k_major(w_out[l, :, c:c + 256])
            j -= MIX_PIECES
            if j < 2 * FFN_BLOCKS:
                w = f_u if j % 2 else f_g
                c = 256 * (j // 2)
                return k_major(w[0, :, c:c + 256])
            dp, part = divmod(j - 2 * FFN_BLOCKS, 3)
            k0, nk = DOWN_K[part]
            return k_major(f_d[0, P * k0:P * (k0 + nk), 256 * dp:256 * dp + 256])

        def half_views(j, half):
            slot = raw[:, j % NRAW, :]
            l, i = divmod(j, LAYER1)
            if j >= MOE0 or 8 <= i < 12:
                k, c = 4, 256
                return slot[:, HCOLS * half:HCOLS * half + HCOLS].rearrange("p (k c) -> p k c", k=k), k, c
            k, width = (4, 512) if 20 <= i < 24 else (KD, 256)
            if i >= MIX_PIECES + 2 * FFN_BLOCKS:
                k = DOWN_K[(i - MIX_PIECES - 2 * FFN_BLOCKS) % 3][1]
            c = width // 2
            whole = slot[:, 0:k * width].rearrange("p (k c) -> p k c", k=k)
            return whole[:, :, c * half:c * half + c], k, c

        def ring(parts, i, k, c):
            return parts[:, i % NHALF, 0:k * c].rearrange("p (k c) -> p k c", k=k)

        def job_order():
            order = [("g", 0, 0), ("g", 0, 1), ("u", 0, 0), ("u", 0, 1)]
            for n in range(1, UNITS):
                order += [("g", n, 0), ("g", n, 1), ("u", n, 0), ("u", n, 1), ("d", n - 1, 0), ("d", n - 1, 1)]
            return order + [("d", UNITS - 1, 0), ("d", UNITS - 1, 1)]

        def expert_source(e, kind, n, half):
            if kind == "d":
                r = 512 * n + 256 * half
                return k_major(m_d[0, e, r:r + 256, :])
            w = m_g if kind == "g" else m_u
            return k_major(w[0, e, 512 * half:512 * half + 512, 512 * n:512 * n + 512])

        def uses(j, turn):
            return j // NRAW + 1 + turn * (JOB // NRAW)

        block = ctx.enter_context(nc.Block())

        @block.sync
        def _(sp):
            sp.dma_start(h[:, :, :], xT).then_inc(x_in, 16)

            def load(j, source, turn=0):
                s = j % NRAW
                if j >= NRAW:
                    sp.wait_ge(lo_done, turn * HJOB + 2 * (j - NRAW + 1))
                n = source.shape[1] * source.shape[2]
                sp.dma_start(raw[:, s, 0:n].rearrange("p (k c) -> p k c", k=source.shape[1]),
                             source).then_inc(landed[s], 16)

            for l in range(LAYERS):
                for j in range(MIX_PIECES + (FFN_PIECES if l == 0 else 0)):
                    load(l * LAYER1 + j, dense_source(l, j))
            with sp.Fori(0, NE) as e:
                for q, (kind, n, half) in enumerate(job_order()):
                    load(MOE0 + q, expert_source(e, kind, n, half), e)
            for q in range(EMPTY):
                load(MOE0 + NE * JOB + q, consts[:, 0:16].rearrange("p (a b) -> p a b", a=1))
            sp.wait_ge(table_ready, 1)
            over = sp.value_load(tab[0:1, 3:4], min_val=0, max_val=MAX_OVER)
            with sp.Fori(0, MAX_OVER) as o:
                with sp.If(o < over):
                    e = sp.value_load(tab[0:1, bass.ds(o, 1)], min_val=0, max_val=NE - 1)
                    for q, (kind, n, half) in enumerate(job_order()):
                        load(OVER0 + q, expert_source(e, kind, n, half), o)
            for c in range(KD):
                sp.wait_ge(out_ready, c + 1)
                sp.dma_start(outT[:, c, :], outb[:, c, :]).then_inc(out_done, 16)
            sp.wait_ge(out_done, 16 * KD)

        @block.gpsimd
        def _(pool):
            pool.memset(ones[:, :], 1.0).then_inc(pool_set, 1)
            pool.memset(eps[:, :], EPS).then_inc(pool_set, 1)
            pool.memset(ff_hi[:, :].bitcast(F32), 0.0).then_inc(pool_set, 1)
            pool.memset(ff_lo[:, :].bitcast(F32), 0.0).then_inc(pool_set, 1)

        @block.scalar
        def _(act):
            link = Chain(act, act_chain)

            def split(i, turn=0, skipped=0):
                j, half = divmod(i, 2)
                act.wait_ge(landed[j % NRAW], uses(j, turn) * 16)
                if NHALF <= i < 2 * MOE0 + NHALF:
                    act.wait_ge(strip_done, strips_to_half(i - NHALF))
                elif i >= NHALF:
                    act.wait_ge(half_used, turn * HJOB + (i - NHALF + 1 - skipped - 2 * MOE0))
                src, k, c = half_views(j, half)
                act.activation(ring(w_hi, i, k, c), src, ACT.Copy).then_inc(hi_done, 1)

            def after(l, j, half):
                split(2 * (l * LAYER1 + j) + half + HI_AHEAD)

            def x_part(n, c, gain):
                act.activation(x_hi[n % 2][:, c, :], h[:, c, :], ACT.Copy, scale=gain).then_inc(x_hi_done, 1)
                square(n, c)

            def square(n, c):
                i = 8 * n + c
                if i >= 2:
                    act.wait_ge(stat_done, i - 1)
                act.activation(sq[:, c % 2, :], h[:, c, :], ACT.Square).then_inc(sq_ready, 1)

            def rstd(n):
                act.wait_ge(stat_done, 8 * n + 8)
                link(act.activation(rb[:, :], OB[:, 0:T], ACT.Ln, bias=eps[:, 0:1], scale=1.0 / D))
                act.activation(rb[:, :], rb[:, :], ACT.Exp, scale=-0.5).then_inc(rstd_ready, 1)

            act.dma_start(vec[:, :], vecs).then_inc(vec_in, 16)
            act.dma_start(cst[:, :], consts).then_inc(tables_in, 16)
            act.dma_start(lam_raw, lam).then_inc(tables_in, 16)
            act.wait_ge(vec_in, 16)
            act.wait_ge(pool_set, 4)
            act.activation(ff_hi[:, 0:128], vec[:, V_FF:V_FF + 128], ACT.Copy).then_inc(small_hi, 1)
            act.activation(rw_hi[:, :, :].rearrange("p a b -> p (a b)"), vec[:, V_RT:V_RT + 64], ACT.Copy)\
                .then_inc(small_hi, 1)
            act.wait_ge(x_in, 16)
            for c in range(KD):
                x_part(0, c, vec[:, V_GMIX + c:V_GMIX + c + 1])
            for i in range(HI_AHEAD):
                split(i)
            rstd(0)
            act.wait_ge(lam_sum, 4)
            act.activation(lam4[:, :], lam4[:, :], ACT.Exp).then_inc(lam_exp, 1)

            def attention_exp(l, u):
                un = 8 * l + u
                act.wait_ge(nmx_ready, un + 1)
                for m in range(2):
                    for i, (c0, w) in enumerate(SEG):
                        k = 3 * m + i
                        ins = act.activation(score[:, m, c0:c0 + w], score[:, m, c0:c0 + w], ACT.Exp,
                                             bias=nmx[:, u % 2, k:k + 1], accum_out=sm[:, u % 2, k:k + 1])
                ins.then_inc(exp_done, 1)

            def evacuate_aT(l, u):
                un = 8 * l + u
                act.wait_ge(tr_done, un + 1)
                if un:
                    act.wait_ge(pv_done, un)
                heads = 1 if u < 4 else 2
                for m in range(heads):
                    act.activation(aT[:, m, 0:384], TP[m][:, 0:384], ACT.Copy)
                    act.activation(aT[0:16, m, 384:400], TP[m][0:16, 384:400], ACT.Copy)
                act.activation(aT[0:16, 0:heads, 400:656],
                               TP[2][0:16, 0:256 * heads].rearrange("p (m c) -> p m c", m=heads),
                               ACT.Copy).then_inc(aT_ready, 1)

            def o_square(l, u):
                act.wait_ge(o_free, 4 * l + u + 1)
                act.activation(o_sq, o_raw[:, :], ACT.Square).then_inc(o_sq_ready, 1)

            def o_rstd(l, u):
                act.wait_ge(o_stat, 4 * l + u + 1)
                link(act.activation(o_rs, TP[1][:, 0:T], ACT.Ln, bias=eps[:, 0:1], scale=1.0 / P))
                act.activation(o_rs, o_rs, ACT.Exp, scale=-0.5).then_inc(o_rs_ready, 1)

            def o_part(l, u):
                if u < 4:
                    act.wait_ge(o_norm, 4 * l + u + 1)
                    source = o_raw[:, :]
                else:
                    act.wait_ge(pv_done, 8 * l + u + 1)
                    source = OB[:, 0:T]
                act.activation(x_hi[1][:, u, :], source, ACT.Copy).then_inc(o_hi, 1)

            for l in range(LAYERS):
                proj0 = l * (MIX_TILES + FFN_TILES)
                for j in range(12):
                    for half in range(2):
                        after(l, j, half)
                    if j == 1:
                        act.wait_ge(fz_ready, l + 1)
                        link(act.activation(fz[:, 1, :], fz[:, 0, :], ACT.Abs))
                        link(act.activation(fz[:, 1, :], fz[:, 1, :], ACT.Exp, scale=-1.0))
                        act.activation(fz[:, 1, :], fz[:, 1, :], ACT.Ln, bias=1.0).then_inc(fz_act, 1)
                for u in range(8):
                    attention_exp(l, u)
                    if 1 <= u <= 4:
                        o_square(l, u - 1)
                    after(l, 12 + u, 0)
                    if 1 <= u <= 4:
                        o_rstd(l, u - 1)
                    after(l, 12 + u, 1)
                    if 1 <= u <= 4:
                        o_part(l, u - 1)
                    evacuate_aT(l, u)
                    if u >= 4:
                        o_part(l, u)
                for q in range(4):
                    act.wait_ge(proj_free, proj0 + GATE_TILE + 4 * q + 4)
                    act.activation(gate[:, 4 * q:4 * q + 4, :], gate[:, 4 * q:4 * q + 4, :], ACT.Sigmoid)\
                        .then_inc(gate_e, 1)
                    after(l, 20 + q // 2, q % 2)
                for j in range(22, 24):
                    for half in range(2):
                        for c in range(4 * (j - 22) + 2 * half, 4 * (j - 22) + 2 * half + 2):
                            act.wait_ge(merged, 8 * l + c + 1)
                            act.activation(x_hi[0][:, c, :], gate[:, 8 + c, :], ACT.Copy).then_inc(x_hi_done, 1)
                        after(l, j, half)
                n = 2 * l + 1
                for c in range(KD):
                    act.wait_ge(proj_free, proj0 + OUT_TILE + c + 1)
                    x_part(n, c, vec[:, V_GFFN + 8 * l + c:V_GFFN + 8 * l + c + 1])
                    if c < KD - 1:
                        after(l, 24 + c // 2, c % 2)
                rstd(n)
                after(l, 27, 1)
                if l == 0:
                    for b in range(FFN_BLOCKS):
                        for i in range(2):
                            act.wait_ge(proj_free, MIX_TILES + 4 * b + i + 1)
                            act.activation(gbuf[:, i, :], gbuf[:, i, :], ACT.Silu).then_inc(silu_f, 1)
                            after(0, MIX_PIECES + 2 * b, i)
                        for i in range(2):
                            act.wait_ge(ffh, 2 * b + i + 1)
                            act.activation(ffh_hi[:, 2 * b + i, :], ubuf[:, i, :], ACT.Copy).then_inc(ffh_hi_done, 1)
                            after(0, MIX_PIECES + 2 * b + 1, i)
                    for dp in range(4):
                        for part in range(3):
                            for i in range(2):
                                c = 2 * dp + i
                                if part == 2:
                                    act.wait_ge(proj_free, DOWN_TILE + c + 1)
                                    x_part(2, c, vec[:, V_GMIX + 8 + c:V_GMIX + 8 + c + 1])
                                if c < KD - 1 or part < 2:
                                    after(0, MIX_PIECES + 2 * FFN_BLOCKS + 3 * dp + part, i)
                    rstd(2)
                    after(0, MIX_PIECES + FFN_PIECES - 1, 1)

            link(act.activation(ident_r[:, :], cst[:, C_ID:C_ID + P], ACT.Copy))
            act.nop().then_inc(ident_done, 1)
            act.wait_ge(rt_ready, 3)
            for i in range(4):
                tt, half = divmod(i, 2)
                act.wait_ge(xt_psum, i + 1)
                act.activation(xt_hi[:, tt, 512 * half:512 * half + 512], XT_BANK(SB, TP, i)[:, :], ACT.Copy,
                               scale=rt[:, tt + 1:tt + 2]).then_inc(xt_hi_done, 1)
            act.wait_ge(top_diff, 1)
            act.activation(top[:, 4, :], top[:, 3, :], ACT.Exp).then_inc(top_exp, 1)

            def xg_part(g):
                act.wait_ge(xg_psum, g + 1)
                act.activation(xg_hi[:, 0:512], SB[0][:, :], ACT.Copy)
                act.activation(xg_hi[:, 512:1024], SB[1][:, :], ACT.Copy).then_inc(xg_hi_done, 1)

            def put_part(s):
                act.wait_ge(put_psum, s + 1)
                act.activation(put_hi[:, :], OB[:, 0:2 * P], ACT.Copy).then_inc(put_hi_done, 1)

            def job(J, j0, turn, skipped, main):
                q = 0

                def used(count=1):
                    nonlocal q
                    for _ in range(count):
                        if main or q + HI_AHEAD < HJOB:
                            split(2 * j0 + q + HI_AHEAD, turn, skipped)
                        q += 1

                def hT_part(n):
                    act.wait_ge(hT_psum, J * UNITS + (n + 1))
                    act.activation(hT_hi[:, :], TP[0][:, :], ACT.Copy).then_inc(hT_hi_done, 1)

                if not main:
                    act.wait_ge(lo_done, turn * HJOB + 2 * j0)
                    for i in range(HI_AHEAD):
                        split(2 * j0 + i, turn, skipped)
                    xg_part(J + 1)
                    put_part(J)
                for n in range(UNITS):
                    used(2)
                    if n:
                        hT_part(n - 1)
                    used()
                    if n == 2 and main:
                        put_part(J)
                    act.wait_ge(half_used, J * HJOB + 2 * (6 * n if n else 2))
                    act.wait_ge(hm_done, J * UNITS + (n + 1))
                    act.activation(sg[:, :], (PJ if n % 2 == 0 else SB)[0][:, :], ACT.Silu).then_inc(silu_done, 1)
                    used()
                    used(4)
                    if 0 < n < UNITS - 1:
                        used(4)
                used(3)
                act.wait_ge(half_used, J * HJOB + (HJOB - 4))
                hT_part(UNITS - 1)
                used()
                if main:
                    xg_part(J + 1)
                used(3)
                act.wait_ge(half_used, J * HJOB + HJOB)
                act.activation(y_hi[:, 0:512], TP[1][:, :], ACT.Copy)
                act.activation(y_hi[:, 512:1024], TP[2][:, :], ACT.Copy).then_inc(y_hi_done, 1)
                used()

            act.nop().then_inc(silu_done, 1)
            xg_part(0)
            with act.Fori(0, NE) as e:
                job(e, MOE0, e, 0, True)
            act.wait_ge(table_ready, 1)
            over = act.value_load(tab[0:1, 3:4], min_val=0, max_val=MAX_OVER)
            with act.Fori(0, MAX_OVER) as o:
                with act.If(o < over):
                    job(o + NE, OVER0, o, 2 * EMPTY, False)
            act.wait_ge(h_final, 1)
            for c in range(KD):
                square(4, c)
            act.wait_ge(stat_done, 40)
            link(act.activation(rb[:, :], OB[:, 0:T], ACT.Ln, bias=eps[:, 0:1], scale=1.0 / D))
            act.activation(rb[:, :], rb[:, :], ACT.Exp, scale=-0.5).then_inc(rstd_ready, 1)

        @block.vector
        def _(dve):
            link = Chain(dve, dve_chain)

            def split(i, turn=0):
                dve.wait_ge(hi_done, turn * HJOB + (i + 1))
                src, k, c = half_views(i // 2, i % 2)
                dve.tensor_tensor(ring(w_lo, i, k, c), src, ring(w_hi, i, k, c).bitcast(F32),
                                  ALU.subtract).then_inc(lo_done, 1)

            def after(l, j, half):
                split(2 * (l * LAYER1 + j) + half + LO_AHEAD)

            def x_part(n, c, gain):
                dve.wait_ge(x_hi_done, X_HI_COUNT(n) + c + 1)
                dve.scalar_tensor_tensor(x_lo[n % 2][:, c, :], h[:, c, :], gain, x_hi[n % 2][:, c, :].bitcast(F32),
                                         ALU.mult, ALU.subtract).then_inc(x_lo_done, 1)

            dve.wait_ge(small_hi, 2)
            dve.tensor_tensor(ff_lo[:, 0:128], vec[:, V_FF:V_FF + 128], ff_hi[:, 0:128].bitcast(F32),
                              ALU.subtract).then_inc(small_lo, 1)
            dve.tensor_tensor(rw_lo[:, :, :].rearrange("p a b -> p (a b)"), vec[:, V_RT:V_RT + 64],
                              rw_hi[:, :, :].rearrange("p a b -> p (a b)").bitcast(F32),
                              ALU.subtract).then_inc(small_lo, 1)
            for c in range(KD):
                x_part(0, c, vec[:, V_GMIX + c:V_GMIX + c + 1])
            dve.wait_ge(tables_in, 32)
            for k in range(4):
                dve.tensor_tensor_reduce(out=o_raw[:, 64 * k:64 * k + 64], in0=lam_raw[:, 128 * k:128 * k + 64],
                                         in1=lam_raw[:, 128 * k + 64:128 * k + 128], scale=1.0, scalar=0.0,
                                         op0=ALU.mult, op1=ALU.add, accum_out=lam4[:, k:k + 1]).then_inc(lam_sum, 1)
            for i in range(LO_AHEAD):
                split(i)
            dve.wait_ge(lam_exp, 1)
            for l in range(LAYERS):
                link(dve.tensor_tensor(nlam[:, l:l + 1], lam4[:, 2 * l + 1:2 * l + 2], lam4[:, 2 * l:2 * l + 1],
                                       ALU.subtract))
                link(dve.tensor_scalar(nlam[:, l:l + 1], nlam[:, l:l + 1], -lam_init[l], None, ALU.add))
                link(dve.tensor_scalar(subg[:, l:l + 1], vec[:, V_SUB + l:V_SUB + l + 1], 1.0 - lam_init[l], None,
                                       ALU.mult))

            def attention_max(l, u):
                un = 8 * l + u
                if un:
                    dve.wait_ge(tr_done, un)
                for m in range(2):
                    dve.wait_ge(s_done, 2 * un + m + 1)
                    for i, (c0, w) in enumerate(SEG):
                        k = 3 * m + i
                        ins = dve.tensor_tensor_reduce(
                            out=score[:, m, c0:c0 + w], in0=SB[m][:, c0:c0 + w],
                            in1=cst[:, C_MASK + c0:C_MASK + c0 + w], scale=SCALE, scalar=-3e38,
                            op0=ALU.add, op1=ALU.max, accum_out=mx[:, k:k + 1])
                    ins.then_inc(s_free, 1)
                dve.wait_ge(s_free, 2 * un + 2)
                dve.tensor_scalar(nmx[:, u % 2, :], mx[:, :], -1.0, None, ALU.mult).then_inc(nmx_ready, 1)
                dve.wait_ge(nmx_ready, un + 1)

            def attention_normalise(l, u):
                un = 8 * l + u
                dve.wait_ge(exp_done, un + 1)
                link(dve.reciprocal(rs[:, :], sm[:, u % 2, :]))
                if u < 4:
                    link(dve.tensor_scalar(rs[:, 3:6], rs[:, 3:6], nlam[:, l:l + 1], None, ALU.mult))
                    for i, (c0, w) in enumerate(SEG):
                        a = score[:, 0, c0:c0 + w]
                        ins = dve.tensor_scalar(a, a, rs[:, i:i + 1], None, ALU.mult)
                    link(ins)
                    for i, (c0, w) in enumerate(SEG):
                        a = score[:, 0, c0:c0 + w]
                        ins = dve.scalar_tensor_tensor(a, score[:, 1, c0:c0 + w], rs[:, 3 + i:4 + i], a,
                                                       ALU.mult, ALU.add)
                else:
                    for m in range(2):
                        for i, (c0, w) in enumerate(SEG):
                            a = score[:, m, c0:c0 + w]
                            ins = dve.tensor_scalar(a, a, rs[:, 3 * m + i:3 * m + i + 1], None, ALU.mult)
                ins.then_inc(a_ready, 1)
                dve.wait_ge(a_ready, un + 1)

            def free(t):
                dve.wait_ge(proj_free, t + 1)

            def rope(l, i):
                dve.wait_ge(rot_done, 8 * l + i + 1)
                link(dve.tensor_tensor(rope_t, TP[1 + i % 2][:, 0:T], cst[:, C_SIN:C_SIN + T], ALU.mult))
                link(dve.tensor_tensor(qk[0][:, i, :], qk[0][:, i, :], cst[:, C_COS:C_COS + T], ALU.mult))
                dve.tensor_tensor(qk[0][:, i, :], qk[0][:, i, :], rope_t, ALU.add).then_inc(rope_done, 1)
                dve.wait_ge(rope_done, 8 * l + i + 1)

            def o_evacuate(l, u):
                un = 8 * l + u
                if u < 4:
                    dve.wait_ge(pv_done, un + 1)
                    dve.tensor_copy(o_raw[:, :], OB[:, 0:T]).then_inc(o_free, 1)
                    dve.wait_ge(o_free, 4 * l + u + 1)
                else:
                    dve.wait_ge(o_hi, un + 1)
                    dve.tensor_tensor(x_lo[1][:, u, :], OB[:, 0:T], x_hi[1][:, u, :].bitcast(F32),
                                      ALU.subtract).then_inc(o_lo, 1)

            def o_normalise(l, u):
                dve.wait_ge(o_rs_ready, 4 * l + u + 1)
                dve.scalar_tensor_tensor(o_raw[:, :], o_raw[:, :], subg[:, l:l + 1], o_rs, ALU.mult,
                                         ALU.mult).then_inc(o_norm, 1)
                dve.wait_ge(o_norm, 4 * l + u + 1)

            def o_part(l, u):
                dve.wait_ge(o_hi, 8 * l + u + 1)
                dve.tensor_tensor(x_lo[1][:, u, :], o_raw[:, :], x_hi[1][:, u, :].bitcast(F32),
                                  ALU.subtract).then_inc(o_lo, 1)
                dve.wait_ge(o_lo, 8 * l + u + 1)

            def merged_part(l, c):
                dve.wait_ge(x_hi_done, X_HI_COUNT(2 * l + 1) - 8 + c + 1)
                dve.tensor_tensor(x_lo[0][:, c, :], gate[:, 8 + c, :], x_hi[0][:, c, :].bitcast(F32),
                                  ALU.subtract).then_inc(x_lo_done, 1)

            for l in range(LAYERS):
                t0 = l * (MIX_TILES + FFN_TILES)
                dve.wait_ge(rstd_ready, 2 * l + 1)
                dve.wait_ge(strip_done, strips_to_tile(t0))
                dve.tensor_tensor(fz[:, 0, :], PJ[t0 % 2][0:8, 0:T], rb[0:8, :], ALU.mult).then_inc(proj_free, 1)
                free(t0)
                dve.tensor_scalar(fz[:, 0, :], fz[:, 0, :], vec[0:8, V_BF + l:V_BF + l + 1], None,
                                  ALU.add).then_inc(fz_ready, 1)
                dve.wait_ge(fz_ready, l + 1)
                for j in range(8):
                    for i in range(2):
                        t = t0 + 1 + 2 * j + i
                        dve.wait_ge(strip_done, strips_to_tile(t))
                        dve.tensor_tensor(qk[j // 4][:, (2 * j + i) % 8, :], PJ[t % 2][:, 0:T], rb[:, :],
                                          ALU.mult).then_inc(proj_free, 1)
                        after(l, j, i)
                    free(t)
                    if 1 <= j <= 4:
                        rope(l, 2 * j - 2)
                        rope(l, 2 * j - 1)
                    if j == 0:
                        dve.wait_ge(rt_psum, l + 1)
                        dve.tensor_copy(rt[:, :], TP[0][:, 0:6].rearrange("p (a b) -> p a b", b=2)[:, :, 0])\
                            .then_inc(rt_ready, 1)
                    if j == 5:
                        dve.wait_ge(fz_act, l + 1)
                        link(dve.tensor_scalar(fz[:, 0, :], fz[:, 0, :], 0.0, None, ALU.min))
                        link(dve.tensor_tensor(fz[:, 2, :], fz[:, 0, :], fz[:, 1, :], ALU.subtract))
                        a, s = 2, 1
                        while s < T:
                            b = 1 if a == 2 else 2
                            dve.tensor_copy(fz[:, b, 0:s], fz[:, a, 0:s])
                            link(dve.tensor_tensor(fz[:, b, s:T], fz[:, a, s:T], fz[:, a, 0:T - s], ALU.add))
                            a, s = b, 2 * s
                        dve.tensor_scalar(cneg, fz[:, a, :], -1.0 / SCALE, None, ALU.mult)\
                            .then_inc(cneg_ready, 1)
                        dve.wait_ge(cneg_ready, l + 1)
                dve.wait_ge(rt_ready, l + 1)
                for j in range(8, 12):
                    for w in range(3):
                        t = t0 + V_TILE + 3 * (j - 8) + w
                        dve.wait_ge(strip_done, strips_to_tile(t))
                        dve.tensor_scalar(v[:, w, 256 * (j - 8):256 * (j - 8) + 256], PJ[t % 2][:, 0:256],
                                          rt[:, w:w + 1], None, ALU.mult).then_inc(proj_free, 1)
                        if w != 1:
                            after(l, j, w // 2)
                    free(t)
                for u in range(8):
                    attention_max(l, u)
                    if u:
                        o_evacuate(l, u - 1)
                    for i in range(2):
                        g = 2 * u + i
                        t = t0 + GATE_TILE + g
                        dve.wait_ge(strip_done, strips_to_tile(t))
                        dve.tensor_tensor(gate[:, g, :], PJ[t % 2][:, 0:T], rb[:, :], ALU.mult).then_inc(proj_free, 1)
                        if i == 0:
                            attention_normalise(l, u)
                            after(l, 12 + u, i)
                            if 1 <= u <= 4:
                                o_normalise(l, u - 1)
                        else:
                            after(l, 12 + u, i)
                            if 1 <= u <= 4:
                                o_part(l, u - 1)
                o_evacuate(l, 7)
                for j in range(20, 24):
                    for i in range(4):
                        c = 4 * (j % 2) + i
                        t = t0 + (BD_TILE if j < 22 else BF_TILE) + c
                        g = c if j < 22 else 8 + c
                        dve.wait_ge(gate_e, 4 * l + g // 4 + 1)
                        dve.wait_ge(strip_done, strips_to_tile(t))
                        dve.tensor_tensor(gate[:, g, :], PJ[t % 2][:, 0:T], gate[:, g, :], ALU.mult)\
                            .then_inc(proj_free, 1)
                        free(t)
                        if j >= 22:
                            dve.tensor_tensor(gate[:, g, :], gate[:, g, :], gate[:, c, :], ALU.add)\
                                .then_inc(merged, 1)
                            if c:
                                merged_part(l, c - 1)
                        if i % 2:
                            after(l, j, i // 2)
                merged_part(l, KD - 1)
                n = 2 * l + 1
                for c in range(KD):
                    t = t0 + OUT_TILE + c
                    dve.wait_ge(strip_done, strips_to_tile(t))
                    dve.tensor_tensor(h[:, c, :], PJ[t % 2][:, 0:T], h[:, c, :], ALU.add).then_inc(proj_free, 1)
                    free(t)
                    if c == KD - 1:
                        x_part(n, c, vec[:, V_GFFN + 8 * l + c:V_GFFN + 8 * l + c + 1])
                    after(l, 24 + c // 2, c % 2)
                    if c < KD - 1:
                        x_part(n, c, vec[:, V_GFFN + 8 * l + c:V_GFFN + 8 * l + c + 1])
                if l == 0:
                    f0 = MIX_TILES

                    def ffh_part(f):
                        dve.wait_ge(ffh_hi_done, f + 1)
                        dve.tensor_tensor(ffh_lo[:, f, :], ubuf[:, f % 2, :], ffh_hi[:, f, :].bitcast(F32),
                                          ALU.subtract).then_inc(ffh_lo_done, 1)

                    dve.wait_ge(rstd_ready, 2)
                    for b in range(FFN_BLOCKS):
                        for i in range(2):
                            t = f0 + 4 * b + i
                            if b:
                                dve.wait_ge(ffh, 2 * b - 1 + i)
                            dve.wait_ge(strip_done, strips_to_tile(t))
                            dve.tensor_tensor(gbuf[:, i, :], PJ[t % 2][:, 0:T], rb[:, :], ALU.mult)\
                                .then_inc(proj_free, 1)
                            if b and i == 0:
                                ffh_part(2 * b - 1)
                            after(0, MIX_PIECES + 2 * b, i)
                        for i in range(2):
                            t = f0 + 4 * b + 2 + i
                            if b:
                                dve.wait_ge(ffh_lo_done, 2 * b - 1 + i)
                            dve.wait_ge(strip_done, strips_to_tile(t))
                            dve.tensor_tensor(ubuf[:, i, :], PJ[t % 2][:, 0:T], rb[:, :], ALU.mult)\
                                .then_inc(proj_free, 1)
                            free(t)
                            dve.wait_ge(silu_f, 2 * b + i + 1)
                            dve.tensor_tensor(ubuf[:, i, :], ubuf[:, i, :], gbuf[:, i, :], ALU.mult)\
                                .then_inc(ffh, 1)
                            after(0, MIX_PIECES + 2 * b + 1, i)
                            if i == 0:
                                ffh_part(2 * b)
                    ffh_part(FT - 1)
                    for dp in range(4):
                        for part in range(3):
                            for i in range(2):
                                c = 2 * dp + i
                                t = f0 + 4 * FFN_BLOCKS + c
                                if part == 2:
                                    dve.wait_ge(strip_done, strips_to_tile(t))
                                    dve.tensor_tensor(h[:, c, :], PJ[t % 2][:, 0:T], h[:, c, :], ALU.add)\
                                        .then_inc(proj_free, 1)
                                    free(t)
                                if part == 2 and c == KD - 1:
                                    x_part(2, c, vec[:, V_GMIX + 8 + c:V_GMIX + 8 + c + 1])
                                after(0, MIX_PIECES + 2 * FFN_BLOCKS + 3 * dp + part, i)
                                if part == 2 and c < KD - 1:
                                    x_part(2, c, vec[:, V_GMIX + 8 + c:V_GMIX + 8 + c + 1])

            dve.memset(y_hi[:, :].bitcast(F32), 0.0)
            dve.memset(y_lo[:, :].bitcast(F32), 0.0)
            dve.memset(put_hi[:, :].bitcast(F32), 0.0)
            dve.memset(put_lo[:, :].bitcast(F32), 0.0)
            dve.memset(pos[:, :, NE:NE + 1], -1.0)
            link(dve.memset(comb[:, :, NE:NE + 1], 0.0))
            dve.wait_ge(rt_psum, 3)
            dve.tensor_copy(rt[:, :], TP[0][:, 0:6].rearrange("p (a b) -> p a b", b=2)[:, :, 0]).then_inc(rt_ready, 1)
            dve.wait_ge(rt_ready, 3)
            dve.wait_ge(logit_done, 1)
            for tt in range(2):
                link(dve.tensor_scalar(lg[:, tt, :], OB[:, 8 * tt:8 * tt + 8], rt[:, tt + 1:tt + 2], None, ALU.mult))
            rev = cst[:, C_REV:C_REV + 16].rearrange("p (a b) -> p a b", a=2)

            def wide(ap):
                return ap.unsqueeze(2).broadcast_to([P, 2, NE])

            def first_max(sel, value):
                link(dve.tensor_reduce(value, lg[:, :, :], AX, ALU.max))
                link(dve.tensor_tensor(eq[:, :, :], lg[:, :, :], wide(value), ALU.is_equal))
                link(dve.tensor_tensor(eq[:, :, :], eq[:, :, :], rev, ALU.mult))
                link(dve.tensor_reduce(top[:, 2, :], eq[:, :, :], AX, ALU.max))
                link(dve.tensor_tensor(sel[:, :, :], eq[:, :, :], wide(top[:, 2, :]), ALU.is_equal))

            first_max(sel1, top[:, 0, :])
            link(dve.scalar_tensor_tensor(lg[:, :, :], sel1[:, :, :], -3e38, lg[:, :, :], ALU.mult, ALU.add))
            first_max(sel2, top[:, 1, :])
            link(dve.tensor_tensor(mask[:, :, :], sel1[:, :, :], sel2[:, :, :], ALU.add))
            dve.nop().then_inc(mask_ready, 1)
            link(dve.tensor_tensor(top[:, 3, :], top[:, 1, :], top[:, 0, :], ALU.subtract))
            dve.nop().then_inc(top_diff, 1)
            dve.wait_ge(top_exp, 1)
            link(dve.tensor_scalar(top[:, 5, :], top[:, 4, :], 1.0, None, ALU.add))
            link(dve.reciprocal(top[:, 5, :], top[:, 5, :]))
            link(dve.tensor_tensor(top[:, 6, :], top[:, 4, :], top[:, 5, :], ALU.mult))
            link(dve.tensor_tensor(sel1[:, :, :], sel1[:, :, :], wide(top[:, 5, :]), ALU.mult))
            link(dve.tensor_tensor(sel2[:, :, :], sel2[:, :, :], wide(top[:, 6, :]), ALU.mult))
            link(dve.tensor_tensor(comb[:, :, 0:NE], sel1[:, :, :], sel2[:, :, :], ALU.add))
            dve.wait_ge(rank_done, 1)
            link(dve.tensor_copy(cnt[:, :, :], OB[:, 32:56].rearrange("p (a b) -> p a b", a=3)))
            link(dve.scalar_tensor_tensor(pos[:, :, 0:NE], cnt[:, 0:2, :], 1.0, mask[:, :, :], ALU.add, ALU.mult))
            link(dve.tensor_scalar(pos[:, :, 0:NE], pos[:, :, 0:NE], -1.0, None, ALU.add))
            for i in range(4):
                tt, half = divmod(i, 2)
                dve.wait_ge(xt_hi_done, i + 1)
                dve.scalar_tensor_tensor(xt_lo[:, tt, 512 * half:512 * half + 512], XT_BANK(SB, TP, i)[:, :],
                                         rt[:, tt + 1:tt + 2],
                                         xt_hi[:, tt, 512 * half:512 * half + 512].bitcast(F32),
                                         ALU.mult, ALU.subtract).then_inc(xt_lo_done, 1)

            def build_pick(e, block):
                iota = cst[:, C_IOTA + P * block:C_IOTA + P * block + P]
                for tt in range(2):
                    where = pos[:, tt, bass.ds(e, 1)]
                    dve.tensor_scalar(pick[:, tt, :], iota, where, None, ALU.is_equal)
                    ins = dve.tensor_scalar(pickw[:, tt, :], iota, where, comb[:, tt, bass.ds(e, 1)], ALU.is_equal,
                                            ALU.mult)
                ins.then_inc(pick_ready, 1)

            build_pick(0, 0)
            o1, o2, o3 = cnt[0:1, 0, :], cnt[0:1, 1, :], cnt[0:1, 2, :]
            link(dve.tensor_scalar(o1, o3, float(P), None, ALU.is_gt))
            link(dve.tensor_reduce(tab_f[0:1, 3:4], o1, AX, ALU.add))
            for o in range(MAX_OVER):
                link(dve.tensor_tensor(o2, o1, rev[0:1, 0, :], ALU.mult))
                link(dve.tensor_reduce(tab_f[0:1, o:o + 1], o2, AX, ALU.max))
                link(dve.tensor_scalar(o2, o2, tab_f[0:1, o:o + 1], None, ALU.is_lt))
                link(dve.tensor_tensor(o1, o1, o2, ALU.mult))
                link(dve.tensor_scalar(tab_f[0:1, o:o + 1], tab_f[0:1, o:o + 1], -1.0, float(NE), ALU.mult, ALU.add))
                link(dve.tensor_scalar(tab_f[0:1, o:o + 1], tab_f[0:1, o:o + 1], float(NE - 1), None, ALU.min))
            dve.tensor_copy(tab[0:1, :], tab_f[0:1, :]).then_inc(table_ready, 1)
            dve.wait_ge(table_ready, 1)

            def xg_part(g):
                dve.wait_ge(xg_hi_done, g + 1)
                dve.tensor_tensor(xg_lo[:, 0:512], SB[0][:, :], xg_hi[:, 0:512].bitcast(F32), ALU.subtract)
                dve.tensor_tensor(xg_lo[:, 512:1024], SB[1][:, :], xg_hi[:, 512:1024].bitcast(F32),
                                  ALU.subtract).then_inc(xg_lo_done, 1)

            def put_part(s):
                dve.wait_ge(put_hi_done, s + 1)
                dve.tensor_tensor(put_lo[:, :], OB[:, 0:2 * P], put_hi[:, :].bitcast(F32), ALU.subtract)\
                    .then_inc(put_lo_done, 1)

            def add_scatter(s, r):
                dve.wait_ge(sc_psum, s * 4 + (r + 1))
                dve.tensor_tensor(h[:, 2 * r:2 * r + 2, NMETA:T], OB[:, :].rearrange("p (a b) -> p a b", a=2),
                                  h[:, 2 * r:2 * r + 2, NMETA:T], ALU.add).then_inc(sc_add, 1)

            def job(J, j0, turn, main, e=None):
                q = 0

                def used(count=1):
                    nonlocal q
                    for _ in range(count):
                        if main or q + LO_AHEAD < HJOB:
                            split(2 * j0 + q + LO_AHEAD, turn)
                        q += 1

                def hT_part(n):
                    dve.wait_ge(hT_hi_done, J * UNITS + (n + 1))
                    dve.tensor_tensor(hT_lo[:, :], TP[0][:, :], hT_hi[:, :].bitcast(F32), ALU.subtract)\
                        .then_inc(hT_lo_done, 1)

                if not main:
                    for i in range(LO_AHEAD):
                        split(2 * j0 + i, turn)
                    dve.wait_ge(xg_psum, J + 1)
                    dve.wait_ge(put_psum, J)
                    build_pick(e, 1)
                    xg_part(J + 1)
                    put_part(J)
                for n in range(UNITS):
                    adding = n == 1 and main
                    used()
                    if adding:
                        add_scatter(J, 0)
                    used(2)
                    if n:
                        hT_part(n - 1)
                    if adding:
                        add_scatter(J, 1)
                    used()
                    if n == 2 and main:
                        put_part(J)
                    if n == 4 and main:
                        dve.wait_ge(xg_psum, J + 1)
                        dve.wait_ge(put_psum, J + 1)
                        build_pick(J + 1, 0)
                    used()
                    if adding:
                        add_scatter(J, 2)
                    used(2)
                    if adding:
                        add_scatter(J, 3)
                    used()
                    dve.wait_ge(silu_done, J * UNITS + (n + 2))
                    dve.wait_ge(half_used, J * HJOB + 2 * (6 * n + 2 if n else 4))
                    dve.tensor_tensor(hb[:, :], (PJ if n % 2 == 0 else SB)[1][:, :], sg[:, :], ALU.mult)\
                        .then_inc(hm_done, 1)
                    if n:
                        used(4)
                hT_part(UNITS - 1)
                used()
                if main:
                    xg_part(J + 1)
                used(3)
                dve.wait_ge(y_hi_done, J + 1)
                dve.tensor_tensor(y_lo[:, 0:512], TP[1][:, :], y_hi[:, 0:512].bitcast(F32), ALU.subtract)
                dve.tensor_tensor(y_lo[:, 512:1024], TP[2][:, :], y_hi[:, 512:1024].bitcast(F32),
                                  ALU.subtract).then_inc(y_lo_done, 1)
                if not main:
                    for r in range(4):
                        add_scatter(J + 1, r)

            dve.nop().then_inc(hm_done, 1)
            dve.nop().then_inc(hT_lo_done, 1)
            dve.nop().then_inc(y_lo_done, 1)
            dve.nop().then_inc(put_lo_done, 1)
            dve.nop().then_inc(sc_add, 1)
            xg_part(0)
            with dve.Fori(0, NE) as e:
                job(e, MOE0, e, True)
            split(2 * OVER0 - 1)
            for r in range(4):
                add_scatter(NE, r)
            over = dve.value_load(tab[0:1, 3:4], min_val=0, max_val=MAX_OVER)
            with dve.Fori(0, MAX_OVER) as o:
                with dve.If(o < over):
                    e = dve.value_load(tab[0:1, bass.ds(o, 1)], min_val=0, max_val=NE - 1)
                    job(o + NE, OVER0, o, False, e)
            dve.drain().then_inc(h_final, 1)
            dve.wait_ge(rstd_ready, 5)
            for c in range(KD):
                dve.scalar_tensor_tensor(outb[:, c, :], h[:, c, NMETA:T], vec[:, V_GFIN + c:V_GFIN + c + 1],
                                         rb[:, NMETA:T], ALU.mult, ALU.mult).then_inc(out_ready, 1)

        @block.tensor
        def _(pe):
            def mm3(out, l_hi, l_lo, r_hi, r_lo, first, last):
                pe.matmul(out, l_hi, r_hi, start=first, stop=False)
                pe.matmul(out, l_hi, r_lo, start=False, stop=False)
                return pe.matmul(out, l_lo, r_hi, start=False, stop=last)

            ident = cst[:, C_ID:C_ID + P]

            def stat(n, c):
                pe.wait_ge(sq_ready, 8 * n + c + 1)
                pe.matmul(OB[:, 0:T], ones[:, :], sq[:, c % 2, :], start=(c == 0), stop=(c == KD - 1))\
                    .then_inc(stat_done, 1)

            def row_rstd(k):
                for w in range(3):
                    ins = pe.matmul(TP[0][:, 2 * w:2 * w + 2], rb[0:1, WIN[w]:WIN[w] + P], ones[0:1, 0:2],
                                    start=True, stop=True)
                ins.then_inc(rt_psum, 1)

            def take(i, turn=0):
                pe.wait_ge(lo_done, turn * HJOB + (i + 1))
                return w_hi[:, i % NHALF, :], w_lo[:, i % NHALF, :]

            def begin(t):
                if t >= 2:
                    pe.wait_ge(proj_free, t - 1)
                return PJ[t % 2]

            def stationary(t, half, nk, r_hi, r_lo, r0, c0=0, width=P, first=True, last=True):
                hi, lo = half
                for k in range(nk):
                    c = width * k + c0
                    ins = mm3(PJ[t % 2][:, 0:T], hi[:, c:c + P], lo[:, c:c + P], r_hi[:, r0 + k, :],
                              r_lo[:, r0 + k, :], first and k == 0, last and k == nk - 1)
                return ins

            def queries_keys(l, u):
                un = 8 * l + u
                src, i = qk[u // 4], u % 4
                if u == 0:
                    pe.wait_ge(rope_done, 8 * l + 8)
                if u == 4:
                    pe.wait_ge(cneg_ready, l + 1)
                if un:
                    pe.wait_ge(s_free, 2 * un)
                for m in range(2):
                    r = slice(64 * m, 64 * m + 64)
                    for s, (c0, w) in enumerate(SEG):
                        out = SB[m][:, c0:c0 + w]
                        ins = pe.matmul(out, src[r, i, WIN[s]:WIN[s] + P], src[r, 4 + i, 0:w], start=True,
                                        stop=(u < 4))
                        if u >= 4:
                            head = 2 * (u - 4) + m
                            ins = pe.matmul(out, cst[0:8, C_ID + head:C_ID + head + 1].to_broadcast([8, P]),
                                            cneg[:, 0:w], start=False, stop=True)
                    ins.then_inc(s_done, 1)

            def transposes(l, u):
                un = 8 * l + u
                pe.wait_ge(a_ready, un + 1)
                if un:
                    pe.wait_ge(aT_ready, un)
                if u == 0:
                    pe.wait_ge(rt_ready, l + 1)
                if u >= 4:
                    pe.wait_ge(o_rs_ready, 4 * l + 4)
                for m in range(1 if u < 4 else 2):
                    a = score[:, m, :]
                    c1, c2 = SEG[1][0], SEG[2][0]
                    for out, src in ((TP[m][:, 0:128], a[:, c1 + 16:c1 + 144]),
                                     (TP[m][:, 128:256], a[:, c2 + 16:c2 + 144]),
                                     (TP[m][:, 256:384], a[:, c2 + 144:c2 + 272]),
                                     (TP[2][0:16, 256 * m:256 * m + 128], a[:, c1:c1 + 16]),
                                     (TP[2][0:16, 256 * m + 128:256 * m + 256], a[:, c2:c2 + 16])):
                        pe.transpose(out, src, ident)
                    ins = pe.transpose(TP[m][0:16, 384:400], a[0:16, 0:16], ident[0:16, 0:16])
                ins.then_inc(tr_done, 1)

            def values(l, u):
                un = 8 * l + u
                pe.wait_ge(aT_ready, un + 1)
                if 1 <= u <= 4:
                    pe.wait_ge(o_free, 4 * l + u)
                elif un:
                    pe.wait_ge(o_lo, un)
                for m in range(1 if u < 4 else 2):
                    c, w = (P * u, P) if u < 4 else (512 + P * (u - 4) + 64 * m, 64)
                    r = slice(64 * m, 64 * m + w)
                    pe.matmul(OB[r, 0:T], v[0:16, 0, c:c + w], aT[0:16, m, 384:656], start=True, stop=False)
                    pe.matmul(OB[r, 16:T], v[:, 1, c:c + w], aT[:, m, 0:256], start=False, stop=False)
                    ins = pe.matmul(OB[r, 144:T], v[:, 2, c:c + w], aT[:, m, 256:384], start=False, stop=True)
                ins.then_inc(pv_done, 1)

            def o_statistics(l, u):
                pe.wait_ge(o_sq_ready, 4 * l + u + 1)
                pe.matmul(TP[1][:, 0:T], ones[:, :], o_sq, start=True, stop=True).then_inc(o_stat, 1)

            pe.wait_ge(pool_set, 4)
            for c in range(KD):
                stat(0, c)
            pe.wait_ge(small_lo, 2)
            for l in range(LAYERS):
                t0 = l * (MIX_TILES + FFN_TILES)
                p0 = l * LAYER1
                xh, xl = x_hi[0], x_lo[0]
                begin(t0)
                for k in range(KD):
                    pe.wait_ge(x_lo_done, X_HI_COUNT(2 * l) + k + 1)
                    c = 64 * l + 8 * k
                    ins = mm3(PJ[t0 % 2][:, 0:T], ff_hi[:, c:c + P], ff_lo[:, c:c + P], xh[:, k, :], xl[:, k, :],
                              k == 0, k == KD - 1)
                ins.then_inc(strip_done, 1)
                for j in range(8):
                    for i in range(2):
                        t = t0 + 1 + 2 * j + i
                        half = take(2 * (p0 + j) + i)
                        begin(t)
                        stationary(t, half, KD, xh, xl, 0).then_inc(strip_done, 1)
                    if j == 0:
                        pe.wait_ge(rstd_ready, 2 * l + 1)
                        row_rstd(l)
                    if l == 0 and j == 1:
                        pe.wait_ge(tables_in, 32)
                    if 1 <= j <= 4:
                        for i in (2 * j - 2, 2 * j - 1):
                            pe.wait_ge(proj_free, t0 + 2 + i)
                            if i >= 2:
                                pe.wait_ge(rope_done, 8 * l + i - 1)
                            elif l:
                                pe.wait_ge(aT_ready, 8 * l)
                            pe.matmul(TP[1 + i % 2][:, 0:T], cst[:, C_ROT:C_ROT + P], qk[0][:, i, :], start=True,
                                      stop=True).then_inc(rot_done, 1)
                for j in range(8, 12):
                    halves = [take(2 * (p0 + j) + i) for i in range(2)]
                    for w in range(3):
                        t = t0 + V_TILE + 3 * (j - 8) + w
                        begin(t)
                        for k in range(KD):
                            hi, lo = halves[k // 4]
                            c = 256 * (k % 4)
                            ins = mm3(PJ[t % 2][:, 0:256], xh[:, k, WIN[w]:WIN[w] + P], xl[:, k, WIN[w]:WIN[w] + P],
                                      hi[:, c:c + 256], lo[:, c:c + 256], k == 0, k == KD - 1)
                        ins.then_inc(strip_done, 1)
                pe.wait_ge(proj_free, t0 + GATE_TILE)
                queries_keys(l, 0)
                for u in range(8):
                    for i in range(2):
                        t = t0 + GATE_TILE + 2 * u + i
                        half = take(2 * (p0 + 12 + u) + i)
                        begin(t)
                        stationary(t, half, KD, xh, xl, 0).then_inc(strip_done, 1)
                        if i == 0 and 1 <= u <= 4:
                            o_statistics(l, u - 1)
                    if u < 7:
                        queries_keys(l, u + 1)
                    transposes(l, u)
                    values(l, u)
                for j in range(20, 24):
                    pe.wait_ge(o_lo, 8 * l + (4 if j < 22 else 8))
                    for i in range(4):
                        t = t0 + (BD_TILE if j < 22 else BF_TILE) + 4 * (j % 2) + i
                        half = take(2 * (p0 + j) + i // 2)
                        begin(t)
                        stationary(t, half, 4, x_hi[1], x_lo[1], 0 if j < 22 else 4, P * (i % 2), 2 * P)\
                            .then_inc(strip_done, 1)
                n = 2 * l + 1
                pe.wait_ge(x_lo_done, X_HI_COUNT(n))
                for c in range(KD):
                    t = t0 + OUT_TILE + c
                    half = take(2 * (p0 + 24) + c)
                    begin(t)
                    stationary(t, half, KD, xh, xl, 0).then_inc(strip_done, 1)
                    if c >= 1:
                        stat(n, c - 1)
                stat(n, KD - 1)
                if l == 0:
                    f0 = MIX_TILES
                    for b in range(FFN_BLOCKS):
                        for s in range(2):
                            for i in range(2):
                                t = f0 + 4 * b + 2 * s + i
                                hi, lo = take(2 * (MIX_PIECES + 2 * b + s) + i)
                                begin(t)
                                for k in range(KD):
                                    if b == 0 and s == 0 and i == 0:
                                        pe.wait_ge(x_lo_done, X_HI_COUNT(1) + k + 1)
                                    c = P * k
                                    ins = mm3(PJ[t % 2][:, 0:T], hi[:, c:c + P], lo[:, c:c + P], x_hi[1][:, k, :],
                                              x_lo[1][:, k, :], k == 0, k == KD - 1)
                                ins.then_inc(strip_done, 1)
                    for dp in range(4):
                        for part, (k0, nk) in enumerate(DOWN_K):
                            pe.wait_ge(ffh_lo_done, k0 + nk)
                            for i in range(2):
                                t = f0 + 4 * FFN_BLOCKS + 2 * dp + i
                                half = take(2 * (MIX_PIECES + 2 * FFN_BLOCKS + 3 * dp + part) + i)
                                if part == 0:
                                    begin(t)
                                ins = stationary(t, half, nk, ffh_hi, ffh_lo, k0, first=(part == 0),
                                                 last=(part == 2))
                                ins.then_inc(strip_done, 1)
                        if dp:
                            stat(2, 2 * dp - 2)
                            stat(2, 2 * dp - 1)
                    stat(2, 6)
                    stat(2, 7)

            pe.wait_ge(ident_done, 1)
            pe.wait_ge(aT_ready, 8 * LAYERS)
            pe.wait_ge(s_free, 16 * LAYERS)
            pe.wait_ge(x_lo_done, X_HI_COUNT(3) + KD)
            for i in range(4):
                tt, half = divmod(i, 2)
                w = slice(WIN[tt + 1], WIN[tt + 1] + P)
                for k in range(4):
                    out = XT_BANK(SB, TP, i)[:, P * k:P * k + P]
                    pe.matmul(out, x_hi[1][:, 4 * half + k, w], ident_r[:, :], start=True, stop=False)
                    ins = pe.matmul(out, x_lo[1][:, 4 * half + k, w], ident_r[:, :], start=False, stop=True)
                ins.then_inc(xt_psum, 1)
            pe.wait_ge(rstd_ready, 4)
            row_rstd(2)
            for tt in range(2):
                for k in range(KD):
                    pe.wait_ge(x_lo_done, X_HI_COUNT(3) + k + 1)
                    w = slice(WIN[tt + 1], WIN[tt + 1] + P)
                    ins = mm3(OB[:, 8 * tt:8 * tt + 8], x_hi[1][:, k, w], x_lo[1][:, k, w], rw_hi[:, k, :],
                              rw_lo[:, k, :], k == 0, k == KD - 1)
            ins.then_inc(logit_done, 1)
            pe.wait_ge(mask_ready, 1)
            tri = cst[:, C_TRI:C_TRI + P]
            pe.matmul(OB[:, 32:40], tri, mask[:, 0, :], start=True, stop=True)
            pe.matmul(OB[:, 40:48], tri, mask[:, 1, :], start=True, stop=False)
            pe.matmul(OB[:, 40:48], ones[:, :], mask[:, 0, :], start=False, stop=True)
            pe.matmul(OB[:, 48:56], ones[:, :], mask[:, 0, :], start=True, stop=False)
            pe.matmul(OB[:, 48:56], ones[:, :], mask[:, 1, :], start=False, stop=True).then_inc(rank_done, 1)

            def gather(g):
                pe.wait_ge(pick_ready, g + 1)
                for c in range(KD):
                    out = SB[c // 4][:, P * (c % 4):P * (c % 4) + P]
                    for tt in range(2):
                        pe.matmul(out, xt_hi[:, tt, P * c:P * c + P], pick[:, tt, :], start=(tt == 0), stop=False)
                        ins = pe.matmul(out, xt_lo[:, tt, P * c:P * c + P], pick[:, tt, :], start=False,
                                        stop=(tt == 1))
                ins.then_inc(xg_psum, 1)

            def put_transpose(s):
                pe.wait_ge(pick_ready, s + 1)
                for tt in range(2):
                    ins = pe.transpose(OB[:, P * tt:P * tt + P], pickw[:, tt, :], ident)
                ins.then_inc(put_psum, 1)

            def scatter(s, r):
                if r == 0:
                    pe.wait_ge(y_lo_done, s + 1)
                    pe.wait_ge(put_lo_done, s + 1)
                else:
                    pe.wait_ge(sc_add, s * 4 + (r + 1))
                for i in range(2):
                    c = P * (2 * r + i)
                    ins = mm3(OB[:, 256 * i:256 * i + 256], y_hi[:, c:c + P], y_lo[:, c:c + P], put_hi[:, :],
                              put_lo[:, :], True, True)
                ins.then_inc(sc_psum, 1)

            def job(J, j0, turn, main):
                q = 0

                def half():
                    nonlocal q
                    q += 1
                    return take(2 * j0 + q - 1, turn)

                def up_half(out, part):
                    for i in range(2):
                        hi, lo = half()
                        for k in range(2):
                            c = P * (4 * part + 2 * i + k)
                            ins = mm3(out, xg_hi[:, c:c + P], xg_lo[:, c:c + P], hi[:, 512 * k:512 * k + 512],
                                      lo[:, 512 * k:512 * k + 512], c == 0, c == 7 * P)
                        ins.then_inc(half_used, 1)

                def turn_hidden(n):
                    pe.wait_ge(hm_done, J * UNITS + (n + 2))
                    pe.wait_ge(hT_lo_done, J * UNITS + (n + 1))
                    for i in range(4):
                        ins = pe.transpose(TP[0][:, P * i:P * i + P], hb[:, P * i:P * i + P], ident)
                    ins.then_inc(hT_psum, 1)

                def down_half(n, part):
                    pe.wait_ge(hT_lo_done, J * UNITS + (n + 2))
                    if n == 0:
                        pe.wait_ge(y_lo_done, J + 1)
                    for i in range(2):
                        hi, lo = half()
                        c = P * (2 * part + i)
                        for s in range(2):
                            ins = mm3(TP[1 + s][:, :], hT_hi[:, c:c + P], hT_lo[:, c:c + P],
                                      hi[:, 512 * s:512 * s + 512], lo[:, 512 * s:512 * s + 512],
                                      n == 0 and c == 0, n == UNITS - 1 and c == 3 * P)
                        ins.then_inc(half_used, 1)

                if not main:
                    gather(J + 1)
                    put_transpose_over(J)
                pe.wait_ge(xg_lo_done, J + (1 if main else 2))
                for n in range(UNITS):
                    G, U = PJ if n % 2 == 0 else SB
                    if n != 1:
                        pe.wait_ge(silu_done, J * UNITS + (n if n else 1))
                    up_half(G[:, :], 0)
                    if n:
                        turn_hidden(n - 1)
                    if n == 1 and main:
                        scatter(J, 1)
                    if n == 2 and main:
                        pe.wait_ge(sc_add, J * 4 + 5)
                        put_transpose(J)
                    up_half(G[:, :], 1)
                    if n == 1 and main:
                        scatter(J, 2)
                    if n != 1:
                        pe.wait_ge(hm_done, J * UNITS + (n if n else 1))
                    up_half(U[:, :], 0)
                    if n == 1 and main:
                        scatter(J, 3)
                    up_half(U[:, :], 1)
                    if n == 0 and main:
                        scatter(J, 0)
                    if n:
                        down_half(n - 1, 0)
                        if n == UNITS - 1:
                            turn_hidden(n)
                        down_half(n - 1, 1)
                if main:
                    gather(J + 1)
                down_half(UNITS - 1, 0)
                down_half(UNITS - 1, 1)
                if not main:
                    for r in range(4):
                        scatter(J + 1, r)

            def put_transpose_over(s):
                for tt in range(2):
                    ins = pe.transpose(OB[:, P * tt:P * tt + P], pickw[:, tt, :], ident)
                ins.then_inc(put_psum, 1)

            pe.wait_ge(xt_lo_done, 4)
            pe.wait_ge(proj_free, LAYERS * MIX_TILES + FFN_TILES)
            gather(0)
            with pe.Fori(0, NE) as e:
                job(e, MOE0, e, True)
            pe.wait_ge(xg_lo_done, NE + 1)
            for r in range(4):
                scatter(NE, r)
            pe.wait_ge(table_ready, 1)
            over = pe.value_load(tab[0:1, 3:4], min_val=0, max_val=MAX_OVER)
            with pe.Fori(0, MAX_OVER) as o:
                with pe.If(o < over):
                    pe.wait_ge(sc_add, o * 4 + (4 * NE + 5))
                    job(o + NE, OVER0, o, False)
            pe.wait_ge(h_final, 1)
            for c in range(KD):
                stat(4, c)


def X_HI_COUNT(n):
    return 8 * n + 8 * ((n + 1) // 2)


def XT_BANK(SB, TP, i):
    return (SB[0], SB[1], TP[1], TP[2])[i]


def kernel(**inputs):
    import numpy as np
    import concourse.bacc as bacc
    from concourse import mybir as mb
    from concourse.bass_utils import run_bass_kernel_spmd as run

    a = {k: np.asarray(x) for k, x in inputs.items()}
    f32 = np.float32

    def on_partitions(x):
        return np.ascontiguousarray(np.moveaxis(x.reshape(*x.shape[:-1], -1, P), -1, 0).reshape(P, -1))

    tokens = np.concatenate([a["meta_tokens"], a["x"][0]], axis=0)
    xT = np.ascontiguousarray(tokens.T.reshape(KD, P, T).transpose(1, 0, 2))

    vecs = np.zeros((P, V_W), f32)
    vecs[:, V_GMIX:V_GMIX + 16] = on_partitions(a["norm_mix_g"])
    vecs[:, V_GFFN:V_GFFN + 16] = on_partitions(a["norm_ffn_g"])
    vecs[:, V_GFIN:V_GFIN + 8] = on_partitions(a["final_norm_g"])
    vecs[:, V_SUB:V_SUB + 2] = a["diff_subln_g"].T
    vecs[0:8, V_BF:V_BF + 2] = a["b_forget"].T
    ff = a["w_in"][:, :, FF_COL:FF_COL + 8].reshape(LAYERS, KD, P, 8)
    vecs[:, V_FF:V_FF + 128] = ff.transpose(2, 0, 1, 3).reshape(P, -1)
    vecs[:, V_RT:V_RT + 64] = a["moe_router"][0].reshape(KD, P, NE).transpose(1, 0, 2).reshape(P, -1)
    lam = np.ascontiguousarray(np.broadcast_to(a["diff_lambda"].reshape(1, -1), (P, 512)))

    c = np.zeros((P, C_W), f32)
    rows = np.arange(P)
    for (c0, w), start in zip(SEG, WIN):
        seen = np.arange(w)[None, :] <= (start + rows)[:, None]
        c[:, C_MASK + c0:C_MASK + c0 + w] = np.where(seen, 0.0, -BIG / SCALE)
    c[:, C_ID:C_ID + P] = np.eye(P)
    c[:, C_TRI:C_TRI + P] = rows[:, None] < rows[None, :]
    c[:, C_IOTA:C_IOTA + 2 * P] = np.arange(2 * P)
    inv = f32(500000.0) ** (-np.arange(0, 16, 2, dtype=f32) / f32(16))
    ang = np.arange(T, dtype=f32)[None, :] * inv[:, None].astype(f32)
    d = rows % 64
    c[:, C_COS:C_COS + T] = np.where(d[:, None] < 16, np.cos(ang)[d % 8], 1.0)
    c[:, C_SIN:C_SIN + T] = np.where(d[:, None] < 16, np.sin(ang)[d % 8], 0.0) * np.where(d < 8, -1, 1)[:, None]
    for p in rows[d < 16]:
        c[p ^ 8, C_ROT + p] = 1.0
    c[:, C_REV:C_REV + 16] = NE - np.arange(16) % NE

    arrays = {"xT": xT, "w_in": a["w_in"], "lam": lam, "w_bd": a["w_branch_diff"], "w_bf": a["w_branch_fox"],
              "w_out": a["w_out"], "f_g": a["ffn_w_gate"], "f_u": a["ffn_w_up"], "f_d": a["ffn_w_down"],
              "m_g": a["moe_w_gate"], "m_u": a["moe_w_up"], "m_d": a["moe_w_down"], "consts": c, "vecs": vecs}
    nc = bacc.Bacc("TRN2", target_bir_lowering=False, num_devices=1)
    args = [nc.dram_tensor(name, x.shape, mb.dt.from_np(x.dtype), kind="ExternalInput").ap()
            for name, x in arrays.items()]
    out = nc.dram_tensor("outT", (P, KD, SEQ), mb.dt.float32, kind="ExternalOutput").ap()
    trunk(nc, *args, out)
    r = run(nc, [arrays], core_ids=[0])
    got = r.results[0]["outT"]
    return np.ascontiguousarray(got.transpose(1, 0, 2).reshape(D, SEQ).T).reshape(1, SEQ, D)
```

```python
import math
from contextlib import ExitStack

import concourse.bass as bass
from concourse import mybir

F32 = mybir.dt.float32
F32R = mybir.dt.float32r
I32 = mybir.dt.int32
ACT = mybir.ActivationFunctionType
ALU = mybir.AluOpType
AX = mybir.AxisListType.X

P = 128
D = 1024
KD = D // P
NMETA = 16
SEQ = 256
T = NMETA + SEQ
LAYERS = 2
DFF = 2816
FT = DFF // P
NE = 8
DFE = 3584
EPS = 1e-6
SCALE = 64 ** -0.5
BIG = 1e30
WIN = [0, NMETA, NMETA + P]
FF_COL = 3072
GATE_COL = FF_COL + 8
SEG = [(0, 16), (16, 144), (160, 272)]

NRAW = 6
COLS = 2048
NHALF = 6
HCOLS = COLS // 2
HI_AHEAD = NHALF
LO_AHEAD = NHALF - 1
MIX_PIECES = 28
FFN_BLOCKS = DFF // 256
FFN_PIECES = 2 * FFN_BLOCKS + 12
FFN_UNROLL = 3
FFN_TURNS = (FFN_BLOCKS - 2) // FFN_UNROLL
FFN_STEP = 4 * FFN_UNROLL
LAYER1 = MIX_PIECES + FFN_PIECES
MOE0 = LAYER1 + MIX_PIECES
UNITS = DFE // 512
JOB = 6 * UNITS
HJOB = 2 * JOB
EMPTY = NHALF // 2
OVER0 = MOE0 + NE * JOB + EMPTY
MAX_OVER = 3
assert MOE0 % NRAW == 0 and JOB % NRAW == 0 and HJOB % NHALF == 0 and 2 * MOE0 % NHALF == 0
assert FFN_BLOCKS == 2 + FFN_TURNS * FFN_UNROLL and FFN_STEP % (2 * NRAW) == 0 and FFN_STEP % NHALF == 0
DOWN_K = [(0, 8), (8, 8), (16, 6)]

MIX_TILES = 69
FFN_TILES = 4 * FFN_BLOCKS + 8
V_TILE, GATE_TILE, BD_TILE, BF_TILE, OUT_TILE = 17, 29, 45, 53, 61
DOWN_TILE = MIX_TILES + 4 * FFN_BLOCKS
FFN_STRIPS = 4 * FFN_BLOCKS + 24


def strips_to_tile(t):
    if t < DOWN_TILE:
        return t + 1
    if t < MIX_TILES + FFN_TILES:
        dp, i = divmod(t - DOWN_TILE, 2)
        return DOWN_TILE + 6 * dp + 4 + i + 1
    return t + 1 + FFN_STRIPS - FFN_TILES


def strips_to_half(i):
    j, half = divmod(i, 2)
    l, j = divmod(j, LAYER1)
    base = l * (MIX_TILES + FFN_STRIPS)
    if 8 <= j < 12:
        return base + V_TILE + 3 * (j - 7)
    for first, last, start, each in ((0, 8, 1, 1), (12, 20, GATE_TILE, 1), (20, 24, BD_TILE, 2),
                                     (24, LAYER1, OUT_TILE, 1)):
        if first <= j < last:
            return base + start + each * (2 * (j - first) + half + 1)


C_MASK, C_ID, C_TRI, C_IOTA, C_ROT, C_COS, C_SIN, C_REV = 0, 432, 560, 688, 944, 1072, 1344, 1616
C_W = 1632
V_GMIX, V_GFFN, V_GFIN, V_SUB, V_BF, V_FF, V_RT = 0, 16, 32, 40, 42, 44, 172
V_W = 236
SMALL = V_W - V_FF


class Chain:

    def __init__(self, eng, sem):
        self.eng, self.sem, self.k = eng, sem, 0

    def __call__(self, ins):
        self.k += 1
        ins.then_inc(self.sem, 1)
        self.eng.wait_ge(self.sem, self.k)


def trunk(nc, xT, w_in, lam, w_bd, w_bf, w_out, f_g, f_u, f_d, m_g, m_u, m_d, consts, vecs, outT):
    lam_init = [0.8 - 0.6 * math.exp(-0.3 * l) for l in range(LAYERS)]
    ctx = ExitStack()
    with ctx:
        def sb(name, shape, dt=F32, scope=ctx):
            return scope.enter_context(nc.sbuf_tensor(name, shape, dt))

        def bank(name):
            return ctx.enter_context(nc.psum_tensor(name, [P, 512], F32))

        def sem(name):
            return ctx.enter_context(nc.semaphore(name))

        raw = sb("raw", [P, NRAW, COLS])
        w_hi = sb("w_hi", [P, NHALF, HCOLS], F32R)
        w_lo = sb("w_lo", [P, NHALF, HCOLS], F32R)
        h = sb("h", [P, KD, T])
        x_hi = [sb(f"x_hi{i}", [P, KD, T], F32R) for i in range(2)]
        x_lo = [sb(f"x_lo{i}", [P, KD, T], F32R) for i in range(2)]
        sq = sb("sq", [P, 2, T])
        rb = sb("rb", [P, T])
        rt = sb("rt", [P, 3])
        cst = sb("cst", [P, C_W])
        vec = sb("vec", [P, V_W])
        ones = sb("ones", [P, P])
        eps = sb("eps", [P, 1])
        ff_hi = sb("ff_hi", [P, SMALL + P - 8], F32R)
        ff_lo = sb("ff_lo", [P, SMALL + P - 8], F32R)
        ident_r = ff_hi[:, 0:P]
        lam4 = sb("lam4", [P, 4])
        nlam = sb("nlam", [P, LAYERS])
        subg = sb("subg", [P, LAYERS])
        with ExitStack() as att:
            qk = [sb(f"qk{i}", [P, 8, T], scope=att) for i in range(2)]
            v = sb("v", [P, 3, D], scope=att)
            gate = sb("gate", [P, 16, T], scope=att)
            score = sb("score", [P, 2, 432], scope=att)
            aT = sb("aT", [P, 2, 656], scope=att)
            o_raw = sb("o_raw", [P, T], scope=att)
            mx = sb("mx", [P, 6], scope=att)
            nmx = sb("nmx", [P, 2, 6], scope=att)
            sm = sb("sm", [P, 2, 6], scope=att)
            rs = sb("rs", [P, 6], scope=att)
            aT_row = aT[:, :, :].rearrange("p a b -> p (a b)")
            fz = aT_row[0:8, 0:3 * T].rearrange("p (a b) -> p a b", a=3)
            rope_t = aT_row[:, 3 * T:4 * T]
            cneg = gate[0:8, 15, :]
            lam_raw = score[:, :, :].rearrange("p a b -> p (a b)")[:, 0:512]
            o_sq = sq[:, 0, :]
            o_rs = sq[:, 1, :]
        with ExitStack() as ffn:
            ffh_hi = sb("ffh_hi", [P, FT, T], F32R, scope=ffn)
            ffh_lo = sb("ffh_lo", [P, FT, T], F32R, scope=ffn)
            gbuf = sb("gbuf", [P, 2, T], scope=ffn)
            ubuf = sb("ubuf", [P, 2, T], scope=ffn)
        with ExitStack() as moe:
            xt_hi = sb("xt_hi", [P, 2, D], F32R, scope=moe)
            xt_lo = sb("xt_lo", [P, 2, D], F32R, scope=moe)
            xg_hi = sb("xg_hi", [P, D], F32R, scope=moe)
            xg_lo = sb("xg_lo", [P, D], F32R, scope=moe)
            sg = sb("sg", [P, 512], scope=moe)
            hb = sb("hb", [P, 512], scope=moe)
            hT_hi = sb("hT_hi", [P, 512], F32R, scope=moe)
            hT_lo = sb("hT_lo", [P, 512], F32R, scope=moe)
            y_hi = sb("y_hi", [P, D], F32R, scope=moe)
            y_lo = sb("y_lo", [P, D], F32R, scope=moe)
            pick = sb("pick", [P, 2, P], F32R, scope=moe)
            pickw = sb("pickw", [P, 2, P], scope=moe)
            put_hi = sb("put_hi", [P, 2 * P], F32R, scope=moe)
            put_lo = sb("put_lo", [P, 2 * P], F32R, scope=moe)
            lg = sb("lg", [P, 2, NE], scope=moe)
            eq = sb("eq", [P, 2, NE], scope=moe)
            sel1 = sb("sel1", [P, 2, NE], scope=moe)
            sel2 = sb("sel2", [P, 2, NE], scope=moe)
            mask = sb("mask", [P, 2, NE], scope=moe)
            comb = sb("comb", [P, 2, NE + 1], scope=moe)
            pos = sb("pos", [P, 2, NE + 1], scope=moe)
            top = sb("top", [P, 8, 2], scope=moe)
            cnt = sb("cnt", [P, 3, NE], scope=moe)
            tab_f = sb("tab_f", [P, 4], scope=moe)
            tab = sb("tab", [P, 4], I32, scope=moe)
            outb = sb("outb", [P, KD, SEQ], scope=moe)
            lgT = pickw[0:NE, :, :]

        PJ = [bank("pj0"), bank("pj1")]
        SB = [bank("s0"), bank("s1")]
        TP = [bank("tp0"), bank("tp1"), bank("tp2")]
        OB = bank("ob")
        LOGIT = PJ[(LAYERS * MIX_TILES + FFN_TILES) % 2]
        SPREAD = (OB, SB[0], SB[1], PJ[0])

        vec_in = sem("vec_in")
        tables_in = sem("tables_in")
        x_in = sem("x_in")
        pool_set = sem("pool_set")
        small_hi = sem("small_hi")
        small_lo = sem("small_lo")
        lam_sum = sem("lam_sum")
        lam_exp = sem("lam_exp")
        landed = [sem(f"landed{i}") for i in range(NRAW)]
        hi_done = sem("hi_done")
        lo_done = sem("lo_done")
        half_used = sem("half_used")
        x_hi_done = sem("x_hi_done")
        x_lo_done = sem("x_lo_done")
        sq_ready = sem("sq_ready")
        stat_done = sem("stat_done")
        rstd_ready = sem("rstd_ready")
        rt_psum = sem("rt_psum")
        rt_ready = sem("rt_ready")
        strip_done = sem("strip_done")
        proj_free = sem("proj_free")
        rot_done = sem("rot_done")
        rope_done = sem("rope_done")
        fz_ready = sem("fz_ready")
        fz_act = sem("fz_act")
        cneg_ready = sem("cneg_ready")
        gate_e = sem("gate_e")
        merged = sem("merged")
        s_done = sem("s_done")
        s_free = sem("s_free")
        nmx_ready = sem("nmx_ready")
        exp_done = sem("exp_done")
        a_ready = sem("a_ready")
        tr_done = sem("tr_done")
        aT_ready = sem("aT_ready")
        pv_done = sem("pv_done")
        o_free = sem("o_free")
        o_sq_ready = sem("o_sq_ready")
        o_stat = sem("o_stat")
        o_rs_ready = sem("o_rs_ready")
        o_norm = sem("o_norm")
        o_hi = sem("o_hi")
        o_lo = sem("o_lo")
        silu_f = sem("silu_f")
        ffh = sem("ffh")
        ffh_hi_done = sem("ffh_hi_done")
        ffh_lo_done = sem("ffh_lo_done")
        logit_done = sem("logit_done")
        lgT_ready = sem("lgT_ready")
        logit_turned = sem("logit_turned")
        xt_psum = sem("xt_psum")
        xt_hi_done = sem("xt_hi_done")
        xt_lo_done = sem("xt_lo_done")
        ident_done = sem("ident_done")
        top_diff = sem("top_diff")
        top_exp = sem("top_exp")
        mask_ready = sem("mask_ready")
        rank_done = sem("rank_done")
        table_ready = sem("table_ready")
        silu_done = sem("silu_done")
        hm_done = sem("hm_done")
        hT_psum = sem("hT_psum")
        hT_hi_done = sem("hT_hi_done")
        hT_lo_done = sem("hT_lo_done")
        y_hi_done = sem("y_hi_done")
        y_lo_done = sem("y_lo_done")
        pick_ready = sem("pick_ready")
        xg_psum = sem("xg_psum")
        xg_hi_done = sem("xg_hi_done")
        xg_lo_done = sem("xg_lo_done")
        put_psum = sem("put_psum")
        put_hi_done = sem("put_hi_done")
        put_lo_done = sem("put_lo_done")
        sc_psum = sem("sc_psum")
        sc_add = sem("sc_add")
        h_final = sem("h_final")
        fin_sq_act = sem("fin_sq_act")
        fin_sq_dve = sem("fin_sq_dve")
        out_ready = sem("out_ready")
        out_done = sem("out_done")
        dve_chain = sem("dve_chain")
        act_chain = sem("act_chain")

        def k_major(ap):
            return ap.rearrange("(k p) n -> p k n", p=P)

        def dense_source(l, j):
            if j < 12:
                c = (0, 512, 1536, 2048, 1024, 2560)[j // 2] + 256 * (j % 2)
                return k_major(w_in[l, :, c:c + 256])
            if j < 20:
                c = GATE_COL + 256 * (j - 12)
                return k_major(w_in[l, :, c:c + 256])
            if j < 24:
                w = w_bd if j < 22 else w_bf
                c = 512 * (j % 2)
                return k_major(w[l, :, c:c + 512])
            if j < MIX_PIECES:
                c = 256 * (j - 24)
                return k_major(w_out[l, :, c:c + 256])
            dp, part = divmod(j - MIX_PIECES - 2 * FFN_BLOCKS, 3)
            k0, nk = DOWN_K[part]
            return k_major(f_d[0, P * k0:P * (k0 + nk), 256 * dp:256 * dp + 256])

        def half_views(j, half):
            slot = raw[:, j % NRAW, :]
            l, i = divmod(j, LAYER1)
            if j >= MOE0 or 8 <= i < 12:
                k, c = 4, 256
                return slot[:, HCOLS * half:HCOLS * half + HCOLS].rearrange("p (k c) -> p k c", k=k), k, c
            k, width = (4, 512) if 20 <= i < 24 else (KD, 256)
            if i >= MIX_PIECES + 2 * FFN_BLOCKS:
                k = DOWN_K[(i - MIX_PIECES - 2 * FFN_BLOCKS) % 3][1]
            c = width // 2
            whole = slot[:, 0:k * width].rearrange("p (k c) -> p k c", k=k)
            return whole[:, :, c * half:c * half + c], k, c

        def ring(parts, i, k, c):
            return parts[:, i % NHALF, 0:k * c].rearrange("p (k c) -> p k c", k=k)

        def hidden(f, m):
            return bass.ds(m * (2 * FFN_UNROLL) + f, 1)

        def job_order():
            order = [("g", 0, 0), ("g", 0, 1), ("u", 0, 0), ("u", 0, 1)]
            for n in range(1, UNITS):
                order += [("g", n, 0), ("g", n, 1), ("u", n, 0), ("u", n, 1), ("d", n - 1, 0), ("d", n - 1, 1)]
            return order + [("d", UNITS - 1, 0), ("d", UNITS - 1, 1)]

        def expert_source(e, kind, n, half):
            if kind == "d":
                r = 512 * n + 256 * half
                return k_major(m_d[0, e, r:r + 256, :])
            w = m_g if kind == "g" else m_u
            return k_major(w[0, e, 512 * half:512 * half + 512, 512 * n:512 * n + 512])

        def uses(j, turn):
            return j // NRAW + 1 + turn * (JOB // NRAW)

        block = ctx.enter_context(nc.Block())

        @block.sync
        def _(sp):
            for c in (0, 4):
                sp.dma_start(h[:, c:c + 4, :], xT[:, c:c + 4, :]).then_inc(x_in, 16)

            def load(j, source, turn=0, per=HJOB):
                s = j % NRAW
                if j >= NRAW:
                    sp.wait_ge(lo_done, turn * per + 2 * (j - NRAW + 1))
                n = source.shape[1] * source.shape[2]
                sp.dma_start(raw[:, s, 0:n].rearrange("p (k c) -> p k c", k=source.shape[1]),
                             source).then_inc(landed[s], 16)

            def ffn_block(b, m=0):
                for i, w in enumerate((f_g, f_u)):
                    load(MIX_PIECES + 2 * b + i, k_major(w[0, :, bass.ds(m * (256 * FFN_UNROLL) + 256 * b, 256)]), m,
                         FFN_STEP)

            for j in range(MIX_PIECES):
                load(j, dense_source(0, j))
            ffn_block(0)
            with sp.Fori(0, FFN_TURNS) as m:
                for b in range(1, 1 + FFN_UNROLL):
                    ffn_block(b, m)
            ffn_block(FFN_BLOCKS - 1)
            for j in range(MIX_PIECES + 2 * FFN_BLOCKS, LAYER1):
                load(j, dense_source(0, j))
            for j in range(MIX_PIECES):
                load(LAYER1 + j, dense_source(1, j))
            with sp.Fori(0, NE) as e:
                for q, (kind, n, half) in enumerate(job_order()):
                    load(MOE0 + q, expert_source(e, kind, n, half), e)
            for q in range(EMPTY):
                load(MOE0 + NE * JOB + q, consts[:, 0:16].rearrange("p (a b) -> p a b", a=1))
            sp.wait_ge(table_ready, 1)
            over = sp.value_load(tab[0:1, 3:4], min_val=0, max_val=MAX_OVER)
            with sp.Fori(0, MAX_OVER) as o:
                with sp.If(o < over):
                    e = sp.value_load(tab[0:1, bass.ds(o, 1)], min_val=0, max_val=NE - 1)
                    for q, (kind, n, half) in enumerate(job_order()):
                        load(OVER0 + q, expert_source(e, kind, n, half), o)
            for c in range(0, KD, 2):
                sp.wait_ge(out_ready, c + 2)
                sp.dma_start(outT[:, c:c + 2, :], outb[:, c:c + 2, :]).then_inc(out_done, 16)
            sp.wait_ge(out_done, 16 * KD // 2)

        @block.gpsimd
        def _(pool):
            pool.memset(ones[:, :], 1.0).then_inc(pool_set, 1)
            pool.memset(eps[:, :], EPS).then_inc(pool_set, 1)
            pool.memset(ff_hi[:, :].bitcast(F32), 0.0).then_inc(pool_set, 1)
            pool.memset(ff_lo[:, :].bitcast(F32), 0.0).then_inc(pool_set, 1)

        @block.scalar
        def _(act):
            link = Chain(act, act_chain)

            def split(i, turn=0, skipped=0, m=0):
                j, half = divmod(i, 2)
                act.wait_ge(landed[j % NRAW], m * (FFN_STEP // (2 * NRAW) * 16) + uses(j, turn) * 16)
                if NHALF <= i < 2 * MOE0 + NHALF:
                    act.wait_ge(strip_done, m * FFN_STEP + strips_to_half(i - NHALF))
                elif i >= NHALF:
                    act.wait_ge(half_used, turn * HJOB + (i - NHALF + 1 - skipped - 2 * MOE0))
                src, k, c = half_views(j, half)
                act.activation(ring(w_hi, i, k, c), src, ACT.Copy).then_inc(hi_done, 1)

            def after(l, j, half, m=0):
                split(2 * (l * LAYER1 + j) + half + HI_AHEAD, m=m)

            def x_part(n, c, gain):
                act.activation(x_hi[n % 2][:, c, :], h[:, c, :], ACT.Copy, scale=gain).then_inc(x_hi_done, 1)
                square(n, c)

            def square(n, c):
                i = 8 * n + c
                if i >= 2:
                    act.wait_ge(stat_done, i - 1)
                act.activation(sq[:, c % 2, :], h[:, c, :], ACT.Square).then_inc(sq_ready, 1)

            def rstd(n):
                act.wait_ge(stat_done, 8 * n + 8)
                link(act.activation(rb[:, :], OB[:, 0:T], ACT.Ln, bias=eps[:, 0:1], scale=1.0 / D))
                act.activation(rb[:, :], rb[:, :], ACT.Exp, scale=-0.5).then_inc(rstd_ready, 1)

            act.dma_start(vec[:, :], vecs).then_inc(vec_in, 16)
            act.wait_ge(vec_in, 16)
            act.wait_ge(pool_set, 4)
            act.activation(ff_hi[:, 0:SMALL], vec[:, V_FF:V_FF + SMALL], ACT.Copy).then_inc(small_hi, 1)
            for c in range(KD):
                if c % 4 == 0:
                    act.wait_ge(x_in, 32)
                x_part(0, c, vec[:, V_GMIX + c:V_GMIX + c + 1])
            act.dma_start(cst[:, :], consts).then_inc(tables_in, 16)
            act.dma_start(lam_raw, lam).then_inc(tables_in, 16)
            rstd(0)
            for i in range(HI_AHEAD):
                split(i)

            def attention_exp(l, u):
                un = 8 * l + u
                act.wait_ge(nmx_ready, un + 1)
                for m in range(2):
                    for i, (c0, w) in enumerate(SEG):
                        k = 3 * m + i
                        ins = act.activation(score[:, m, c0:c0 + w], score[:, m, c0:c0 + w], ACT.Exp,
                                             bias=nmx[:, u % 2, k:k + 1], accum_out=sm[:, u % 2, k:k + 1])
                ins.then_inc(exp_done, 1)

            def evacuate_aT(l, u):
                un = 8 * l + u
                act.wait_ge(tr_done, un + 1)
                if un:
                    act.wait_ge(pv_done, un)
                heads = 1 if u < 4 else 2
                for m in range(heads):
                    act.activation(aT[:, m, 0:384], TP[m][:, 0:384], ACT.Copy)
                    act.activation(aT[0:16, m, 384:400], TP[m][0:16, 384:400], ACT.Copy)
                act.activation(aT[0:16, 0:heads, 400:656],
                               TP[2][0:16, 0:256 * heads].rearrange("p (m c) -> p m c", m=heads),
                               ACT.Copy).then_inc(aT_ready, 1)

            def o_square(l, u):
                act.wait_ge(o_free, 4 * l + u + 1)
                act.activation(o_sq, o_raw[:, :], ACT.Square).then_inc(o_sq_ready, 1)

            def o_rstd(l, u):
                act.wait_ge(o_stat, 4 * l + u + 1)
                link(act.activation(o_rs, OB[:, 0:T], ACT.Ln, bias=eps[:, 0:1], scale=1.0 / P))
                act.activation(o_rs, o_rs, ACT.Exp, scale=-0.5).then_inc(o_rs_ready, 1)

            def o_part(l, u):
                if u < 4:
                    act.wait_ge(o_norm, 4 * l + u + 1)
                    source = o_raw[:, :]
                else:
                    act.wait_ge(pv_done, 8 * l + u + 1)
                    source = OB[:, 0:T]
                act.activation(x_hi[1][:, u, :], source, ACT.Copy).then_inc(o_hi, 1)

            for l in range(LAYERS):
                proj0 = l * (MIX_TILES + FFN_TILES)
                for j in range(12):
                    for half in range(2):
                        after(l, j, half)
                    if j == 1:
                        act.wait_ge(fz_ready, l + 1)
                        link(act.activation(fz[:, 1, :], fz[:, 0, :], ACT.Abs))
                        link(act.activation(fz[:, 1, :], fz[:, 1, :], ACT.Exp, scale=-1.0))
                        act.activation(fz[:, 1, :], fz[:, 1, :], ACT.Ln, bias=1.0).then_inc(fz_act, 1)
                    if l == LAYERS - 1 and j == 9:
                        act.activation(ident_r, cst[:, C_ID:C_ID + P], ACT.Copy).then_inc(ident_done, 1)
                    if l == 0 and j == 9:
                        act.wait_ge(lam_sum, 4)
                        act.activation(lam4[:, :], lam4[:, :], ACT.Exp).then_inc(lam_exp, 1)
                for u in range(8):
                    attention_exp(l, u)
                    after(l, 12 + u, 0)
                    if 1 <= u <= 4:
                        o_square(l, u - 1)
                    elif u > 4:
                        o_part(l, u - 1)
                    after(l, 12 + u, 1)
                    if 1 <= u <= 4:
                        o_rstd(l, u - 1)
                    evacuate_aT(l, u)
                    if 1 <= u <= 4:
                        o_part(l, u - 1)
                for q in range(4):
                    act.wait_ge(proj_free, proj0 + GATE_TILE + 4 * q + 4)
                    act.activation(gate[:, 4 * q:4 * q + 4, :], gate[:, 4 * q:4 * q + 4, :], ACT.Sigmoid)\
                        .then_inc(gate_e, 1)
                    after(l, 20 + q // 2, q % 2)
                    if q == 0:
                        o_part(l, 7)
                for j in range(22, 24):
                    for half in range(2):
                        for c in range(4 * (j - 22) + 2 * half, 4 * (j - 22) + 2 * half + 2):
                            act.wait_ge(merged, 8 * l + c + 1)
                            act.activation(x_hi[0][:, c, :], gate[:, 8 + c, :], ACT.Copy).then_inc(x_hi_done, 1)
                        after(l, j, half)
                n = 2 * l + 1
                for c in range(KD):
                    act.wait_ge(proj_free, proj0 + OUT_TILE + c + 1)
                    x_part(n, c, vec[:, V_GFFN + 8 * l + c:V_GFFN + 8 * l + c + 1])
                    if c < KD - 1:
                        after(l, 24 + c // 2, c % 2)
                rstd(n)
                after(l, 27, 1)
                if l == 0:
                    def ffn_block(b, m=0):
                        for i in range(2):
                            act.wait_ge(proj_free, m * FFN_STEP + (MIX_TILES + 4 * b + i + 1))
                            act.activation(gbuf[:, i, :], gbuf[:, i, :], ACT.Silu).then_inc(silu_f, 1)
                            after(0, MIX_PIECES + 2 * b, i, m)
                        for i in range(2):
                            act.wait_ge(ffh, m * (2 * FFN_UNROLL) + (2 * b + i + 1))
                            act.activation(ffh_hi[:, hidden(2 * b + i, m), :], ubuf[:, i:i + 1, :], ACT.Copy)\
                                .then_inc(ffh_hi_done, 1)
                            after(0, MIX_PIECES + 2 * b + 1, i, m)

                    ffn_block(0)
                    with act.Fori(0, FFN_TURNS) as m:
                        for b in range(1, 1 + FFN_UNROLL):
                            ffn_block(b, m)
                    ffn_block(FFN_BLOCKS - 1)
                    for dp in range(4):
                        for part in range(3):
                            for i in range(2):
                                c = 2 * dp + i
                                if part == 2:
                                    act.wait_ge(proj_free, DOWN_TILE + c + 1)
                                    x_part(2, c, vec[:, V_GMIX + 8 + c:V_GMIX + 8 + c + 1])
                                if c < KD - 1 or part < 2:
                                    after(0, MIX_PIECES + 2 * FFN_BLOCKS + 3 * dp + part, i)
                    rstd(2)
                    after(0, MIX_PIECES + FFN_PIECES - 1, 1)

            act.wait_ge(rt_ready, 3)
            for i in range(4):
                half, tt = divmod(i, 2)
                act.wait_ge(xt_psum, i + 1)
                act.activation(xt_hi[:, tt, 512 * half:512 * half + 512], xt_bank(SB, TP, i)[:, :], ACT.Copy,
                               scale=rt[:, tt + 1:tt + 2]).then_inc(xt_hi_done, 1)
            act.wait_ge(top_diff, 1)
            act.activation(top[:, 4, :], top[:, 3, :], ACT.Exp).then_inc(top_exp, 1)

            def xg_part(g):
                act.wait_ge(xg_psum, g + 1)
                act.activation(xg_hi[:, 0:512], SB[0][:, :], ACT.Copy)
                act.activation(xg_hi[:, 512:1024], SB[1][:, :], ACT.Copy).then_inc(xg_hi_done, 1)

            def put_part(s):
                act.wait_ge(put_psum, s + 1)
                act.activation(put_hi[:, :], OB[:, 0:2 * P], ACT.Copy).then_inc(put_hi_done, 1)

            def job(J, j0, turn, skipped, main):
                q = 0

                def used(count=1):
                    nonlocal q
                    for _ in range(count):
                        if main or q + HI_AHEAD < HJOB:
                            split(2 * j0 + q + HI_AHEAD, turn, skipped)
                        q += 1

                def hT_part(n):
                    act.wait_ge(hT_psum, J * UNITS + (n + 1))
                    act.activation(hT_hi[:, :], TP[0][:, :], ACT.Copy).then_inc(hT_hi_done, 1)

                if not main:
                    act.wait_ge(lo_done, turn * HJOB + 2 * j0)
                    for i in range(HI_AHEAD):
                        split(2 * j0 + i, turn, skipped)
                    xg_part(J + 1)
                    put_part(J)
                for n in range(UNITS):
                    used(2)
                    if n:
                        hT_part(n - 1)
                    used()
                    if n == 2 and main:
                        put_part(J)
                    act.wait_ge(half_used, J * HJOB + 2 * (6 * n if n else 2))
                    act.wait_ge(hm_done, J * UNITS + (n + 1))
                    act.activation(sg[:, :], (PJ if n % 2 == 0 else SB)[0][:, :], ACT.Silu).then_inc(silu_done, 1)
                    used()
                    used(4)
                    if 0 < n < UNITS - 1:
                        used(4)
                used(3)
                act.wait_ge(half_used, J * HJOB + (HJOB - 4))
                hT_part(UNITS - 1)
                used()
                if main:
                    xg_part(J + 1)
                used(3)
                act.wait_ge(half_used, J * HJOB + HJOB)
                act.activation(y_hi[:, 0:512], TP[1][:, :], ACT.Copy)
                act.activation(y_hi[:, 512:1024], TP[2][:, :], ACT.Copy).then_inc(y_hi_done, 1)
                used()

            act.nop().then_inc(silu_done, 1)
            xg_part(0)
            with act.Fori(0, NE) as e:
                job(e, MOE0, e, 0, True)
            act.wait_ge(table_ready, 1)
            over = act.value_load(tab[0:1, 3:4], min_val=0, max_val=MAX_OVER)
            with act.Fori(0, MAX_OVER) as o:
                with act.If(o < over):
                    job(o + NE, OVER0, o, 2 * EMPTY, False)
            act.wait_ge(h_final, 1)
            act.activation(outb[:, 0:4, :], h[:, 0:4, NMETA:T], ACT.Square).then_inc(fin_sq_act, 1)
            act.wait_ge(stat_done, 33)
            link(act.activation(rb[:, NMETA:T], OB[:, 0:SEQ], ACT.Ln, bias=eps[:, 0:1], scale=1.0 / D))
            act.activation(rb[:, NMETA:T], rb[:, NMETA:T], ACT.Exp, scale=-0.5).then_inc(rstd_ready, 1)

        @block.vector
        def _(dve):
            link = Chain(dve, dve_chain)

            def split(i, turn=0, per=HJOB):
                dve.wait_ge(hi_done, turn * per + (i + 1))
                src, k, c = half_views(i // 2, i % 2)
                dve.tensor_tensor(ring(w_lo, i, k, c), src, ring(w_hi, i, k, c).bitcast(F32),
                                  ALU.subtract).then_inc(lo_done, 1)

            def after(l, j, half, m=0):
                split(2 * (l * LAYER1 + j) + half + LO_AHEAD, m, FFN_STEP)

            def x_part(n, c, gain):
                dve.wait_ge(x_hi_done, counts_before(n) + c + 1)
                dve.scalar_tensor_tensor(x_lo[n % 2][:, c, :], h[:, c, :], gain, x_hi[n % 2][:, c, :].bitcast(F32),
                                         ALU.mult, ALU.subtract).then_inc(x_lo_done, 1)

            dve.wait_ge(small_hi, 1)
            dve.tensor_tensor(ff_lo[:, 0:SMALL], vec[:, V_FF:V_FF + SMALL], ff_hi[:, 0:SMALL].bitcast(F32),
                              ALU.subtract).then_inc(small_lo, 1)
            for c in range(KD):
                x_part(0, c, vec[:, V_GMIX + c:V_GMIX + c + 1])
            for i in range(2):
                split(i)

            def attention_max(l, u):
                un = 8 * l + u
                if un:
                    dve.wait_ge(tr_done, un)
                for m in range(2):
                    dve.wait_ge(s_done, 2 * un + m + 1)
                    for i, (c0, w) in enumerate(SEG):
                        k = 3 * m + i
                        ins = dve.tensor_tensor_reduce(
                            out=score[:, m, c0:c0 + w], in0=SB[m][:, c0:c0 + w],
                            in1=cst[:, C_MASK + c0:C_MASK + c0 + w], scale=SCALE, scalar=-3e38,
                            op0=ALU.add, op1=ALU.max, accum_out=mx[:, k:k + 1])
                    ins.then_inc(s_free, 1)
                dve.wait_ge(s_free, 2 * un + 2)
                dve.tensor_scalar(nmx[:, u % 2, :], mx[:, :], -1.0, None, ALU.mult).then_inc(nmx_ready, 1)
                dve.wait_ge(nmx_ready, un + 1)

            def attention_normalise(l, u):
                un = 8 * l + u
                dve.wait_ge(exp_done, un + 1)
                link(dve.reciprocal(rs[:, :], sm[:, u % 2, :]))
                if u < 4:
                    link(dve.tensor_scalar(rs[:, 3:6], rs[:, 3:6], nlam[:, l:l + 1], None, ALU.mult))
                    for i, (c0, w) in enumerate(SEG):
                        a = score[:, 0, c0:c0 + w]
                        ins = dve.tensor_scalar(a, a, rs[:, i:i + 1], None, ALU.mult)
                    link(ins)
                    for i, (c0, w) in enumerate(SEG):
                        a = score[:, 0, c0:c0 + w]
                        ins = dve.scalar_tensor_tensor(a, score[:, 1, c0:c0 + w], rs[:, 3 + i:4 + i], a,
                                                       ALU.mult, ALU.add)
                else:
                    for m in range(2):
                        for i, (c0, w) in enumerate(SEG):
                            a = score[:, m, c0:c0 + w]
                            ins = dve.tensor_scalar(a, a, rs[:, 3 * m + i:3 * m + i + 1], None, ALU.mult)
                ins.then_inc(a_ready, 1)
                dve.wait_ge(a_ready, un + 1)

            def free(t):
                dve.wait_ge(proj_free, t + 1)

            def rope(l, i):
                dve.wait_ge(rot_done, 8 * l + i + 1)
                link(dve.tensor_tensor(rope_t, TP[1 + i % 2][:, 0:T], cst[:, C_SIN:C_SIN + T], ALU.mult))
                link(dve.tensor_tensor(qk[0][:, i, :], qk[0][:, i, :], cst[:, C_COS:C_COS + T], ALU.mult))
                dve.tensor_tensor(qk[0][:, i, :], qk[0][:, i, :], rope_t, ALU.add).then_inc(rope_done, 1)
                dve.wait_ge(rope_done, 8 * l + i + 1)

            def o_evacuate(l, u):
                un = 8 * l + u
                if u < 4:
                    dve.wait_ge(pv_done, un + 1)
                    dve.tensor_copy(o_raw[:, :], OB[:, 0:T]).then_inc(o_free, 1)
                    dve.wait_ge(o_free, 4 * l + u + 1)
                else:
                    dve.wait_ge(o_hi, un + 1)
                    dve.tensor_tensor(x_lo[1][:, u, :], OB[:, 0:T], x_hi[1][:, u, :].bitcast(F32),
                                      ALU.subtract).then_inc(o_lo, 1)

            def o_normalise(l, u):
                dve.wait_ge(o_rs_ready, 4 * l + u + 1)
                dve.scalar_tensor_tensor(o_raw[:, :], o_raw[:, :], subg[:, l:l + 1], o_rs, ALU.mult,
                                         ALU.mult).then_inc(o_norm, 1)
                dve.wait_ge(o_norm, 4 * l + u + 1)

            def o_part(l, u):
                dve.wait_ge(o_hi, 8 * l + u + 1)
                dve.tensor_tensor(x_lo[1][:, u, :], o_raw[:, :], x_hi[1][:, u, :].bitcast(F32),
                                  ALU.subtract).then_inc(o_lo, 1)
                dve.wait_ge(o_lo, 8 * l + u + 1)

            shift = place = 0

            def merged_part(l, c):
                dve.wait_ge(x_hi_done, counts_before(2 * l + 1) - 8 + c + 1)
                dve.tensor_tensor(x_lo[0][:, c, :], gate[:, 8 + c, :], x_hi[0][:, c, :].bitcast(F32),
                                  ALU.subtract).then_inc(x_lo_done, 1)

            for l in range(LAYERS):
                t0 = l * (MIX_TILES + FFN_TILES)
                dve.wait_ge(rstd_ready, 2 * l + 1)
                dve.wait_ge(strip_done, strips_to_tile(t0))
                dve.tensor_tensor(fz[:, 0, :], PJ[t0 % 2][0:8, 0:T], rb[0:8, :], ALU.mult).then_inc(proj_free, 1)
                free(t0)
                dve.tensor_scalar(fz[:, 0, :], fz[:, 0, :], vec[0:8, V_BF + l:V_BF + l + 1], None,
                                  ALU.add).then_inc(fz_ready, 1)
                dve.wait_ge(fz_ready, l + 1)
                if l == 0:
                    for i in range(2, LO_AHEAD):
                        split(i)
                for j in range(8):
                    for i in range(2):
                        t = t0 + 1 + 2 * j + i
                        dve.wait_ge(strip_done, strips_to_tile(t))
                        dve.tensor_tensor(qk[j // 4][:, (2 * j + i) % 8, :], PJ[t % 2][:, 0:T], rb[:, :],
                                          ALU.mult).then_inc(proj_free, 1)
                        after(l, j, i)
                    free(t)
                    if 1 <= j <= 4:
                        rope(l, 2 * j - 2)
                        rope(l, 2 * j - 1)
                    if j == 0:
                        dve.wait_ge(rt_psum, l + 1)
                        dve.tensor_copy(rt[:, :], TP[0][:, 0:6].rearrange("p (a b) -> p a b", b=2)[:, :, 0])\
                            .then_inc(rt_ready, 1)
                    if j == 6:
                        dve.wait_ge(fz_act, l + 1)
                        link(dve.tensor_scalar(fz[:, 0, :], fz[:, 0, :], 0.0, None, ALU.min))
                        link(dve.tensor_tensor(fz[:, 2, :], fz[:, 0, :], fz[:, 1, :], ALU.subtract))
                        shift, place = 1, 2

                        def log_f_steps(count):
                            nonlocal shift, place
                            for _ in range(count):
                                a, b = place, 3 - place
                                dve.tensor_copy(fz[:, b, 0:shift], fz[:, a, 0:shift])
                                link(dve.tensor_tensor(fz[:, b, shift:T], fz[:, a, shift:T], fz[:, a, 0:T - shift],
                                                       ALU.add))
                                shift, place = 2 * shift, b

                dve.wait_ge(rt_ready, l + 1)
                for j in range(8, 12):
                    if j > 8:
                        log_f_steps(3)
                    if l == 0 and j == 8:
                        dve.wait_ge(tables_in, 32)
                        for k in range(4):
                            dve.tensor_tensor_reduce(out=o_raw[:, 64 * k:64 * k + 64], in0=lam_raw[:, 128 * k:128 * k + 64],
                                                     in1=lam_raw[:, 128 * k + 64:128 * k + 128], scale=1.0, scalar=0.0,
                                                     op0=ALU.mult, op1=ALU.add, accum_out=lam4[:, k:k + 1]).then_inc(lam_sum, 1)
                    if l == 0 and j == 11:
                        dve.wait_ge(lam_exp, 1)
                        for m in range(LAYERS):
                            link(dve.tensor_tensor(nlam[:, m:m + 1], lam4[:, 2 * m + 1:2 * m + 2], lam4[:, 2 * m:2 * m + 1],
                                                   ALU.subtract))
                            link(dve.tensor_scalar(nlam[:, m:m + 1], nlam[:, m:m + 1], -lam_init[m], None, ALU.add))
                            link(dve.tensor_scalar(subg[:, m:m + 1], vec[:, V_SUB + m:V_SUB + m + 1], 1.0 - lam_init[m], None,
                                                   ALU.mult))
                    for w in range(3):
                        t = t0 + V_TILE + 3 * (j - 8) + w
                        dve.wait_ge(strip_done, strips_to_tile(t))
                        dve.tensor_scalar(v[:, w, 256 * (j - 8):256 * (j - 8) + 256], PJ[t % 2][:, 0:256],
                                          rt[:, w:w + 1], None, ALU.mult).then_inc(proj_free, 1)
                        if w != 1:
                            after(l, j, w // 2)
                    free(t)
                assert shift >= T
                dve.tensor_scalar(cneg, fz[:, place, :], -1.0 / SCALE, None, ALU.mult).then_inc(cneg_ready, 1)
                dve.wait_ge(cneg_ready, l + 1)
                for u in range(8):
                    attention_max(l, u)
                    if 2 <= u <= 5:
                        o_part(l, u - 2)
                    for i in range(2):
                        g = 2 * u + i
                        t = t0 + GATE_TILE + g
                        dve.wait_ge(strip_done, strips_to_tile(t))
                        dve.tensor_tensor(gate[:, g, :], PJ[t % 2][:, 0:T], rb[:, :], ALU.mult).then_inc(proj_free, 1)
                        if i == 0:
                            after(l, 12 + u, i)
                            attention_normalise(l, u)
                            if u:
                                o_evacuate(l, u - 1)
                        else:
                            after(l, 12 + u, i)
                            if 1 <= u <= 4:
                                o_normalise(l, u - 1)
                for j in range(20, 24):
                    for i in range(4):
                        c = 4 * (j % 2) + i
                        t = t0 + (BD_TILE if j < 22 else BF_TILE) + c
                        g = c if j < 22 else 8 + c
                        dve.wait_ge(gate_e, 4 * l + g // 4 + 1)
                        dve.wait_ge(strip_done, strips_to_tile(t))
                        dve.tensor_tensor(gate[:, g, :], PJ[t % 2][:, 0:T], gate[:, g, :], ALU.mult)\
                            .then_inc(proj_free, 1)
                        free(t)
                        if j >= 22:
                            dve.tensor_tensor(gate[:, g, :], gate[:, g, :], gate[:, c, :], ALU.add)\
                                .then_inc(merged, 1)
                            if c:
                                merged_part(l, c - 1)
                        if i % 2:
                            after(l, j, i // 2)
                        if j == 20 and i == 1:
                            o_evacuate(l, 7)
                merged_part(l, KD - 1)
                n = 2 * l + 1
                for c in range(KD):
                    t = t0 + OUT_TILE + c
                    dve.wait_ge(strip_done, strips_to_tile(t))
                    dve.tensor_tensor(h[:, c, :], PJ[t % 2][:, 0:T], h[:, c, :], ALU.add).then_inc(proj_free, 1)
                    free(t)
                    if c == KD - 1:
                        x_part(n, c, vec[:, V_GFFN + 8 * l + c:V_GFFN + 8 * l + c + 1])
                    after(l, 24 + c // 2, c % 2)
                    if c < KD - 1:
                        x_part(n, c, vec[:, V_GFFN + 8 * l + c:V_GFFN + 8 * l + c + 1])
                if l == 0:
                    f0 = MIX_TILES

                    def ffh_part(f, m=0):
                        dve.wait_ge(ffh_hi_done, m * (2 * FFN_UNROLL) + (f + 1))
                        dve.tensor_tensor(ffh_lo[:, hidden(f, m), :], ubuf[:, f % 2:f % 2 + 1, :],
                                          ffh_hi[:, hidden(f, m), :].bitcast(F32), ALU.subtract)\
                            .then_inc(ffh_lo_done, 1)

                    def ffn_block(b, m=0):
                        for i in range(2):
                            t = f0 + 4 * b + i
                            if b:
                                dve.wait_ge(ffh, m * (2 * FFN_UNROLL) + (2 * b - 1 + i))
                            dve.wait_ge(strip_done, m * FFN_STEP + strips_to_tile(t))
                            dve.tensor_tensor(gbuf[:, i, :], PJ[t % 2][:, 0:T], rb[:, :], ALU.mult)\
                                .then_inc(proj_free, 1)
                            if b and i == 0:
                                ffh_part(2 * b - 1, m)
                            after(0, MIX_PIECES + 2 * b, i, m)
                        for i in range(2):
                            t = f0 + 4 * b + 2 + i
                            if b:
                                dve.wait_ge(ffh_lo_done, m * (2 * FFN_UNROLL) + (2 * b - 1 + i))
                            dve.wait_ge(strip_done, m * FFN_STEP + strips_to_tile(t))
                            dve.tensor_tensor(ubuf[:, i, :], PJ[t % 2][:, 0:T], rb[:, :], ALU.mult)\
                                .then_inc(proj_free, 1)
                            dve.wait_ge(proj_free, m * FFN_STEP + (t + 1))
                            dve.wait_ge(silu_f, m * (2 * FFN_UNROLL) + (2 * b + i + 1))
                            dve.tensor_tensor(ubuf[:, i, :], ubuf[:, i, :], gbuf[:, i, :], ALU.mult)\
                                .then_inc(ffh, 1)
                            after(0, MIX_PIECES + 2 * b + 1, i, m)
                            if i == 0:
                                ffh_part(2 * b, m)

                    dve.wait_ge(rstd_ready, 2)
                    ffn_block(0)
                    with dve.Fori(0, FFN_TURNS) as m:
                        for b in range(1, 1 + FFN_UNROLL):
                            ffn_block(b, m)
                    ffn_block(FFN_BLOCKS - 1)
                    ffh_part(FT - 1)
                    for dp in range(4):
                        for part in range(3):
                            for i in range(2):
                                c = 2 * dp + i
                                t = f0 + 4 * FFN_BLOCKS + c
                                if part == 2:
                                    dve.wait_ge(strip_done, strips_to_tile(t))
                                    dve.tensor_tensor(h[:, c, :], PJ[t % 2][:, 0:T], h[:, c, :], ALU.add)\
                                        .then_inc(proj_free, 1)
                                    free(t)
                                if part == 2 and c == KD - 1:
                                    x_part(2, c, vec[:, V_GMIX + 8 + c:V_GMIX + 8 + c + 1])
                                after(0, MIX_PIECES + 2 * FFN_BLOCKS + 3 * dp + part, i)
                                if part == 2 and c < KD - 1:
                                    x_part(2, c, vec[:, V_GMIX + 8 + c:V_GMIX + 8 + c + 1])

            dve.memset(y_hi[:, :].bitcast(F32), 0.0)
            dve.memset(y_lo[:, :].bitcast(F32), 0.0)
            dve.memset(put_hi[:, :].bitcast(F32), 0.0)
            dve.memset(put_lo[:, :].bitcast(F32), 0.0)
            dve.memset(pos[:, :, NE:NE + 1], -1.0)
            link(dve.memset(comb[:, :, NE:NE + 1], 0.0))
            dve.wait_ge(logit_done, 1)
            dve.wait_ge(rstd_ready, 4)
            dve.tensor_tensor(lgT, LOGIT[0:NE, 0:SEQ].rearrange("p (a b) -> p a b", a=2),
                              rb[0:NE, NMETA:T].rearrange("p (a b) -> p a b", a=2), ALU.mult).then_inc(lgT_ready, 1)
            dve.wait_ge(rt_psum, 3)
            dve.tensor_copy(rt[:, :], TP[0][:, 0:6].rearrange("p (a b) -> p a b", b=2)[:, :, 0]).then_inc(rt_ready, 1)
            dve.wait_ge(rt_ready, 3)
            dve.wait_ge(logit_turned, 1)
            link(dve.tensor_copy(lg[:, :, :], OB[:, 0:2 * NE].rearrange("p (a b) -> p a b", a=2)))
            rev = cst[:, C_REV:C_REV + 16].rearrange("p (a b) -> p a b", a=2)

            def wide(ap):
                return ap.unsqueeze(2).broadcast_to([P, 2, NE])

            def first_max(sel, value):
                link(dve.tensor_reduce(value, lg[:, :, :], AX, ALU.max))
                link(dve.tensor_tensor(eq[:, :, :], lg[:, :, :], wide(value), ALU.is_equal))
                link(dve.tensor_tensor(eq[:, :, :], eq[:, :, :], rev, ALU.mult))
                link(dve.tensor_reduce(top[:, 2, :], eq[:, :, :], AX, ALU.max))
                link(dve.tensor_tensor(sel[:, :, :], eq[:, :, :], wide(top[:, 2, :]), ALU.is_equal))

            first_max(sel1, top[:, 0, :])
            link(dve.scalar_tensor_tensor(lg[:, :, :], sel1[:, :, :], -3e38, lg[:, :, :], ALU.mult, ALU.add))
            first_max(sel2, top[:, 1, :])
            link(dve.tensor_tensor(mask[:, :, :], sel1[:, :, :], sel2[:, :, :], ALU.add))
            dve.nop().then_inc(mask_ready, 1)
            link(dve.tensor_tensor(top[:, 3, :], top[:, 1, :], top[:, 0, :], ALU.subtract))
            dve.nop().then_inc(top_diff, 1)
            def xt_part(i):
                half, tt = divmod(i, 2)
                dve.wait_ge(xt_hi_done, i + 1)
                dve.scalar_tensor_tensor(xt_lo[:, tt, 512 * half:512 * half + 512], xt_bank(SB, TP, i)[:, :],
                                         rt[:, tt + 1:tt + 2],
                                         xt_hi[:, tt, 512 * half:512 * half + 512].bitcast(F32),
                                         ALU.mult, ALU.subtract).then_inc(xt_lo_done, 1)

            xt_part(0)
            xt_part(1)
            dve.wait_ge(rank_done, 1)
            link(dve.tensor_copy(cnt[:, :, :], OB[:, 32:56].rearrange("p (a b) -> p a b", a=3)))
            link(dve.scalar_tensor_tensor(pos[:, :, 0:NE], cnt[:, 0:2, :], 1.0, mask[:, :, :], ALU.add, ALU.mult))
            link(dve.tensor_scalar(pos[:, :, 0:NE], pos[:, :, 0:NE], -1.0, None, ALU.add))

            def build_pick(e, block):
                iota = cst[:, C_IOTA + P * block:C_IOTA + P * block + P]
                for tt in range(2):
                    where = pos[:, tt, bass.ds(e, 1)]
                    dve.tensor_scalar(pick[:, tt, :], iota, where, None, ALU.is_equal)
                    ins = dve.tensor_scalar(pickw[:, tt, :], iota, where, comb[:, tt, bass.ds(e, 1)], ALU.is_equal,
                                            ALU.mult)
                ins.then_inc(pick_ready, 1)

            for tt in range(2):
                ins = dve.tensor_scalar(pick[:, tt, :], cst[:, C_IOTA:C_IOTA + P], pos[:, tt, 0:1], None, ALU.is_equal)
            ins.then_inc(pick_ready, 1)
            xt_part(2)
            xt_part(3)
            dve.wait_ge(top_exp, 1)
            link(dve.tensor_scalar(top[:, 5, :], top[:, 4, :], 1.0, None, ALU.add))
            link(dve.reciprocal(top[:, 5, :], top[:, 5, :]))
            link(dve.tensor_tensor(top[:, 6, :], top[:, 4, :], top[:, 5, :], ALU.mult))
            link(dve.tensor_tensor(sel1[:, :, :], sel1[:, :, :], wide(top[:, 5, :]), ALU.mult))
            link(dve.tensor_tensor(sel2[:, :, :], sel2[:, :, :], wide(top[:, 6, :]), ALU.mult))
            link(dve.tensor_tensor(comb[:, :, 0:NE], sel1[:, :, :], sel2[:, :, :], ALU.add))
            for tt in range(2):
                ins = dve.tensor_scalar(pickw[:, tt, :], cst[:, C_IOTA:C_IOTA + P], pos[:, tt, 0:1],
                                        comb[:, tt, 0:1], ALU.is_equal, ALU.mult)
            link(ins)
            over_rev, found = cnt[0:1, 0, :], cnt[0:1, 1, 0:MAX_OVER]
            experts = tab_f[0:1, 0:MAX_OVER]
            link(dve.scalar_tensor_tensor(over_rev, cnt[0:1, 2, :], float(P), rev[0:1, 0, :], ALU.is_gt, ALU.mult))
            for o in range(MAX_OVER):
                link(dve.tensor_reduce(tab_f[0:1, o:o + 1], over_rev, AX, ALU.max))
                link(dve.scalar_tensor_tensor(over_rev, over_rev, tab_f[0:1, o:o + 1], over_rev, ALU.is_lt,
                                              ALU.mult))
            link(dve.tensor_scalar(found, experts, 0.0, None, ALU.is_gt))
            link(dve.tensor_reduce(tab_f[0:1, MAX_OVER:MAX_OVER + 1], found, AX, ALU.add))
            link(dve.tensor_scalar(experts, experts, -1.0, float(NE), ALU.mult, ALU.add))
            link(dve.tensor_scalar(experts, experts, float(NE - 1), None, ALU.min))
            dve.tensor_copy(tab[0:1, :], tab_f[0:1, :]).then_inc(table_ready, 1)
            dve.wait_ge(table_ready, 1)

            def xg_part(g):
                dve.wait_ge(xg_hi_done, g + 1)
                dve.tensor_tensor(xg_lo[:, 0:512], SB[0][:, :], xg_hi[:, 0:512].bitcast(F32), ALU.subtract)
                dve.tensor_tensor(xg_lo[:, 512:1024], SB[1][:, :], xg_hi[:, 512:1024].bitcast(F32),
                                  ALU.subtract).then_inc(xg_lo_done, 1)

            def put_part(s):
                dve.wait_ge(put_hi_done, s + 1)
                dve.tensor_tensor(put_lo[:, :], OB[:, 0:2 * P], put_hi[:, :].bitcast(F32), ALU.subtract)\
                    .then_inc(put_lo_done, 1)

            def add_scatter(s, r, out=OB):
                dve.wait_ge(sc_psum, s * 4 + (r + 1))
                dve.tensor_tensor(h[:, 2 * r:2 * r + 2, NMETA:T], out[:, :].rearrange("p (a b) -> p a b", a=2),
                                  h[:, 2 * r:2 * r + 2, NMETA:T], ALU.add).then_inc(sc_add, 1)

            def job(J, j0, turn, main, e=None):
                q = 0

                def used(count=1):
                    nonlocal q
                    for _ in range(count):
                        if main or q + LO_AHEAD < HJOB:
                            split(2 * j0 + q + LO_AHEAD, turn)
                        q += 1

                def hT_part(n):
                    dve.wait_ge(hT_hi_done, J * UNITS + (n + 1))
                    dve.tensor_tensor(hT_lo[:, :], TP[0][:, :], hT_hi[:, :].bitcast(F32), ALU.subtract)\
                        .then_inc(hT_lo_done, 1)

                if not main:
                    for i in range(LO_AHEAD):
                        split(2 * j0 + i, turn)
                    dve.wait_ge(xg_psum, J + 1)
                    dve.wait_ge(put_psum, J)
                    build_pick(e, 1)
                    xg_part(J + 1)
                    put_part(J)
                for n in range(UNITS):
                    adding = n == 1 and main
                    used()
                    if adding:
                        add_scatter(J, 0)
                    used(2)
                    if n:
                        hT_part(n - 1)
                    if adding:
                        add_scatter(J, 1)
                    used()
                    if n == 2 and main:
                        put_part(J)
                    if n == 4 and main:
                        dve.wait_ge(xg_psum, J + 1)
                        dve.wait_ge(put_psum, J + 1)
                        build_pick(J + 1, 0)
                    used()
                    if adding:
                        add_scatter(J, 2)
                    used(2)
                    if adding:
                        add_scatter(J, 3)
                    used()
                    dve.wait_ge(silu_done, J * UNITS + (n + 2))
                    dve.wait_ge(half_used, J * HJOB + 2 * (6 * n + 2 if n else 4))
                    dve.tensor_tensor(hb[:, :], (PJ if n % 2 == 0 else SB)[1][:, :], sg[:, :], ALU.mult)\
                        .then_inc(hm_done, 1)
                    if n:
                        used(4)
                hT_part(UNITS - 1)
                used()
                if main:
                    xg_part(J + 1)
                used(3)
                dve.wait_ge(y_hi_done, J + 1)
                dve.tensor_tensor(y_lo[:, 0:512], TP[1][:, :], y_hi[:, 0:512].bitcast(F32), ALU.subtract)
                dve.tensor_tensor(y_lo[:, 512:1024], TP[2][:, :], y_hi[:, 512:1024].bitcast(F32),
                                  ALU.subtract).then_inc(y_lo_done, 1)
                if not main:
                    for r in range(4):
                        add_scatter(J + 1, r, SPREAD[r])

            dve.nop().then_inc(hm_done, 1)
            dve.nop().then_inc(hT_lo_done, 1)
            dve.nop().then_inc(y_lo_done, 1)
            dve.nop().then_inc(put_lo_done, 1)
            dve.nop().then_inc(sc_add, 1)
            xg_part(0)
            with dve.Fori(0, NE) as e:
                job(e, MOE0, e, True)
            split(2 * OVER0 - 1)
            for r in range(4):
                add_scatter(NE, r, SPREAD[r])
            dve.wait_ge(table_ready, 1)
            over = dve.value_load(tab[0:1, 3:4], min_val=0, max_val=MAX_OVER)
            with dve.Fori(0, MAX_OVER) as o:
                with dve.If(o < over):
                    e = dve.value_load(tab[0:1, bass.ds(o, 1)], min_val=0, max_val=NE - 1)
                    job(o + NE, OVER0, o, False, e)
            dve.drain().then_inc(h_final, 1)
            dve.wait_ge(h_final, 1)
            link(dve.tensor_tensor(outb[:, 4:8, :], h[:, 4:8, NMETA:T], h[:, 4:8, NMETA:T], ALU.mult))
            dve.wait_ge(fin_sq_act, 1)
            dve.tensor_tensor(outb[:, 0:4, :], outb[:, 0:4, :], outb[:, 4:8, :], ALU.add).then_inc(fin_sq_dve, 1)
            dve.wait_ge(rstd_ready, 5)
            for c in range(KD):
                dve.scalar_tensor_tensor(outb[:, c, :], h[:, c, NMETA:T], vec[:, V_GFIN + c:V_GFIN + c + 1],
                                         rb[:, NMETA:T], ALU.mult, ALU.mult).then_inc(out_ready, 1)

        @block.tensor
        def _(pe):
            def mm3(out, l_hi, l_lo, r_hi, r_lo, first, last):
                pe.matmul(out, l_hi, r_hi, start=first, stop=False)
                pe.matmul(out, l_hi, r_lo, start=False, stop=False)
                return pe.matmul(out, l_lo, r_hi, start=False, stop=last)

            ident = cst[:, C_ID:C_ID + P]

            def stat(n, c):
                pe.wait_ge(sq_ready, 8 * n + c + 1)
                pe.matmul(OB[:, 0:T], ones[:, :], sq[:, c % 2, :], start=(c == 0), stop=(c == KD - 1))\
                    .then_inc(stat_done, 1)

            def row_rstd(k):
                for w in range(3):
                    ins = pe.matmul(TP[0][:, 2 * w:2 * w + 2], rb[0:1, WIN[w]:WIN[w] + P], ones[0:1, 0:2],
                                    start=True, stop=True)
                ins.then_inc(rt_psum, 1)

            def take(i, turn=0, per=HJOB):
                pe.wait_ge(lo_done, turn * per + (i + 1))
                return w_hi[:, i % NHALF, :], w_lo[:, i % NHALF, :]

            def begin(t, m=0):
                if t >= 2:
                    pe.wait_ge(proj_free, m * FFN_STEP + (t - 1))
                return PJ[t % 2]

            def stationary(t, half, nk, r_hi, r_lo, r0, c0=0, width=P, first=True, last=True, before=None):
                hi, lo = half
                for k in range(nk):
                    c = width * k + c0
                    if before:
                        before(k)
                    ins = mm3(PJ[t % 2][:, 0:T], hi[:, c:c + P], lo[:, c:c + P], r_hi[:, r0 + k, :],
                              r_lo[:, r0 + k, :], first and k == 0, last and k == nk - 1)
                return ins

            def queries_keys(l, u):
                un = 8 * l + u
                src, i = qk[u // 4], u % 4
                if u == 0:
                    pe.wait_ge(rope_done, 8 * l + 8)
                if u == 4:
                    pe.wait_ge(cneg_ready, l + 1)
                if un:
                    pe.wait_ge(s_free, 2 * un)
                for m in range(2):
                    r = slice(64 * m, 64 * m + 64)
                    for s, (c0, w) in enumerate(SEG):
                        out = SB[m][:, c0:c0 + w]
                        ins = pe.matmul(out, src[r, i, WIN[s]:WIN[s] + P], src[r, 4 + i, 0:w], start=True,
                                        stop=(u < 4))
                        if u >= 4:
                            head = 2 * (u - 4) + m
                            ins = pe.matmul(out, cst[0:8, C_ID + head:C_ID + head + 1].to_broadcast([8, P]),
                                            cneg[:, 0:w], start=False, stop=True)
                    ins.then_inc(s_done, 1)

            def transposes(l, u):
                un = 8 * l + u
                pe.wait_ge(a_ready, un + 1)
                if un:
                    pe.wait_ge(aT_ready, un)
                if u == 0:
                    pe.wait_ge(rt_ready, l + 1)
                for m in range(1 if u < 4 else 2):
                    a = score[:, m, :]
                    c1, c2 = SEG[1][0], SEG[2][0]
                    for out, src in ((TP[m][:, 0:128], a[:, c1 + 16:c1 + 144]),
                                     (TP[m][:, 128:256], a[:, c2 + 16:c2 + 144]),
                                     (TP[m][:, 256:384], a[:, c2 + 144:c2 + 272]),
                                     (TP[2][0:16, 256 * m:256 * m + 128], a[:, c1:c1 + 16]),
                                     (TP[2][0:16, 256 * m + 128:256 * m + 256], a[:, c2:c2 + 16])):
                        pe.transpose(out, src, ident)
                    ins = pe.transpose(TP[m][0:16, 384:400], a[0:16, 0:16], ident[0:16, 0:16])
                ins.then_inc(tr_done, 1)

            def values(l, u):
                un = 8 * l + u
                pe.wait_ge(aT_ready, un + 1)
                if 1 <= u <= 4:
                    pe.wait_ge(o_rs_ready, 4 * l + u)
                elif un:
                    pe.wait_ge(o_lo, un)
                for m in range(1 if u < 4 else 2):
                    c, w = (P * u, P) if u < 4 else (512 + P * (u - 4) + 64 * m, 64)
                    r = slice(64 * m, 64 * m + w)
                    pe.matmul(OB[r, 0:T], v[0:16, 0, c:c + w], aT[0:16, m, 384:656], start=True, stop=False)
                    pe.matmul(OB[r, 16:T], v[:, 1, c:c + w], aT[:, m, 0:256], start=False, stop=False)
                    ins = pe.matmul(OB[r, 144:T], v[:, 2, c:c + w], aT[:, m, 256:384], start=False, stop=True)
                ins.then_inc(pv_done, 1)

            def o_statistics(l, u):
                pe.wait_ge(o_sq_ready, 4 * l + u + 1)
                pe.matmul(OB[:, 0:T], ones[:, :], o_sq, start=True, stop=True).then_inc(o_stat, 1)

            pe.wait_ge(pool_set, 4)
            for c in range(KD):
                stat(0, c)
            pe.wait_ge(small_lo, 1)
            for l in range(LAYERS):
                t0 = l * (MIX_TILES + FFN_TILES)
                p0 = l * LAYER1
                xh, xl = x_hi[0], x_lo[0]
                begin(t0)
                for k in range(KD):
                    if l and k == KD - 2:
                        stat(2, KD - 1)
                    pe.wait_ge(x_lo_done, counts_before(2 * l) + k + 1)
                    c = 64 * l + 8 * k
                    ins = mm3(PJ[t0 % 2][:, 0:T], ff_hi[:, c:c + P], ff_lo[:, c:c + P], xh[:, k, :], xl[:, k, :],
                              k == 0, k == KD - 1)
                ins.then_inc(strip_done, 1)
                for j in range(8):
                    for i in range(2):
                        t = t0 + 1 + 2 * j + i
                        half = take(2 * (p0 + j) + i)
                        begin(t)
                        stationary(t, half, KD, xh, xl, 0).then_inc(strip_done, 1)
                    if j == 0:
                        pe.wait_ge(rstd_ready, 2 * l + 1)
                        row_rstd(l)
                    if l == 0 and j == 1:
                        pe.wait_ge(tables_in, 32)
                    if 1 <= j <= 4:
                        for i in (2 * j - 2, 2 * j - 1):
                            pe.wait_ge(proj_free, t0 + 2 + i)
                            if i >= 2:
                                pe.wait_ge(rope_done, 8 * l + i - 1)
                            elif l:
                                pe.wait_ge(aT_ready, 8 * l)
                            pe.matmul(TP[1 + i % 2][:, 0:T], cst[:, C_ROT:C_ROT + P], qk[0][:, i, :], start=True,
                                      stop=True).then_inc(rot_done, 1)
                for j in range(8, 12):
                    halves = [take(2 * (p0 + j) + i) for i in range(2)]
                    for w in range(3):
                        t = t0 + V_TILE + 3 * (j - 8) + w
                        begin(t)
                        for k in range(KD):
                            hi, lo = halves[k // 4]
                            c = 256 * (k % 4)
                            ins = mm3(PJ[t % 2][:, 0:256], xh[:, k, WIN[w]:WIN[w] + P], xl[:, k, WIN[w]:WIN[w] + P],
                                      hi[:, c:c + 256], lo[:, c:c + 256], k == 0, k == KD - 1)
                        ins.then_inc(strip_done, 1)
                pe.wait_ge(proj_free, t0 + GATE_TILE)
                queries_keys(l, 0)
                for u in range(8):
                    for i in range(2):
                        t = t0 + GATE_TILE + 2 * u + i
                        half = take(2 * (p0 + 12 + u) + i)
                        begin(t)
                        stationary(t, half, KD, xh, xl, 0).then_inc(strip_done, 1)
                        if i == 0 and u:
                            values(l, u - 1)
                    if u < 7:
                        queries_keys(l, u + 1)
                    if 1 <= u <= 4:
                        o_statistics(l, u - 1)
                    transposes(l, u)
                for j in range(20, 24):
                    pe.wait_ge(o_lo, 8 * l + (4 if j < 22 else 8))
                    for i in range(4):
                        t = t0 + (BD_TILE if j < 22 else BF_TILE) + 4 * (j % 2) + i
                        half = take(2 * (p0 + j) + i // 2)
                        begin(t)
                        stationary(t, half, 4, x_hi[1], x_lo[1], 0 if j < 22 else 4, P * (i % 2), 2 * P)\
                            .then_inc(strip_done, 1)
                        if j == 20 and i == 0:
                            values(l, 7)
                n = 2 * l + 1
                for c in range(KD):
                    t = t0 + OUT_TILE + c
                    half = take(2 * (p0 + 24) + c)
                    begin(t)
                    before = (lambda k: pe.wait_ge(x_lo_done, counts_before(n) - KD + k + 1)) if c == 0 else None
                    stationary(t, half, KD, xh, xl, 0, before=before).then_inc(strip_done, 1)
                    if c >= 1:
                        stat(n, c - 1)
                if l == 0:
                    f0 = MIX_TILES

                    def first_chunks(k):
                        if k == KD - 2:
                            stat(1, KD - 1)
                        pe.wait_ge(x_lo_done, counts_before(1) + k + 1)

                    def ffn_block(b, m=0):
                        for i in range(4):
                            t = f0 + 4 * b + i
                            half = take(2 * MIX_PIECES + 4 * b + i, m, FFN_STEP)
                            begin(t, m)
                            before = first_chunks if b == 0 and i == 0 else None
                            stationary(t, half, KD, x_hi[1], x_lo[1], 0, before=before).then_inc(strip_done, 1)

                    ffn_block(0)
                    with pe.Fori(0, FFN_TURNS) as m:
                        for b in range(1, 1 + FFN_UNROLL):
                            ffn_block(b, m)
                    ffn_block(FFN_BLOCKS - 1)
                    for dp in range(4):
                        for part, (k0, nk) in enumerate(DOWN_K):
                            pe.wait_ge(ffh_lo_done, k0 + nk)
                            for i in range(2):
                                t = f0 + 4 * FFN_BLOCKS + 2 * dp + i
                                half = take(2 * (MIX_PIECES + 2 * FFN_BLOCKS + 3 * dp + part) + i)
                                if part == 0:
                                    begin(t)
                                ins = stationary(t, half, nk, ffh_hi, ffh_lo, k0, first=(part == 0),
                                                 last=(part == 2))
                                ins.then_inc(strip_done, 1)
                        if dp:
                            stat(2, 2 * dp - 2)
                            stat(2, 2 * dp - 1)
                    stat(2, 6)

            def turn_tokens(half):
                pe.wait_ge(x_lo_done, counts_before(3) + 4 * half + 4)
                for tt in range(2):
                    i = 2 * half + tt
                    w = slice(WIN[tt + 1], WIN[tt + 1] + P)
                    for k in range(4):
                        out = xt_bank(SB, TP, i)[:, P * k:P * k + P]
                        pe.matmul(out, x_hi[1][:, 4 * half + k, w], ident_r, start=True, stop=False)
                        ins = pe.matmul(out, x_lo[1][:, 4 * half + k, w], ident_r, start=False, stop=True)
                    ins.then_inc(xt_psum, 1)

            pe.wait_ge(ident_done, 1)
            pe.wait_ge(aT_ready, 8 * LAYERS)
            pe.wait_ge(s_free, 16 * LAYERS)
            turn_tokens(0)
            stat(3, KD - 1)
            pe.wait_ge(proj_free, LAYERS * MIX_TILES + FFN_TILES - 1)
            for k in range(KD):
                pe.wait_ge(x_lo_done, counts_before(3) + k + 1)
                c = V_RT - V_FF + NE * k
                ins = mm3(LOGIT[:, 0:SEQ], ff_hi[:, c:c + P], ff_lo[:, c:c + P], x_hi[1][:, k, NMETA:T],
                          x_lo[1][:, k, NMETA:T], k == 0, k == KD - 1)
            ins.then_inc(logit_done, 1)
            turn_tokens(1)
            pe.wait_ge(rstd_ready, 4)
            row_rstd(2)
            pe.wait_ge(lgT_ready, 1)
            for tt in range(2):
                ins = pe.transpose(OB[:, NE * tt:NE * tt + NE], lgT[:, tt, :], ident[0:NE, 0:NE])
            ins.then_inc(logit_turned, 1)
            pe.wait_ge(mask_ready, 1)
            tri = cst[:, C_TRI:C_TRI + P]
            pe.matmul(OB[:, 32:40], tri, mask[:, 0, :], start=True, stop=True)
            pe.matmul(OB[:, 40:48], tri, mask[:, 1, :], start=True, stop=False)
            pe.matmul(OB[:, 40:48], ones[:, :], mask[:, 0, :], start=False, stop=True)
            pe.matmul(OB[:, 48:56], ones[:, :], mask[:, 0, :], start=True, stop=False)
            pe.matmul(OB[:, 48:56], ones[:, :], mask[:, 1, :], start=False, stop=True).then_inc(rank_done, 1)

            def gather(g, first=False):
                pe.wait_ge(pick_ready, g + 1)
                for c in range(KD):
                    if first and c % 4 == 0:
                        pe.wait_ge(xt_lo_done, 2 + c // 2)
                    out = SB[c // 4][:, P * (c % 4):P * (c % 4) + P]
                    for tt in range(2):
                        pe.matmul(out, xt_hi[:, tt, P * c:P * c + P], pick[:, tt, :], start=(tt == 0), stop=False)
                        ins = pe.matmul(out, xt_lo[:, tt, P * c:P * c + P], pick[:, tt, :], start=False,
                                        stop=(tt == 1))
                ins.then_inc(xg_psum, 1)

            def put_transpose(s):
                pe.wait_ge(pick_ready, s + 1)
                for tt in range(2):
                    ins = pe.transpose(OB[:, P * tt:P * tt + P], pickw[:, tt, :], ident)
                ins.then_inc(put_psum, 1)

            def scatter(s, r, out=OB):
                if r == 0:
                    pe.wait_ge(y_lo_done, s + 1)
                    pe.wait_ge(put_lo_done, s + 1)
                elif out is OB:
                    pe.wait_ge(sc_add, s * 4 + (r + 1))
                for i in range(2):
                    c = P * (2 * r + i)
                    ins = mm3(out[:, 256 * i:256 * i + 256], y_hi[:, c:c + P], y_lo[:, c:c + P], put_hi[:, :],
                              put_lo[:, :], True, True)
                ins.then_inc(sc_psum, 1)

            def job(J, j0, turn, main):
                q = 0

                def half():
                    nonlocal q
                    q += 1
                    return take(2 * j0 + q - 1, turn)

                def up_half(out, part):
                    for i in range(2):
                        hi, lo = half()
                        for k in range(2):
                            c = P * (4 * part + 2 * i + k)
                            ins = mm3(out, xg_hi[:, c:c + P], xg_lo[:, c:c + P], hi[:, 512 * k:512 * k + 512],
                                      lo[:, 512 * k:512 * k + 512], c == 0, c == 7 * P)
                        ins.then_inc(half_used, 1)

                def turn_hidden(n):
                    pe.wait_ge(hm_done, J * UNITS + (n + 2))
                    pe.wait_ge(hT_lo_done, J * UNITS + (n + 1))
                    for i in range(4):
                        ins = pe.transpose(TP[0][:, P * i:P * i + P], hb[:, P * i:P * i + P], ident)
                    ins.then_inc(hT_psum, 1)

                def down_half(n, part):
                    pe.wait_ge(hT_lo_done, J * UNITS + (n + 2))
                    if n == 0:
                        pe.wait_ge(y_lo_done, J + 1)
                    for i in range(2):
                        hi, lo = half()
                        c = P * (2 * part + i)
                        for s in range(2):
                            ins = mm3(TP[1 + s][:, :], hT_hi[:, c:c + P], hT_lo[:, c:c + P],
                                      hi[:, 512 * s:512 * s + 512], lo[:, 512 * s:512 * s + 512],
                                      n == 0 and c == 0, n == UNITS - 1 and c == 3 * P)
                        ins.then_inc(half_used, 1)

                if not main:
                    gather(J + 1)
                    put_transpose_over(J)
                pe.wait_ge(xg_lo_done, J + (1 if main else 2))
                for n in range(UNITS):
                    G, U = PJ if n % 2 == 0 else SB
                    if n != 1:
                        pe.wait_ge(silu_done, J * UNITS + (n if n else 1))
                    up_half(G[:, :], 0)
                    if n:
                        turn_hidden(n - 1)
                    if n == 1 and main:
                        scatter(J, 1)
                    if n == 2 and main:
                        pe.wait_ge(sc_add, J * 4 + 5)
                        put_transpose(J)
                    up_half(G[:, :], 1)
                    if n == 1 and main:
                        scatter(J, 2)
                    if n != 1:
                        pe.wait_ge(hm_done, J * UNITS + (n if n else 1))
                    up_half(U[:, :], 0)
                    if n == 1 and main:
                        scatter(J, 3)
                    up_half(U[:, :], 1)
                    if n == 0 and main:
                        scatter(J, 0)
                    if n:
                        down_half(n - 1, 0)
                        if n == UNITS - 1:
                            turn_hidden(n)
                        down_half(n - 1, 1)
                if main:
                    gather(J + 1)
                down_half(UNITS - 1, 0)
                down_half(UNITS - 1, 1)
                if not main:
                    for r in range(4):
                        scatter(J + 1, r, SPREAD[r])

            def put_transpose_over(s):
                for tt in range(2):
                    ins = pe.transpose(OB[:, P * tt:P * tt + P], pickw[:, tt, :], ident)
                ins.then_inc(put_psum, 1)

            pe.wait_ge(proj_free, LAYERS * MIX_TILES + FFN_TILES)
            gather(0, first=True)
            with pe.Fori(0, NE) as e:
                job(e, MOE0, e, True)
            pe.wait_ge(xg_lo_done, NE + 1)
            for r in range(4):
                scatter(NE, r, SPREAD[r])
            pe.wait_ge(table_ready, 1)
            over = pe.value_load(tab[0:1, 3:4], min_val=0, max_val=MAX_OVER)
            with pe.Fori(0, MAX_OVER) as o:
                with pe.If(o < over):
                    pe.wait_ge(sc_add, o * 4 + (4 * NE + 5))
                    job(o + NE, OVER0, o, False)
            pe.wait_ge(fin_sq_dve, 1)
            for c in range(4):
                ins = pe.matmul(OB[:, 0:SEQ], ones[:, :], outb[:, c, :], start=(c == 0), stop=(c == 3))
            ins.then_inc(stat_done, 1)


def counts_before(n):
    return 8 * n + 8 * ((n + 1) // 2)


def xt_bank(SB, TP, i):
    return (SB[0], SB[1], TP[1], TP[2])[i]


def kernel(**inputs):
    import numpy as np
    import concourse.bacc as bacc
    from concourse import mybir as mb
    from concourse.bass_utils import run_bass_kernel_spmd as run

    a = {k: np.asarray(x) for k, x in inputs.items()}
    f32 = np.float32

    def on_partitions(x):
        return np.ascontiguousarray(np.moveaxis(x.reshape(*x.shape[:-1], -1, P), -1, 0).reshape(P, -1))

    tokens = np.concatenate([a["meta_tokens"], a["x"][0]], axis=0)
    xT = np.ascontiguousarray(tokens.T.reshape(KD, P, T).transpose(1, 0, 2))

    vecs = np.zeros((P, V_W), f32)
    vecs[:, V_GMIX:V_GMIX + 16] = on_partitions(a["norm_mix_g"])
    vecs[:, V_GFFN:V_GFFN + 16] = on_partitions(a["norm_ffn_g"])
    vecs[:, V_GFIN:V_GFIN + 8] = on_partitions(a["final_norm_g"])
    vecs[:, V_SUB:V_SUB + 2] = a["diff_subln_g"].T
    vecs[0:8, V_BF:V_BF + 2] = a["b_forget"].T
    ff = a["w_in"][:, :, FF_COL:FF_COL + 8].reshape(LAYERS, KD, P, 8)
    vecs[:, V_FF:V_FF + 128] = ff.transpose(2, 0, 1, 3).reshape(P, -1)
    vecs[:, V_RT:V_RT + 64] = a["moe_router"][0].reshape(KD, P, NE).transpose(1, 0, 2).reshape(P, -1)
    lam = np.ascontiguousarray(np.broadcast_to(a["diff_lambda"].reshape(1, -1), (P, 512)))

    c = np.zeros((P, C_W), f32)
    rows = np.arange(P)
    for (c0, w), start in zip(SEG, WIN):
        seen = np.arange(w)[None, :] <= (start + rows)[:, None]
        c[:, C_MASK + c0:C_MASK + c0 + w] = np.where(seen, 0.0, -BIG / SCALE)
    c[:, C_ID:C_ID + P] = np.eye(P)
    c[:, C_TRI:C_TRI + P] = rows[:, None] < rows[None, :]
    c[:, C_IOTA:C_IOTA + 2 * P] = np.arange(2 * P)
    inv = f32(500000.0) ** (-np.arange(0, 16, 2, dtype=f32) / f32(16))
    ang = np.arange(T, dtype=f32)[None, :] * inv[:, None].astype(f32)
    d = rows % 64
    c[:, C_COS:C_COS + T] = np.where(d[:, None] < 16, np.cos(ang)[d % 8], 1.0)
    c[:, C_SIN:C_SIN + T] = np.where(d[:, None] < 16, np.sin(ang)[d % 8], 0.0) * np.where(d < 8, -1, 1)[:, None]
    for p in rows[d < 16]:
        c[p ^ 8, C_ROT + p] = 1.0
    c[:, C_REV:C_REV + 16] = NE - np.arange(16) % NE

    arrays = {"xT": xT, "w_in": a["w_in"], "lam": lam, "w_bd": a["w_branch_diff"], "w_bf": a["w_branch_fox"],
              "w_out": a["w_out"], "f_g": a["ffn_w_gate"], "f_u": a["ffn_w_up"], "f_d": a["ffn_w_down"],
              "m_g": a["moe_w_gate"], "m_u": a["moe_w_up"], "m_d": a["moe_w_down"], "consts": c, "vecs": vecs}
    nc = bacc.Bacc("TRN2", target_bir_lowering=False, num_devices=1)
    args = [nc.dram_tensor(name, x.shape, mb.dt.from_np(x.dtype), kind="ExternalInput").ap()
            for name, x in arrays.items()]
    out = nc.dram_tensor("outT", (P, KD, SEQ), mb.dt.float32, kind="ExternalOutput").ap()
    trunk(nc, *args, out)
    r = run(nc, [arrays], core_ids=[0])
    got = r.results[0]["outT"]
    return np.ascontiguousarray(got.transpose(1, 0, 2).reshape(D, SEQ).T).reshape(1, SEQ, D)
```
